# Optimizing a Trainium2 kernel written in Bass

```python
import jax, jax.numpy as jnp
from jax import lax
import numpy as np

D_MODEL = 1024
BATCH = 1
SEQ = 512
DEPTH = 2

CHUNK = 128
A_HEADS = 4
A_HEAD_DIM = D_MODEL // 8
A_WIDTH = A_HEADS * A_HEAD_DIM
POOL_WINDOWS = (2, 4, 8, 16)
POOL_GROUPS = len(POOL_WINDOWS)
POOL_DIM = D_MODEL // 8
B_WIDTH = POOL_GROUPS * POOL_DIM
MIX_WIDTH = A_WIDTH + B_WIDTH
IN_WIDTH = 2 * A_WIDTH + B_WIDTH
CONV_DIM = D_MODEL
CONV_WIDTH = 31
FFN_DIM = ((8 * D_MODEL // 3 + 127) // 128) * 128
FFN_CONV_WIDTH = 3
DEEPNORM_ALPHA = (2 * DEPTH) ** 0.25
DEEPNORM_BETA = (8 * DEPTH) ** -0.25
ADA_INIT = 0.5
LN_EPS = 1e-5
N_EVEN = (DEPTH + 1) // 2
N_ODD = DEPTH // 2


def _layer_norm(x, g, b):
    xf = x.astype(jnp.float32)
    mu = jnp.mean(xf, axis=-1, keepdims=True)
    var = jnp.mean(jnp.square(xf - mu), axis=-1, keepdims=True)
    y = (xf - mu) * lax.rsqrt(var + LN_EPS)
    return (y * g + b).astype(x.dtype)

def _modulation(c, w, b):
    m = jax.nn.silu(c) @ w + b
    shift, scale, gate = jnp.split(m, 3, axis=-1)
    return shift[:, None, :], scale[:, None, :], gate[:, None, :]

def _depthwise_conv(x, w, b):
    ch = w.shape[1]
    y = lax.conv_general_dilated(x, w[:, None, :], window_strides=(1,), padding='SAME',
                                 dimension_numbers=('NWC', 'WIO', 'NWC'), feature_group_count=ch)
    return y + b

def _spatial_gating(u, v, ln_g, ln_b, ws, bs):
    v = _layer_norm(v, ln_g, ln_b)
    nb, s, _ = v.shape
    vh = v.reshape(nb, s // CHUNK, CHUNK, A_HEADS, A_HEAD_DIM)
    mixed = jnp.einsum('hpq,bnqhd->bnphd', ws, vh) + bs.T[None, None, :, :, None]
    return u * mixed.reshape(nb, s, A_WIDTH)

def _centred_mean_minus_self(z, window):
    s = z.shape[1]
    half = window // 2
    prefix = jnp.concatenate([jnp.zeros_like(z[:, :1]), jnp.cumsum(z, axis=1)], axis=1)
    padded = jnp.pad(prefix, ((0, 0), (half, half), (0, 0)), mode='edge')
    total = padded[:, 2 * half:2 * half + s] - padded[:, :s]
    t = jnp.arange(s)
    count = (jnp.minimum(t + half, s) - jnp.maximum(t - half, 0)).astype(jnp.float32)
    return total / count[None, :, None] - z

def _multiscale_pool(z, pool_w, pool_scale):
    nb, s, _ = z.shape
    zf = z.astype(jnp.float32).reshape(nb, s, POOL_GROUPS, POOL_DIM)
    pooled = jnp.stack([_centred_mean_minus_self(zf[:, :, g], w) for g, w in enumerate(POOL_WINDOWS)], axis=2)
    y = jnp.einsum('bsgc,gcd->bsgd', pooled.astype(z.dtype), pool_w)
    return y.reshape(nb, s, B_WIDTH) * pool_scale

def _sgu_pool_mixer(h, w_in, sgu_ln_g, sgu_ln_b, ws, bs, pool_w, pool_scale, w_out):
    proj = h @ w_in
    u_a = jax.nn.gelu(proj[..., :A_WIDTH])
    v_a = jax.nn.gelu(proj[..., A_WIDTH:2 * A_WIDTH])
    z_b = proj[..., 2 * A_WIDTH:]
    out_a = _spatial_gating(u_a, v_a, sgu_ln_g, sgu_ln_b, ws, bs)
    out_b = _multiscale_pool(z_b, pool_w, pool_scale)
    return jnp.concatenate([out_a, out_b], axis=-1) @ w_out

def _conformer_conv(h, w_in, dw, dw_b, ln_g, ln_b, w_out):
    a, g = jnp.split(h @ w_in, 2, axis=-1)
    z = a * jax.nn.sigmoid(g)
    z = _depthwise_conv(z, dw, dw_b)
    z = jax.nn.silu(_layer_norm(z, ln_g, ln_b))
    return z @ w_out

def _conv_ffn(h, w_up, dw, dw_b, w_down):
    z = _depthwise_conv(h @ w_up, dw, dw_b)
    g, v = jnp.split(z, 2, axis=-1)
    return (jax.nn.gelu(g) * v) @ w_down

def first_inputs(seed: int = 0) -> dict:
    key = jax.random.key(seed)
    ks = jax.random.split(key, 32)

    def nrm(k, shape, scale):
        return scale * jax.random.normal(k, shape, jnp.float32)

    d = D_MODEL
    return {
        "x": nrm(ks[0], (BATCH, SEQ, d), 1.0),
        "c": nrm(ks[1], (BATCH, d), 1.0),
        "mix_ada_w": nrm(ks[2], (DEPTH, d, 3 * d), ADA_INIT * d ** -0.5),
        "mix_ada_b": nrm(ks[3], (DEPTH, 3 * d), 0.01),
        "mix_ln_g": 1.0 + nrm(ks[4], (DEPTH, d), 0.02),
        "mix_ln_b": nrm(ks[5], (DEPTH, d), 0.01),
        "ab_w_in": nrm(ks[6], (N_EVEN, d, IN_WIDTH), d ** -0.5),
        "ab_sgu_ln_g": 1.0 + nrm(ks[7], (N_EVEN, A_WIDTH), 0.02),
        "ab_sgu_ln_b": nrm(ks[8], (N_EVEN, A_WIDTH), 0.01),
        "ab_ws": nrm(ks[9], (N_EVEN, A_HEADS, CHUNK, CHUNK), CHUNK ** -0.5),
        "ab_bs": 1.0 + nrm(ks[10], (N_EVEN, A_HEADS, CHUNK), 0.02),
        "ab_pool_w": nrm(ks[11], (N_EVEN, POOL_GROUPS, POOL_DIM, POOL_DIM), POOL_DIM ** -0.5),
        "ab_pool_scale": 1.0 + nrm(ks[12], (N_EVEN, B_WIDTH), 0.1),
        "ab_w_out": nrm(ks[13], (N_EVEN, MIX_WIDTH, d), DEEPNORM_BETA * MIX_WIDTH ** -0.5),
        "cv_w_in": nrm(ks[14], (N_ODD, d, 2 * CONV_DIM), d ** -0.5),
        "cv_dw": nrm(ks[15], (N_ODD, CONV_WIDTH, CONV_DIM), CONV_WIDTH ** -0.5),
        "cv_dw_b": nrm(ks[16], (N_ODD, CONV_DIM), 0.01),
        "cv_ln_g": 1.0 + nrm(ks[17], (N_ODD, CONV_DIM), 0.02),
        "cv_ln_b": nrm(ks[18], (N_ODD, CONV_DIM), 0.01),
        "cv_w_out": nrm(ks[19], (N_ODD, CONV_DIM, d), DEEPNORM_BETA * CONV_DIM ** -0.5),
        "ffn_ada_w": nrm(ks[20], (DEPTH, d, 3 * d), ADA_INIT * d ** -0.5),
        "ffn_ada_b": nrm(ks[21], (DEPTH, 3 * d), 0.01),
        "ffn_w_up": nrm(ks[22], (DEPTH, d, 2 * FFN_DIM), d ** -0.5),
        "ffn_dw": nrm(ks[23], (DEPTH, FFN_CONV_WIDTH, 2 * FFN_DIM), FFN_CONV_WIDTH ** -0.5),
        "ffn_dw_b": nrm(ks[24], (DEPTH, 2 * FFN_DIM), 0.01),
        "ffn_w_down": nrm(ks[25], (DEPTH, FFN_DIM, d), DEEPNORM_BETA * FFN_DIM ** -0.5),
        "ffn_ln_g": 1.0 + nrm(ks[26], (DEPTH, d), 0.02),
        "ffn_ln_b": nrm(ks[27], (DEPTH, d), 0.01),
    }

def first_block(x, c, mix_ada_w, mix_ada_b, mix_ln_g, mix_ln_b,
              ab_w_in, ab_sgu_ln_g, ab_sgu_ln_b, ab_ws, ab_bs, ab_pool_w, ab_pool_scale, ab_w_out,
              cv_w_in, cv_dw, cv_dw_b, cv_ln_g, cv_ln_b, cv_w_out,
              ffn_ada_w, ffn_ada_b, ffn_w_up, ffn_dw, ffn_dw_b, ffn_w_down, ffn_ln_g, ffn_ln_b):
    for i in range(DEPTH):
        j = i // 2
        shift, scale, gate = _modulation(c, mix_ada_w[i], mix_ada_b[i])
        h = x * (1.0 + scale) + shift
        if i % 2 == 0:
            y = _sgu_pool_mixer(h, ab_w_in[j], ab_sgu_ln_g[j], ab_sgu_ln_b[j], ab_ws[j], ab_bs[j],
                                ab_pool_w[j], ab_pool_scale[j], ab_w_out[j])
        else:
            y = _conformer_conv(h, cv_w_in[j], cv_dw[j], cv_dw_b[j], cv_ln_g[j], cv_ln_b[j], cv_w_out[j])
        x = _layer_norm(DEEPNORM_ALPHA * x + (1.0 + gate) * y, mix_ln_g[i], mix_ln_b[i])
        shift, scale, gate = _modulation(c, ffn_ada_w[i], ffn_ada_b[i])
        h = x * (1.0 + scale) + shift
        y = _conv_ffn(h, ffn_w_up[i], ffn_dw[i], ffn_dw_b[i], ffn_w_down[i])
        x = _layer_norm(DEEPNORM_ALPHA * x + (1.0 + gate) * y, ffn_ln_g[i], ffn_ln_b[i])
    return x


_first_inputs = first_inputs


def first_inputs(seed=0):
    import zlib

    import numpy as np

    out = dict(_first_inputs(seed))
    spreads = {}
    factors = {'mix_ada_b': 7.772,
     'mix_ln_b': 3.621,
     'ab_sgu_ln_g': 8.0,
     'ab_sgu_ln_b': 8.0,
     'ab_bs': 8.0,
     'cv_dw_b': 8.0,
     'cv_ln_g': 8.0,
     'cv_ln_b': 8.0,
     'ffn_ada_b': 6.557,
     'ffn_dw_b': 8.0,
     'ffn_ln_b': 3.896}
    for name, (base, spread) in spreads.items():
        noise = np.random.default_rng([zlib.crc32(name.encode()), seed]).standard_normal(out[name].shape)
        drawn = base * np.exp(spread * noise) if base else spread * noise
        out[name] = __import__('jax').numpy.asarray(drawn.astype(out[name].dtype))
    for name, factor in factors.items():
        out[name] = (out[name] * factor).astype(out[name].dtype)
    return out


_narrow_inputs = first_inputs


def first_inputs(seed=0):

    out = dict(_narrow_inputs(seed))
    wider = {'ab_sgu_ln_g': 4.65,
     'ab_sgu_ln_b': 10.3,
     'ab_bs': 4.61,
     'ab_pool_scale': 5.76,
     'cv_ln_g': 3.52,
     'cv_ln_b': 7.0}
    for name, times in wider.items():
        mean = out[name].mean()
        out[name] = (mean + times * (out[name] - mean)).astype(out[name].dtype)
    return out


GRID_W = 64
CTX_LEN = 256
HEAD_DIM = 64
MIX_WIDTH_2 = D_MODEL
A_HEADS_2 = MIX_WIDTH_2 // (2 * HEAD_DIM)
A_WIDTH_2 = A_HEADS_2 * HEAD_DIM
DECAY_LORA = 64
ICLR_LORA = 64
GATE_LORA = 128
B_HEADS = MIX_WIDTH_2 // (2 * HEAD_DIM)
B_KV_HEADS = 2
WINDOW = 128
BLOCK = 128
C_HEADS = MIX_WIDTH_2 // (2 * HEAD_DIM)
NA_KH = 8
NA_KW = 16
NA_QC = 16
NA_KC = 32
D_HEADS = MIX_WIDTH_2 // (2 * HEAD_DIM)
D_KV_HEADS = 2
D_FF = 4 * D_MODEL
ROPE_BASE = 10000.0
NORM_EPS = 1e-6
GN_EPS = 64e-5
NEG_INF = -1e30
ATTN_SCALE = HEAD_DIM ** -0.5
N_EVEN_2 = (DEPTH + 1) // 2
N_ODD_2 = DEPTH // 2
A_IN = 3 * A_WIDTH_2 + 2 * DECAY_LORA + 2 * ICLR_LORA + GATE_LORA
B_IN = (B_HEADS + 2 * B_KV_HEADS) * HEAD_DIM
C_IN = 3 * C_HEADS * HEAD_DIM
D_IN = (D_HEADS + 2 * D_KV_HEADS) * HEAD_DIM
EVEN_IN = A_IN + B_IN
ODD_IN = C_IN + D_IN
A_SPLITS = (A_WIDTH_2, 2 * A_WIDTH_2, 3 * A_WIDTH_2, 3 * A_WIDTH_2 + 2 * DECAY_LORA,
            3 * A_WIDTH_2 + 2 * DECAY_LORA + 2 * ICLR_LORA)


def rms_norm(x, g):
    xf = x.astype(jnp.float32)
    y = xf * lax.rsqrt(jnp.mean(xf * xf, axis=-1, keepdims=True) + NORM_EPS)
    return (y * g.astype(jnp.float32)).astype(x.dtype)

def modulate(h, gain, shift, scale):
    return rms_norm(h, gain) * (1 + scale) + shift

def sqrelu_mlp(u, w1, w2):
    return jnp.square(jax.nn.relu(u @ w1)) @ w2

def axial_angles(n_tok):
    t = jnp.arange(n_tok, dtype=jnp.int32)
    n_freq = HEAD_DIM // 4
    inv_freq = ROPE_BASE ** (-jnp.arange(n_freq, dtype=jnp.float32) / n_freq)
    row = (t // GRID_W).astype(jnp.float32)[:, None] * inv_freq
    col = (t % GRID_W).astype(jnp.float32)[:, None] * inv_freq
    return row, col

def _rotate(x, ang):
    f = ang.shape[-1]
    cos = jnp.cos(ang)[None, :, None, :]
    sin = jnp.sin(ang)[None, :, None, :]
    x1 = x[..., :f].astype(jnp.float32)
    x2 = x[..., f:].astype(jnp.float32)
    return jnp.concatenate([x1 * cos - x2 * sin, x1 * sin + x2 * cos], axis=-1).astype(x.dtype)

def axial_rope(x, ang):
    half = HEAD_DIM // 2
    return jnp.concatenate([_rotate(x[..., :half], ang[0]), _rotate(x[..., half:], ang[1])], axis=-1)

def split_qkv(p, hq, hkv):
    bn, s, _ = p.shape
    q, k, v = jnp.split(p, [hq * HEAD_DIM, (hq + hkv) * HEAD_DIM], axis=-1)
    return (q.reshape(bn, s, hq, HEAD_DIM), k.reshape(bn, s, hkv, HEAD_DIM), v.reshape(bn, s, hkv, HEAD_DIM))

def softmax_with_sink(s, sink):
    sk = jnp.broadcast_to(sink.astype(jnp.float32)[:, :, None, None], s.shape[:-1] + (1,))
    return jax.nn.softmax(jnp.concatenate([s, sk], axis=-1), axis=-1)[..., :-1]

def context_attention(q, k, v, sink=None):
    bn, l, h, d = q.shape
    hkv = k.shape[2]
    qg = q.reshape(bn, l, hkv, h // hkv, d)
    s = jnp.einsum('blkgd,bckd->bkglc', qg, k).astype(jnp.float32) * ATTN_SCALE
    p = jax.nn.softmax(s, axis=-1) if sink is None else softmax_with_sink(s, sink)
    o = jnp.einsum('bkglc,bckd->blkgd', p.astype(v.dtype), v)
    return o.reshape(bn, l, h * d)

def centred_shift(p, mu_prev, mu_next):
    prev = jnp.pad(p, ((0, 0), (1, 0), (0, 0)))[:, :-1]
    nxt = jnp.pad(p, ((0, 0), (0, 1), (0, 0)))[:, 1:]
    return p + mu_prev * (prev - p) + mu_next * (nxt - p)

def rwkv7_prepare(pa, prm):
    p = centred_shift(pa, prm['mu_prev'], prm['mu_next']).astype(jnp.float32)
    bn, s, _ = p.shape
    r, k, v, wl, al, gl = jnp.split(p, A_SPLITS, axis=-1)
    wl = wl.reshape(bn, s, 2, DECAY_LORA)
    al = al.reshape(bn, s, 2, ICLR_LORA)
    w_raw = prm['w0'] + jnp.einsum('bsdl,dlc->bsdc', jnp.tanh(wl), prm['w2'])
    decay = jnp.exp(-jnp.exp(-jax.nn.softplus(-w_raw) - 0.5))
    iclr = jax.nn.sigmoid(prm['a0'] + jnp.einsum('bsdl,dlc->bsdc', al, prm['a2']))
    g = jax.nn.sigmoid(gl) @ prm['g2']
    kk = (k * prm['k_k']).reshape(bn, s, A_HEADS_2, HEAD_DIM)
    kk = kk / jnp.maximum(jnp.sqrt(jnp.sum(kk * kk, axis=-1, keepdims=True)), 1e-12)
    k_dir = k[:, :, None, :] * (1 + (iclr - 1) * prm['k_a'])
    heads = lambda t: t.reshape(t.shape[:-1] + (A_HEADS_2, HEAD_DIM))
    return dict(r=heads(r), v=heads(v), g=g, kk=kk, k=heads(k_dir), w=heads(decay), a=heads(iclr))

def rwkv7_scan(f, d, s0, reverse):
    def step(state, inp):
        r_t, w_t, k_t, v_t, kk_t, a_t = inp
        sa = jnp.einsum('bhvk,bhk->bhv', state, -kk_t)
        state = (state * w_t[:, :, None, :] + sa[..., None] * (kk_t * a_t)[:, :, None, :]
                 + v_t[..., None] * k_t[:, :, None, :])
        return state, jnp.einsum('bhvk,bhk->bhv', state, r_t)
    seq = (f['r'], f['w'][:, :, d], f['k'][:, :, d], f['v'], f['kk'], f['a'][:, :, d])
    xs = tuple(jnp.moveaxis(t, 1, 0) for t in seq)
    s_last, ys = lax.scan(step, s0, xs, reverse=reverse)
    return s_last, jnp.moveaxis(ys, 0, 1)

def rwkv7_output(f, y, prm, dtype):
    bn, s = y.shape[:2]
    mu = jnp.mean(y, axis=-1, keepdims=True)
    var = jnp.mean(jnp.square(y - mu), axis=-1, keepdims=True)
    yn = ((y - mu) * lax.rsqrt(var + GN_EPS)).reshape(bn, s, A_WIDTH_2) * prm['gn_w'] + prm['gn_b']
    bonus = jnp.sum(f['r'][:, :, None] * f['k'] * prm['r_k'], axis=(2, 4))
    yn = yn + (bonus[..., None] * f['v']).reshape(bn, s, A_WIDTH_2)
    return (yn * f['g']).astype(dtype)

def rwkv7_mixer(pa_ctx, pa_lat, prm, need_ctx):
    fc = rwkv7_prepare(pa_ctx, prm)
    fl = rwkv7_prepare(pa_lat, prm)
    zero = jnp.zeros((pa_lat.shape[0], A_HEADS_2, HEAD_DIM, HEAD_DIM), jnp.float32)
    s_cf, yc_f = rwkv7_scan(fc, 0, zero, False)
    _, yl_f = rwkv7_scan(fl, 0, s_cf, False)
    s_cb, yc_b = rwkv7_scan(fc, 1, zero, True)
    _, yl_b = rwkv7_scan(fl, 1, s_cb, True)
    out_lat = rwkv7_output(fl, yl_f + yl_b, prm, pa_lat.dtype)
    out_ctx = rwkv7_output(fc, yc_f + yc_b, prm, pa_ctx.dtype) if need_ctx else None
    return out_lat, out_ctx

def banded_window_attention(q, k, v, k_ctx, v_ctx, sink):
    bn, s, h, d = q.shape
    hkv = k.shape[2]
    nb = s // BLOCK
    qb = q.reshape(bn, nb, BLOCK, hkv, h // hkv, d)

    def band(t):
        tp = jnp.pad(t, ((0, 0), (BLOCK, BLOCK), (0, 0), (0, 0)))
        return jnp.concatenate([tp[:, j * BLOCK: j * BLOCK + s].reshape(bn, nb, BLOCK, hkv, d)
                                for j in range(3)], axis=2)
    kb, vb = band(k), band(v)
    qi = np.arange(BLOCK)[:, None]
    kj = np.arange(3 * BLOCK)[None, :]
    kpos = (np.arange(nb) * BLOCK)[:, None, None] - BLOCK + kj[None]
    ok = (np.abs(kj - BLOCK - qi) <= WINDOW)[None] & (kpos >= 0) & (kpos < s)
    s_lat = jnp.einsum('bnqkgd,bnjkd->bnkgqj', qb, kb).astype(jnp.float32) * ATTN_SCALE
    s_lat = jnp.where(ok[None, :, None, None], s_lat, NEG_INF)
    s_ctx = jnp.einsum('bnqkgd,bckd->bnkgqc', qb, k_ctx).astype(jnp.float32) * ATTN_SCALE
    p = softmax_with_sink(jnp.concatenate([s_lat, s_ctx], axis=-1), sink)
    p_lat, p_ctx = p[..., :3 * BLOCK].astype(v.dtype), p[..., 3 * BLOCK:].astype(v.dtype)
    o = (jnp.einsum('bnkgqj,bnjkd->bnqkgd', p_lat, vb)
         + jnp.einsum('bnkgqc,bckd->bnqkgd', p_ctx, v_ctx))
    return o.reshape(bn, s, h * d)

def neighbourhood_tables(rows):
    kh = min(NA_KH, rows)
    r = np.arange(rows)
    row_idx = np.clip(r - kh // 2, 0, rows - kh)[:, None] + np.arange(kh)[None, :]
    dr = row_idx - r[:, None] + NA_KH - 1
    ncb = GRID_W // NA_QC
    q_col = np.arange(ncb)[:, None] * NA_QC + np.arange(NA_QC)[None, :]
    key_col = (np.clip(np.arange(ncb) * NA_QC - NA_KW // 2, 0, GRID_W - NA_KC)[:, None]
               + np.arange(NA_KC)[None, :])
    win_start = np.clip(q_col - NA_KW // 2, 0, GRID_W - NA_KW)[:, :, None]
    kc = key_col[:, None, :]
    col_ok = (kc >= win_start) & (kc < win_start + NA_KW)
    dc = np.clip(kc - q_col[:, :, None] + NA_KW - 1, 0, 2 * NA_KW - 2)
    return row_idx, dr, key_col, col_ok, dc

def neighbourhood_attention(q, k, v, k_ctx, v_ctx, rpb):
    bn, s, h, d = q.shape
    rows = s // GRID_W
    ncb = GRID_W // NA_QC
    row_idx, dr, key_col, col_ok, dc = neighbourhood_tables(rows)
    kh = row_idx.shape[1]

    def gather(t):
        return t.reshape(bn, rows, GRID_W, h, d)[:, row_idx][:, :, :, key_col]
    kg, vg = gather(k), gather(v)
    qg = q.reshape(bn, rows, ncb, NA_QC, h, d)
    s_lat = jnp.einsum('brmqhd,brtmjhd->brmhqtj', qg, kg).astype(jnp.float32) * ATTN_SCALE
    bias = rpb[:, dr[:, None, None, :, None], dc[None, :, :, None, :]]
    s_lat = s_lat + bias.transpose(1, 2, 0, 3, 4, 5).astype(jnp.float32)
    s_lat = jnp.where(col_ok[:, None, :, None, :], s_lat, NEG_INF)
    s_lat = s_lat.reshape(s_lat.shape[:-2] + (kh * NA_KC,))
    s_ctx = jnp.einsum('brmqhd,bchd->brmhqc', qg, k_ctx).astype(jnp.float32) * ATTN_SCALE
    p = jax.nn.softmax(jnp.concatenate([s_lat, s_ctx], axis=-1), axis=-1)
    p_lat = p[..., :kh * NA_KC].reshape(p.shape[:-1] + (kh, NA_KC)).astype(v.dtype)
    p_ctx = p[..., kh * NA_KC:].astype(v.dtype)
    o = (jnp.einsum('brmhqtj,brtmjhd->brmqhd', p_lat, vg)
         + jnp.einsum('brmhqc,bchd->brmqhd', p_ctx, v_ctx))
    return o.reshape(bn, s, h * d)

def global_block_attention(q, k, v, k_ctx, v_ctx):
    bn, s, h, d = q.shape
    hkv = k.shape[2]
    nb = s // BLOCK
    k_all = jnp.concatenate([k_ctx, k], axis=1)
    v_all = jnp.concatenate([v_ctx, v], axis=1)
    qb = q.reshape(bn, nb, BLOCK, hkv, h // hkv, d).transpose(1, 0, 2, 3, 4, 5)

    def one_block(qblk):
        sc = jnp.einsum('bqkgd,bskd->bkgqs', qblk, k_all).astype(jnp.float32) * ATTN_SCALE
        p = jax.nn.softmax(sc, axis=-1).astype(v_all.dtype)
        return jnp.einsum('bkgqs,bskd->bqkgd', p, v_all)
    o = lax.map(one_block, qb)
    return o.transpose(1, 0, 2, 3, 4, 5).reshape(bn, s, h * d)

def even_mixer(u_ctx, u_lat, w_in, w_out, a_prm, sink, rope_ang, need_ctx):
    p_ctx = u_ctx @ w_in
    p_lat = u_lat @ w_in
    a_lat, a_ctx = rwkv7_mixer(p_ctx[..., :A_IN], p_lat[..., :A_IN], a_prm, need_ctx)
    qc, kc, vc = split_qkv(p_ctx[..., A_IN:], B_HEADS, B_KV_HEADS)
    ql, kl, vl = split_qkv(p_lat[..., A_IN:], B_HEADS, B_KV_HEADS)
    ql, kl = axial_rope(ql, rope_ang), axial_rope(kl, rope_ang)
    sink_g = sink.reshape(B_KV_HEADS, B_HEADS // B_KV_HEADS)
    b_lat = banded_window_attention(ql, kl, vl, kc, vc, sink_g)
    out_lat = jnp.concatenate([a_lat, b_lat], axis=-1) @ w_out
    if not need_ctx:
        return out_lat, None
    b_ctx = context_attention(qc, kc, vc, sink_g)
    return out_lat, jnp.concatenate([a_ctx, b_ctx], axis=-1) @ w_out

def odd_mixer(u_ctx, u_lat, w_in, w_out, rpb, q_gain, k_gain, rope_ang, need_ctx):
    p_ctx = u_ctx @ w_in
    p_lat = u_lat @ w_in
    cq_c, ck_c, cv_c = split_qkv(p_ctx[..., :C_IN], C_HEADS, C_HEADS)
    cq_l, ck_l, cv_l = split_qkv(p_lat[..., :C_IN], C_HEADS, C_HEADS)
    c_lat = neighbourhood_attention(cq_l, ck_l, cv_l, ck_c, cv_c, rpb)
    dq_c, dk_c, dv_c = split_qkv(p_ctx[..., C_IN:], D_HEADS, D_KV_HEADS)
    dq_l, dk_l, dv_l = split_qkv(p_lat[..., C_IN:], D_HEADS, D_KV_HEADS)
    dq_c, dk_c = rms_norm(dq_c, q_gain), rms_norm(dk_c, k_gain)
    dq_l = axial_rope(rms_norm(dq_l, q_gain), rope_ang)
    dk_l = axial_rope(rms_norm(dk_l, k_gain), rope_ang)
    d_lat = global_block_attention(dq_l, dk_l, dv_l, dk_c, dv_c)
    out_lat = jnp.concatenate([c_lat, d_lat], axis=-1) @ w_out
    if not need_ctx:
        return out_lat, None
    c_ctx_o = context_attention(cq_c, ck_c, cv_c)
    d_ctx_o = context_attention(dq_c, dk_c, dv_c)
    return out_lat, jnp.concatenate([c_ctx_o, d_ctx_o], axis=-1) @ w_out

def second_inputs(seed: int = 0) -> dict:
    key = jax.random.key(seed)
    ks = iter(jax.random.split(key, 40))
    nrm = lambda shape, scale: scale * jax.random.normal(next(ks), shape, jnp.float32)
    unif = lambda shape, lo, hi: jax.random.uniform(next(ks), shape, jnp.float32, lo, hi)
    D = D_MODEL
    return {
        "x": nrm((BATCH, SEQ, D), 1.0),
        "c": nrm((BATCH, D), 1.0),
        "ctx": nrm((BATCH, CTX_LEN, D), 1.0),
        "c_ctx": nrm((D,), 1.0),
        "w_ada": nrm((DEPTH, D, 6 * D), 0.5 * D ** -0.5),
        "b_ada": nrm((DEPTH, 6 * D), 0.02),
        "g_pre_mix": 1.0 + nrm((DEPTH, D), 0.05),
        "g_post_mix": 1.0 + nrm((DEPTH, D), 0.05),
        "g_pre_ff": 1.0 + nrm((DEPTH, D), 0.05),
        "g_post_ff": 1.0 + nrm((DEPTH, D), 0.05),
        "w_in_even": nrm((N_EVEN_2, D, EVEN_IN), D ** -0.5),
        "w_in_odd": nrm((N_ODD_2, D, ODD_IN), D ** -0.5),
        "w_out": nrm((DEPTH, MIX_WIDTH_2, D), MIX_WIDTH_2 ** -0.5),
        "w_ff1": nrm((DEPTH, D, D_FF), D ** -0.5),
        "w_ff2": nrm((DEPTH, D_FF, D), D_FF ** -0.5),
        "a_mu_prev": unif((N_EVEN_2, A_IN), 0.05, 0.45),
        "a_mu_next": unif((N_EVEN_2, A_IN), 0.05, 0.45),
        "a_w0": unif((N_EVEN_2, 2, A_WIDTH_2), -5.0, -0.5),
        "a_w2": nrm((N_EVEN_2, 2, DECAY_LORA, A_WIDTH_2), 0.1 * DECAY_LORA ** -0.5),
        "a_a0": nrm((N_EVEN_2, 2, A_WIDTH_2), 0.1),
        "a_a2": nrm((N_EVEN_2, 2, ICLR_LORA, A_WIDTH_2), 0.5 * ICLR_LORA ** -0.5),
        "a_g2": nrm((N_EVEN_2, GATE_LORA, A_WIDTH_2), GATE_LORA ** -0.5),
        "a_k_k": 0.85 + nrm((N_EVEN_2, A_WIDTH_2), 0.05),
        "a_k_a": 1.0 + nrm((N_EVEN_2, A_WIDTH_2), 0.05),
        "a_r_k": nrm((N_EVEN_2, A_HEADS_2, HEAD_DIM), 0.1),
        "a_gn_w": 1.0 + nrm((N_EVEN_2, A_WIDTH_2), 0.05),
        "a_gn_b": nrm((N_EVEN_2, A_WIDTH_2), 0.02),
        "b_sink": nrm((N_EVEN_2, B_HEADS), 0.5),
        "c_rpb": nrm((N_ODD_2, C_HEADS, 2 * NA_KH - 1, 2 * NA_KW - 1), 0.5),
        "d_q_gain": 1.0 + nrm((N_ODD_2, HEAD_DIM), 0.05),
        "d_k_gain": 1.0 + nrm((N_ODD_2, HEAD_DIM), 0.05),
    }

def second_block(x, c, ctx, c_ctx, w_ada, b_ada, g_pre_mix, g_post_mix, g_pre_ff, g_post_ff,
              w_in_even, w_in_odd, w_out, w_ff1, w_ff2,
              a_mu_prev, a_mu_next, a_w0, a_w2, a_a0, a_a2, a_g2, a_k_k, a_k_a, a_r_k, a_gn_w, a_gn_b,
              b_sink, c_rpb, d_q_gain, d_k_gain):
    rope_ang = axial_angles(x.shape[1])
    s_lat = jax.nn.silu(c)[:, None, :]
    s_ctx = jax.nn.silu(c_ctx)[None, None, :]
    h_lat, h_ctx = x, ctx
    for i in range(DEPTH):
        need_ctx = i < DEPTH - 1
        j = i // 2
        ml = jnp.split(s_lat @ w_ada[i] + b_ada[i], 6, axis=-1)
        mc = jnp.split(s_ctx @ w_ada[i] + b_ada[i], 6, axis=-1)
        u_lat = modulate(h_lat, g_pre_mix[i], ml[0], ml[1])
        u_ctx = modulate(h_ctx, g_pre_mix[i], mc[0], mc[1])
        if i % 2 == 0:
            a_prm = dict(mu_prev=a_mu_prev[j], mu_next=a_mu_next[j], w0=a_w0[j], w2=a_w2[j],
                         a0=a_a0[j], a2=a_a2[j], g2=a_g2[j], k_k=a_k_k[j], k_a=a_k_a[j],
                         r_k=a_r_k[j], gn_w=a_gn_w[j], gn_b=a_gn_b[j])
            o_lat, o_ctx = even_mixer(u_ctx, u_lat, w_in_even[j], w_out[i], a_prm, b_sink[j], rope_ang, need_ctx)
        else:
            o_lat, o_ctx = odd_mixer(u_ctx, u_lat, w_in_odd[j], w_out[i], c_rpb[j], d_q_gain[j], d_k_gain[j],
                                     rope_ang, need_ctx)
        h_lat = h_lat + ml[2] * rms_norm(o_lat, g_post_mix[i])
        f_lat = sqrelu_mlp(modulate(h_lat, g_pre_ff[i], ml[3], ml[4]), w_ff1[i], w_ff2[i])
        h_lat = h_lat + ml[5] * rms_norm(f_lat, g_post_ff[i])
        if need_ctx:
            h_ctx = h_ctx + mc[2] * rms_norm(o_ctx, g_post_mix[i])
            f_ctx = sqrelu_mlp(modulate(h_ctx, g_pre_ff[i], mc[3], mc[4]), w_ff1[i], w_ff2[i])
            h_ctx = h_ctx + mc[5] * rms_norm(f_ctx, g_post_ff[i])
    return h_lat


def setup_inputs(seed=0):
    out = dict(first_inputs(seed))
    for name, value in second_inputs(seed + 1).items():
        if name != "x":
            out[name + "_2"] = value
    return out


def reference(
    x, c, mix_ada_w, mix_ada_b, mix_ln_g, mix_ln_b, ab_w_in, ab_sgu_ln_g, ab_sgu_ln_b, ab_ws,
    ab_bs, ab_pool_w, ab_pool_scale, ab_w_out, cv_w_in, cv_dw, cv_dw_b, cv_ln_g, cv_ln_b,
    cv_w_out, ffn_ada_w, ffn_ada_b, ffn_w_up, ffn_dw, ffn_dw_b, ffn_w_down, ffn_ln_g, ffn_ln_b,
    c_2, ctx_2, c_ctx_2, w_ada_2, b_ada_2, g_pre_mix_2, g_post_mix_2, g_pre_ff_2, g_post_ff_2,
    w_in_even_2, w_in_odd_2, w_out_2, w_ff1_2, w_ff2_2, a_mu_prev_2, a_mu_next_2, a_w0_2,
    a_w2_2, a_a0_2, a_a2_2, a_g2_2, a_k_k_2, a_k_a_2, a_r_k_2, a_gn_w_2, a_gn_b_2, b_sink_2,
    c_rpb_2, d_q_gain_2, d_k_gain_2,
):
    x = first_block(
        x, c, mix_ada_w, mix_ada_b, mix_ln_g, mix_ln_b, ab_w_in, ab_sgu_ln_g, ab_sgu_ln_b,
        ab_ws, ab_bs, ab_pool_w, ab_pool_scale, ab_w_out, cv_w_in, cv_dw, cv_dw_b, cv_ln_g,
        cv_ln_b, cv_w_out, ffn_ada_w, ffn_ada_b, ffn_w_up, ffn_dw, ffn_dw_b, ffn_w_down,
        ffn_ln_g, ffn_ln_b,
    )
    return second_block(
        x, c_2, ctx_2, c_ctx_2, w_ada_2, b_ada_2, g_pre_mix_2, g_post_mix_2, g_pre_ff_2,
        g_post_ff_2, w_in_even_2, w_in_odd_2, w_out_2, w_ff1_2, w_ff2_2, a_mu_prev_2,
        a_mu_next_2, a_w0_2, a_w2_2, a_a0_2, a_a2_2, a_g2_2, a_k_k_2, a_k_a_2, a_r_k_2,
        a_gn_w_2, a_gn_b_2, b_sink_2, c_rpb_2, d_q_gain_2, d_k_gain_2,
    )


_drawn_inputs = setup_inputs


def setup_inputs(seed=0):
    import zlib

    import numpy as np

    out = dict(_drawn_inputs(seed))
    spreads = {}
    factors = {'g_post_mix_2': 2.832,
     'g_post_ff_2': 2.887,
     'a_w2_2': 8.0,
     'a_a0_2': 5.018,
     'a_gn_w_2': 4.969,
     'a_gn_b_2': 8.0,
     'b_sink_2': 8.0,
     'c_rpb_2': 5.148,
     'd_q_gain_2': 8.0,
     'd_k_gain_2': 8.0}
    for name, (base, spread) in spreads.items():
        noise = np.random.default_rng([zlib.crc32(name.encode()), seed]).standard_normal(out[name].shape)
        drawn = base * np.exp(spread * noise) if base else spread * noise
        out[name] = __import__('jax').numpy.asarray(drawn.astype(out[name].dtype))
    for name, factor in factors.items():
        out[name] = (out[name] * factor).astype(out[name].dtype)
    return out
```

```python
from contextlib import contextmanager

import numpy as np

import concourse.bass as bass
from concourse import mybir

ALU = mybir.AluOpType
ACT = mybir.ActivationFunctionType
AX_X = mybir.AxisListType.X
F32 = mybir.dt.float32
U8 = mybir.dt.uint8

P = 128
D = 1024
DK = D // P
SEQ, CTX = 512, 256
TOK = CTX + SEQ
LAT = slice(CTX, TOK)
CTX_T, LAT_T = CTX // P, SEQ // P
TOK_T = CTX_T + LAT_T
BANK = 512
NBANK = 8

DEPTH = 2
ALPHA = (2 * DEPTH) ** 0.25
LN_EPS = 1e-5
RMS_EPS = 1e-6
GN_EPS = 64e-5
A_HEADS = 4
FFN = ((8 * D // 3 + 127) // 128) * 128
FK = FFN // P
CONV_W = 31
DFF = 4 * D
HD = 64
GRID_W = 64
NEG_INF = -1e30
ATTN_SCALE = HD ** -0.5

CH = 64
NCH = TOK // CH
CTX_CH = CTX // CH
CW = CH + 1
DECAY = float(np.exp(-0.5))
LEVELS = 6

RING = 4
BLK = 2048


def feature_plan(n_cols, k_tiles=DK, width=256):
    return [(0, k_tiles, c, min(width, n_cols - c)) for c in range(0, n_cols, width)]


def token_plan(n_cols, k_tiles):
    return [(k, min(4, k_tiles - k), c, 512) for c in range(0, n_cols, 512) for k in range(0, k_tiles, 4)]


ADA1 = feature_plan(3 * D)
ADA2 = feature_plan(6 * D)
WEIGHTS = [
    ("ada_mix0", ADA1),
    ("ab_uv", token_plan(1024, DK)), ("ab_z", feature_plan(512)), ("ab_out", token_plan(D, DK)),
    ("ada_ffn0", ADA1), ("up0", feature_plan(2 * FFN)), ("down0", token_plan(D, FK)),
    ("ada_mix1", ADA1),
    ("cv_in", feature_plan(2 * D)), ("cv_out", token_plan(D, DK)),
    ("ada_ffn1", ADA1), ("up1", feature_plan(2 * FFN)), ("down1", token_plan(D, FK)),
    ("ada0", ADA2),
    ("b_qk", feature_plan(768)), ("b_v", feature_plan(P, width=P)),
    ("lora", feature_plan(256) + [(0, DK, 256, P)]),
    ("rkv0", feature_plan(768)), ("rkv1", feature_plan(768)),
    ("out0", token_plan(D, DK)), ("ff1_0", feature_plan(DFF)), ("ff2_0", token_plan(D, DFF // P)),
    ("ada1", ADA2),
    ("c_qk", feature_plan(1024)), ("c_v", token_plan(512, DK)),
    ("d_qk", feature_plan(768)), ("d_v", feature_plan(P, width=P)),
    ("out1", token_plan(D, DK)), ("ff1_1", feature_plan(DFF)), ("ff2_1", token_plan(D, DFF // P)),
]


class WeightStream:

    def __init__(self, nc, drams):
        self.ring = nc.alloc_sbuf_tensor("weight_ring", [P, RING, BLK], F32)
        self.landed = [nc.alloc_semaphore(f"weight_landed{i}") for i in range(RING)]
        self.used = nc.alloc_semaphore("weight_used")
        self.blocks, self.end_of = [], {}
        for name, plan in WEIGHTS:
            at = 0
            for _, nk, _, width in plan:
                n = nk * width
                self.blocks.append((drams[name][at:at + P * n].rearrange("(p n) -> p n", p=P), n, width))
                at += P * n
            self.end_of[name] = len(self.blocks)
        self.loads = self.takes = 0
        self.owed = False

    def load(self, sp, name=None):
        until = min(self.end_of.get(name, 0) + RING, len(self.blocks))
        while self.loads < until:
            i = self.loads
            if i >= RING:
                sp.wait_ge(self.used, i - RING + 1)
            source, n, _ = self.blocks[i]
            sp.dma_start(self.ring[:, i % RING, 0:n], source).then_inc(self.landed[i % RING], 16)
            self.loads += 1

    def used_by(self, product):
        if self.owed:
            product.then_inc(self.used, 1)
            self.owed = False

    def settle(self, pe):
        if self.owed:
            pe.drain().then_inc(self.used, 1)
            self.owed = False

    def take(self, pe):
        i = self.takes
        pe.wait_ge(self.landed[i % RING], 16 * (i // RING + 1))
        self.takes += 1
        _, n, width = self.blocks[i]
        return self.ring[:, i % RING, 0:n].rearrange("p (k n) -> p k n", n=width)


class Chain:

    def __init__(self, engine, sem):
        self.engine, self.sem, self.n = engine, sem, 0

    def __call__(self, ins):
        ins.then_inc(self.sem, 1)
        self.n += 1
        self.engine.wait_ge(self.sem, self.n)


def build(nc, dram, out_dram, debug=None):
    ps = [nc.alloc_psum_tensor(f"bank{i}", [P, BANK], F32) for i in range(NBANK)]
    weights = WeightStream(nc, dram)
    stored = nc.alloc_semaphore("output_stored")

    names = {}

    def unique(name):
        names[name] = names.get(name, 0) + 1
        return f"{name}.{names[name]}"

    def sb(name, shape, dt=F32):
        return nc.alloc_sbuf_tensor(unique(name), shape, dt)

    def sem(name):
        return nc.alloc_semaphore(unique(name))

    @contextmanager
    def stage():
        with nc.cleanup_on_exit():
            yield

    def rows(name):
        return dram[name].partition_broadcast(P)

    def dump(name, ap):
        if debug is None or name not in debug:
            return
        with stage():
            done = sem("dumped")
            with nc.Block() as block:
                @block.sync
                def _(sp):
                    sp.dma_start(debug[name], ap).then_inc(done, 16)
                    sp.wait_ge(done, 16)

    ident = sb("identity", [P, P])
    ones = sb("ones", [P, P])
    head_ones = sb("head_ones", [P, P])
    silu_c1 = sb("silu_c1", [P, DK, 1])
    silu_c2 = sb("silu_c2", [P, DK, 2])
    mod1 = sb("modulation1", [P, 3 * DK, 1])
    mod2 = sb("modulation2", [P, 6 * DK, 2])
    gains = sb("gains", [P, 4, DK])
    resid = sb("residual", [P, TOK_T, D])
    gate_rows = sb("gate_rows", [P, 2, D])
    hT = sb("hT", [P, DK, TOK])

    def feature_products(pe, n_blocks, segments, mm_done, evacuated, g0=0, src=None):
        src = hT if src is None else src
        g = g0
        for _ in range(n_blocks):
            w = weights.take(pe)
            tiles = w.shape[2] // P
            for j in range(tiles):
                for s, seg in enumerate(segments):
                    if g >= NBANK:
                        pe.wait_ge(evacuated, g - NBANK + 1)
                    n = seg.stop - seg.start
                    for k in range(DK):
                        last = nc.tensor.matmul(ps[g % NBANK][:, 0:n], w[:, k, j * P:(j + 1) * P],
                                                src[:, k, seg], start=(k == 0), stop=(k == DK - 1))
                        if k == 0:
                            weights.used_by(last)
                    last.then_inc(mm_done, 1)
                    g += 1
            weights.owed = True
        weights.settle(pe)
        return g

    def token_products(pe, k_tiles, n_halves, tiles, lhs, mm_done, evacuated, g0=0):
        T = len(tiles)
        for n in range(n_halves):
            for k0 in range(0, k_tiles, 4):
                w = weights.take(pe)
                for i, t in enumerate(tiles):
                    g = g0 + n * T + i
                    if k0 == 0 and g >= NBANK:
                        pe.wait_ge(evacuated, g - NBANK + 1)
                    for kk in range(w.shape[1]):
                        k = k0 + kk
                        last = nc.tensor.matmul(ps[g % NBANK][:, :], lhs(k, t), w[:, kk, :],
                                                start=(k == 0), stop=(k == k_tiles - 1))
                        if i == 0 and kk == 0:
                            weights.used_by(last)
                    if k == k_tiles - 1:
                        last.then_inc(mm_done, 1)
                if k == k_tiles - 1:
                    weights.owed = True
                else:
                    last.then_inc(weights.used, 1)
        weights.settle(pe)
        return g0 + n_halves * T

    def setup_stage():
        with stage():
            loaded, made, done = sem("loaded"), sem("memset"), sem("silu_done")
            with nc.Block() as block:
                @block.sync
                def _(sp):
                    sp.dma_start(silu_c1[:, :, 0], dram["c1"]).then_inc(loaded, 16)
                    sp.dma_start(silu_c2[:], dram["c2"]).then_inc(loaded, 16)
                    sp.dma_start(ident[:], dram["identity"]).then_inc(loaded, 16)
                    sp.dma_start(head_ones[:], dram["head_ones"]).then_inc(loaded, 16)
                    sp.dma_start(resid[:, CTX_T:TOK_T, :], dram["x"].rearrange("(t p) d -> p t d", p=P)).then_inc(loaded, 16)
                    sp.dma_start(resid[:, 0:CTX_T, :], dram["ctx"].rearrange("(t p) d -> p t d", p=P)).then_inc(loaded, 16)
                    weights.load(sp)
                    sp.wait_ge(loaded, 6 * 16)

                @block.vector
                def _(dve):
                    nc.vector.memset(ones[:], 1.0)

                @block.scalar
                def _(act):
                    act.wait_ge(loaded, 6 * 16)
                    nc.scalar.activation(silu_c1[:, :, 0], silu_c1[:, :, 0], ACT.Silu)
                    nc.scalar.activation(silu_c2[:], silu_c2[:], ACT.Silu)

    def ada_stage(name, bias_name, layer_row, mod, vec):
        nv = vec.shape[2]
        n_chunks = mod.shape[1]
        with stage():
            bias = sb("ada_bias", [P, n_chunks])
            loaded, chained = sem("loaded"), sem("vector_step")
            with nc.Block() as block:
                @block.sync
                def _(sp):
                    sp.dma_start(bias[:], dram[bias_name][layer_row]).then_inc(loaded, 16)
                    weights.load(sp, name)

                @block.tensor
                def _(pe):
                    for b in range(n_chunks // 2):
                        w = weights.take(pe)
                        for j in range(2):
                            col = (2 * b + j) * nv
                            for k in range(DK):
                                last = nc.tensor.matmul(ps[0][:, col:col + nv], w[:, k, j * P:(j + 1) * P],
                                                        vec[:, k, :], start=(k == 0), stop=(k == DK - 1))
                        last.then_inc(weights.used, 1)

                @block.vector
                def _(dve):
                    step = Chain(dve, chained)
                    dve.wait_ge(loaded, 16)
                    dve.wait_ge(weights.used, weights.end_of[name])
                    for v in range(nv):
                        got = ps[0][:, 0:n_chunks * nv].rearrange("p (c v) -> p c v", v=nv)[:, :, v]
                        step(nc.vector.tensor_tensor(mod[:, :, v], got, bias[:], ALU.add))
                    for c0 in range(DK, n_chunks, 3 * DK):
                        step(nc.vector.tensor_scalar(mod[:, c0:c0 + DK, :], mod[:, c0:c0 + DK, :], 1.0, None, ALU.add))

    def gate_row_stage(sources):
        with stage():
            rep = sb("gate_column_repeated", [P, 2, P])
            filled, mm_done, evac = sem("repeated"), sem("mm_done"), sem("row_copied")
            jobs = [(r, f, col) for r, cols in sources for f, col in enumerate(cols)]
            with nc.Block() as block:
                @block.vector
                def _(dve):
                    for i, (r, f, col) in enumerate(jobs):
                        if i >= 2:
                            dve.wait_ge(mm_done, i - 1)
                        nc.vector.tensor_scalar(rep[:, i % 2, :], ones[:], col, None, ALU.mult).then_inc(filled, 1)

                @block.tensor
                def _(pe):
                    for i, (r, f, col) in enumerate(jobs):
                        pe.wait_ge(filled, i + 1)
                        if i >= NBANK:
                            pe.wait_ge(evac, i - NBANK + 1)
                        nc.tensor.matmul(ps[i % NBANK][:, 0:P], rep[:, i % 2, :], ident[:],
                                         start=True, stop=True).then_inc(mm_done, 1)

                @block.scalar
                def _(act):
                    for i, (r, f, col) in enumerate(jobs):
                        act.wait_ge(mm_done, i + 1)
                        nc.scalar.copy(gate_rows[:, r, f * P:(f + 1) * P], ps[i % NBANK][:, 0:P]).then_inc(evac, 1)

    def to_features_stage(src, tiles, scale, shift, dst=None, rms=False):
        dst = hT if dst is None else dst
        segs = [(0, [t for t in tiles if t >= CTX_T]), (1, [t for t in tiles if t < CTX_T])]
        segs = [(v, ts) for v, ts in segs if ts]
        groups = [(f, v, ts) for f in range(DK) for v, ts in segs]
        with stage():
            mm_done, evac, chained = sem("mm_done"), sem("evacuated"), sem("vector_step")
            squared, normed = sem("squared"), sem("normed")
            act_chained = sem("scalar_step")
            if rms:
                scratch = sb("squares", [P, D])
                stats = sb("sum_of_squares", [P, TOK_T])
                root = sb("root", [P, TOK_T])
                hn = sb("normed", [P, TOK_T, D])
            x = hn if rms else src
            with nc.Block() as block:
                @block.scalar
                def _(act):
                    if rms:
                        step = Chain(act, act_chained)
                        for t in tiles:
                            step(nc.scalar.activation(scratch[:], src[:, t, :], ACT.Square, accum_out=stats[:, t:t + 1]))
                        act.sem_inc(squared, 1)
                        act.wait_ge(squared, 2)
                        nc.scalar.activation(root[:, tiles[0]:tiles[-1] + 1], stats[:, tiles[0]:tiles[-1] + 1], ACT.Sqrt).then_inc(squared, 1)

                @block.vector
                def _(dve):
                    step = Chain(dve, chained)
                    if rms:
                        t0, t1 = tiles[0], tiles[-1] + 1
                        dve.wait_ge(squared, 1)
                        nc.vector.tensor_scalar(stats[:, t0:t1], stats[:, t0:t1], 1.0 / D, RMS_EPS, ALU.mult, ALU.add).then_inc(squared, 1)
                        dve.wait_ge(squared, 3)
                        step(nc.vector.reciprocal(root[:, t0:t1], root[:, t0:t1]))
                        for t in tiles:
                            nc.vector.tensor_scalar(hn[:, t, :], src[:, t, :], root[:, t:t + 1], None, ALU.mult).then_inc(normed, 1)
                    for g, (f, v, ts) in enumerate(groups):
                        dve.wait_ge(mm_done, g + 1)
                        nc.vector.tensor_scalar(dst[:, f, ts[0] * P:(ts[-1] + 1) * P], ps[g % NBANK][:, 0:len(ts) * P],
                                                scale(f, v), shift(f, v), ALU.mult, ALU.add).then_inc(evac, 1)

                @block.tensor
                def _(pe):
                    if rms:
                        pe.wait_ge(normed, len(tiles))
                    for g, (f, v, ts) in enumerate(groups):
                        if g >= NBANK:
                            pe.wait_ge(evac, g - NBANK + 1)
                        for i, t in enumerate(ts):
                            last = nc.tensor.transpose(ps[g % NBANK][:, i * P:(i + 1) * P], x[:, t, f * P:(f + 1) * P], ident[:])
                        last.then_inc(mm_done, 1)

    def out_product_ln_stage(name, k_tiles, lhs, g_row, b_row):
        tiles = list(range(CTX_T, TOK_T))
        T = len(tiles)
        with stage():
            lng, lnb = sb("ln_gain", [P, D]), sb("ln_bias", [P, D])
            gated = sb("gated", [P, 2, BANK])
            stats = sb("bn_stats", [P, T, 2, 6])
            mv = sb("mean_var", [P, T, 2])
            inv = sb("inv_std", [P, T])
            nmean = sb("minus_mean_over_std", [P, T])
            loaded, mm_done, evac = sem("loaded"), sem("mm_done"), sem("evacuated")
            chained, var_ready, root_ready = sem("vector_step"), sem("var_ready"), sem("root_ready")
            inv_ready, centred = sem("inv_ready"), sem("centred")
            scaled, biased = sem("scaled"), sem("biased")
            with nc.Block() as block:
                @block.sync
                def _(sp):
                    sp.dma_start(lng[:], rows(g_row)).then_inc(loaded, 16)
                    sp.dma_start(lnb[:], rows(b_row)).then_inc(loaded, 16)
                    weights.load(sp, name)

                @block.tensor
                def _(pe):
                    token_products(pe, k_tiles, 2, tiles, lhs, mm_done, evac)

                @block.vector
                def _(dve):
                    step = Chain(dve, chained)
                    for n in range(2):
                        cols = slice(n * BANK, (n + 1) * BANK)
                        for i, t in enumerate(tiles):
                            g = n * T + i
                            dve.wait_ge(mm_done, g + 1)
                            ins = nc.vector.tensor_tensor(gated[:, g % 2, :], ps[g % NBANK][:], gate_rows[:, 0, cols], ALU.mult)
                            ins.then_inc(evac, 1)
                            dve.wait_ge(evac, g + 1)
                            step(nc.vector.scalar_tensor_tensor(out=resid[:, t, cols], in0=resid[:, t, cols], scalar=ALPHA,
                                                                in1=gated[:, g % 2, :], op0=ALU.mult, op1=ALU.add))
                            step(nc.vector.bn_stats(stats[:, i, n, :], resid[:, t, cols]))
                            if n == 1:
                                step(nc.vector.bn_aggr(mv[:, i, :], stats[:, i, :, :].rearrange("p a b -> p (a b)")))
                                nc.vector.tensor_scalar(inv[:, i:i + 1], mv[:, i, 1:2], LN_EPS, None, ALU.add).then_inc(var_ready, 1)
                    for i, t in enumerate(tiles):
                        dve.wait_ge(root_ready, i + 1)
                        step(nc.vector.reciprocal(inv[:, i:i + 1], inv[:, i:i + 1]))
                        nc.vector.scalar_tensor_tensor(out=nmean[:, i:i + 1], in0=mv[:, i, 0:1], scalar=-1.0,
                                                       in1=inv[:, i:i + 1], op0=ALU.mult, op1=ALU.mult).then_inc(inv_ready, 1)
                    dve.wait_ge(loaded, 32)
                    for i, t in enumerate(tiles):
                        dve.wait_ge(centred, i + 1)
                        nc.vector.tensor_tensor(resid[:, t, :], resid[:, t, :], lng[:], ALU.mult).then_inc(scaled, 1)

                @block.scalar
                def _(act):
                    for i in range(T):
                        act.wait_ge(var_ready, i + 1)
                        nc.scalar.activation(inv[:, i:i + 1], inv[:, i:i + 1], ACT.Sqrt).then_inc(root_ready, 1)
                    for i, t in enumerate(tiles):
                        act.wait_ge(inv_ready, i + 1)
                        nc.scalar.activation(resid[:, t, :], resid[:, t, :], ACT.Identity, bias=nmean[:, i:i + 1],
                                             scale=inv[:, i:i + 1]).then_inc(centred, 1)

                @block.gpsimd
                def _(pool):
                    pool.wait_ge(loaded, 32)
                    for i, t in enumerate(tiles):
                        pool.wait_ge(scaled, i + 1)
                        nc.gpsimd.tensor_tensor(resid[:, t, :], resid[:, t, :], lnb[:], ALU.add).then_inc(biased, 1)

    def ffn1_stages(layer):
        with stage():
            act_T = sb("ffn_hidden", [P, FK, SEQ])
            with stage():
                taps = sb("ffn_taps", [P, 2 * FK, 4])
                conv = sb("ffn_conv", [P, 4, SEQ])
                gel = sb("ffn_gelu", [P, 2, SEQ])
                loaded, mm_done = sem("loaded"), sem("mm_done")
                centre, chained = sem("centre_tap"), sem("vector_step")
                conv_done, gelu_done, multiplied = sem("conv_done"), sem("gelu_done"), sem("multiplied")
                with nc.Block() as block:
                    @block.sync
                    def _(sp):
                        sp.dma_start(taps[:], dram["ffn_taps"][layer]).then_inc(loaded, 16)
                        weights.load(sp, f"up{layer}")

                    @block.tensor
                    def _(pe):
                        feature_products(pe, FK, [LAT], mm_done, conv_done)

                    @block.scalar
                    def _(act):
                        act.wait_ge(loaded, 16)
                        for j in range(FK):
                            for half in range(2):
                                g = 2 * j + half
                                act.wait_ge(mm_done, g + 1)
                                if g >= 4:
                                    act.wait_ge(multiplied, g // 2 - 1)
                                nc.scalar.activation(conv[:, g % 4, :], ps[g % NBANK][:], ACT.Identity,
                                                     bias=taps[:, g, 3:4], scale=taps[:, g, 1:2]).then_inc(centre, 1)
                            act.wait_ge(conv_done, 2 * j + 1)
                            nc.scalar.activation(gel[:, j % 2, :], conv[:, (2 * j) % 4, :], ACT.Gelu_apprx_tanh).then_inc(gelu_done, 1)

                    @block.vector
                    def _(dve):
                        step = Chain(dve, chained)
                        for j in range(FK):
                            for half in range(2):
                                g = 2 * j + half
                                c, z = conv[:, g % 4, :], ps[g % NBANK]
                                dve.wait_ge(centre, g + 1)
                                step(nc.vector.scalar_tensor_tensor(out=c[:, 1:], in0=z[:, 0:SEQ - 1], scalar=taps[:, g, 0:1],
                                                                    in1=c[:, 1:], op0=ALU.mult, op1=ALU.add))
                                ins = nc.vector.scalar_tensor_tensor(out=c[:, 0:SEQ - 1], in0=z[:, 1:SEQ], scalar=taps[:, g, 2:3],
                                                                     in1=c[:, 0:SEQ - 1], op0=ALU.mult, op1=ALU.add)
                                ins.then_inc(conv_done, 1)
                            dve.wait_ge(gelu_done, j + 1)
                            dve.wait_ge(conv_done, 2 * j + 2)
                            nc.vector.tensor_tensor(act_T[:, j, :], gel[:, j % 2, :], conv[:, (2 * j + 1) % 4, :],
                                                    ALU.mult).then_inc(multiplied, 1)
            dump(f"act{layer}", act_T[:])
            out_product_ln_stage(f"down{layer}", FK, lambda k, t: act_T[:, k, (t - CTX_T) * P:(t - CTX_T + 1) * P],
                                 f"ffn_ln_g{layer}", f"ffn_ln_b{layer}")

    lat_tiles = list(range(CTX_T, TOK_T))

    def modulate1(ada, layer):
        ada_stage(ada, "ada_b_" + ada[4:7], layer, mod1, silu_c1)
        with stage():
            done = sem("gate_plus_one")
            with nc.Block() as block:
                @block.vector
                def _(dve):
                    nc.vector.tensor_scalar(mod1[:, 2 * DK:3 * DK, :], mod1[:, 2 * DK:3 * DK, :], 1.0, None, ALU.add)
        gate_row_stage([(0, [mod1[:, 2 * DK + f, :] for f in range(DK)])])
        to_features_stage(resid, lat_tiles, lambda f, v: mod1[:, DK + f, :], lambda f, v: mod1[:, f, :])

    def sgu_pool_mixer():
        with stage():
            u = sb("u", [P, LAT_T, 512])
            v = sb("v", [P, LAT_T, 512])
            PAD = 16
            ZW = SEQ + 2 * PAD
            z = sb("z_padded", [P, 4, ZW])
            mixT = sb("mixT", [P, DK, SEQ])
            with stage():
                lng, lnb = sb("sgu_gain", [P, 512]), sb("sgu_bias", [P, 512])
                stats = sb("bn_stats", [P, LAT_T, 6])
                mv = sb("mean_var", [P, LAT_T, 2])
                inv = sb("inv_std", [P, LAT_T])
                loaded, mm_done, evac = sem("loaded"), sem("mm_done"), sem("evacuated")
                chained, var_ready, root_ready, zeroed = sem("vector_step"), sem("var_ready"), sem("root_ready"), sem("zeroed")
                with nc.Block() as block:
                    @block.sync
                    def _(sp):
                        sp.dma_start(lng[:], rows("sgu_g")).then_inc(loaded, 16)
                        sp.dma_start(lnb[:], rows("sgu_b")).then_inc(loaded, 16)
                        weights.load(sp, "ab_z")

                    @block.tensor
                    def _(pe):
                        g = token_products(pe, DK, 2, lat_tiles, lambda k, t: hT[:, k, t * P:(t + 1) * P], mm_done, evac)
                        feature_products(pe, 2, [LAT], mm_done, evac, g0=g)

                    @block.gpsimd
                    def _(pool):
                        nc.gpsimd.memset(z[:, :, 0:PAD], 0.0).then_inc(zeroed, 1)
                        nc.gpsimd.memset(z[:, :, PAD + SEQ:ZW], 0.0).then_inc(zeroed, 1)

                    @block.scalar
                    def _(act):
                        for g in range(12):
                            act.wait_ge(mm_done, g + 1)
                            if g < 8:
                                to = (u if g < 4 else v)[:, g % 4, :]
                                nc.scalar.activation(to, ps[g % NBANK][:], ACT.Gelu_apprx_tanh).then_inc(evac, 1)
                            else:
                                nc.scalar.copy(z[:, g - 8, PAD:PAD + SEQ], ps[g % NBANK][:]).then_inc(evac, 1)
                        act.wait_ge(var_ready, 1)
                        nc.scalar.activation(inv[:], inv[:], ACT.Sqrt).then_inc(root_ready, 1)

                    @block.vector
                    def _(dve):
                        step = Chain(dve, chained)
                        for t in range(LAT_T):
                            dve.wait_ge(evac, 4 + t + 1)
                            step(nc.vector.bn_stats(stats[:, t, :], v[:, t, :]))
                            step(nc.vector.bn_aggr(mv[:, t, :], stats[:, t, :]))
                        nc.vector.tensor_scalar(inv[:], mv[:, :, 1], LN_EPS, None, ALU.add).then_inc(var_ready, 1)
                        dve.wait_ge(root_ready, 1)
                        step(nc.vector.reciprocal(inv[:], inv[:]))
                        dve.wait_ge(loaded, 32)
                        for t in range(LAT_T):
                            step(nc.vector.tensor_scalar(v[:, t, :], v[:, t, :], mv[:, t, 0:1], inv[:, t:t + 1], ALU.subtract, ALU.mult))
                            step(nc.vector.tensor_tensor(v[:, t, :], v[:, t, :], lng[:], ALU.mult))
                            step(nc.vector.tensor_tensor(v[:, t, :], v[:, t, :], lnb[:], ALU.add))
            with stage():
                wsT = sb("ws_transposed", [P, A_HEADS, P])
                bs = sb("spatial_bias", [P, A_HEADS])
                pool_w = sb("pool_w", [P, 4, P])
                pool_scale = sb("pool_scale", [P, 4])
                inv_count = sb("inv_count", [P, 4, SEQ])
                pooled = sb("pooled", [P, 4, SEQ])
                sums = sb("window_sums", [P, 2, ZW])
                loaded, mixed, gated, turned, copied = sem("loaded"), sem("mixed"), sem("gated"), sem("turned"), sem("copied")
                chained, pool_done, pool_mm = sem("vector_step"), sem("pooled"), sem("pool_product")
                n_loads = 5
                with nc.Block() as block:
                    @block.sync
                    def _(sp):
                        for dst, name in ((wsT, "wsT"), (bs, "bs"), (pool_w, "pool_w"), (pool_scale, "pool_scale")):
                            sp.dma_start(dst[:], dram[name]).then_inc(loaded, 16)
                        sp.dma_start(inv_count[:], dram["inv_count"].partition_broadcast(P)).then_inc(loaded, 16)

                    @block.tensor
                    def _(pe):
                        pe.wait_ge(loaded, 16 * n_loads)
                        for t in range(LAT_T):
                            for h in range(A_HEADS):
                                last = nc.tensor.matmul(ps[t][:, h * P:(h + 1) * P], wsT[:, h, :], v[:, t, h * P:(h + 1) * P],
                                                        start=True, stop=True)
                            last.then_inc(mixed, 1)
                        pe.wait_ge(gated, LAT_T)
                        for f in range(A_HEADS):
                            for t in range(LAT_T):
                                last = nc.tensor.transpose(ps[4 + f][:, t * P:(t + 1) * P], u[:, t, f * P:(f + 1) * P], ident[:])
                            last.then_inc(turned, 1)
                        for g in range(4):
                            pe.wait_ge(pool_done, g + 1)
                            nc.tensor.matmul(ps[g][:], pool_w[:, g, :], pooled[:, g, :], start=True, stop=True).then_inc(pool_mm, 1)

                    @block.vector
                    def _(dve):
                        step = Chain(dve, chained)
                        dve.wait_ge(loaded, 16 * n_loads)
                        for t in range(LAT_T):
                            dve.wait_ge(mixed, t + 1)
                            for h in range(A_HEADS):
                                cols = slice(h * P, (h + 1) * P)
                                last = nc.vector.scalar_tensor_tensor(out=u[:, t, cols], in0=ps[t][:, cols], scalar=bs[:, h:h + 1],
                                                                      in1=u[:, t, cols], op0=ALU.add, op1=ALU.mult)
                            last.then_inc(gated, 1)
                        for g in range(4):
                            window = 2 << g
                            src = z[:, g, :]
                            for level in range(g + 1):
                                lo, off = (2 << level) - 1, 1 << level
                                dst = sums[:, level % 2, :]
                                step(nc.vector.tensor_tensor(dst[:, lo:ZW], src[:, lo:ZW], src[:, lo - off:ZW - off], ALU.add))
                                src = dst
                            at = PAD + window // 2 - 1
                            step(nc.vector.tensor_tensor(pooled[:, g, :], src[:, at:at + SEQ], inv_count[:, g, :], ALU.mult))
                            ins = nc.vector.tensor_tensor(pooled[:, g, :], pooled[:, g, :], z[:, g, PAD:PAD + SEQ], ALU.subtract)
                            ins.then_inc(pool_done, 1)
                            dve.wait_ge(pool_done, g + 1)

                    @block.scalar
                    def _(act):
                        act.wait_ge(loaded, 16 * n_loads)
                        for f in range(A_HEADS):
                            act.wait_ge(turned, f + 1)
                            nc.scalar.copy(mixT[:, f, :], ps[4 + f][:]).then_inc(copied, 1)
                        for g in range(4):
                            act.wait_ge(pool_mm, g + 1)
                            nc.scalar.mul(mixT[:, 4 + g, :], ps[g][:], pool_scale[:, g:g + 1]).then_inc(copied, 1)
            dump("mixT", mixT[:])
            out_product_ln_stage("ab_out", DK, lambda k, t: mixT[:, k, (t - CTX_T) * P:(t - CTX_T + 1) * P], "mix_ln_g0", "mix_ln_b0")

    def conformer_mixer():
        HALF = CONV_W // 2
        with stage():
            zc = sb("conv_out", [P, DK, SEQ])
            with stage():
                zp = sb("glu_padded", [P, DK, SEQ + 2 * HALF])
                taps = sb("conv_taps", [P, DK, CONV_W + 1])
                gate = sb("sigmoid_gate", [P, 2, SEQ])
                loaded, zeroed, mm_done, evac = sem("loaded"), sem("zeroed"), sem("mm_done"), sem("evacuated")
                gated, chained, centre = sem("gate_done"), sem("vector_step"), sem("first_tap")
                with nc.Block() as block:
                    @block.sync
                    def _(sp):
                        sp.dma_start(taps[:], dram["cv_taps"]).then_inc(loaded, 16)
                        weights.load(sp, "cv_in")

                    @block.gpsimd
                    def _(pool):
                        nc.gpsimd.memset(zp[:, :, 0:HALF], 0.0).then_inc(zeroed, 1)
                        nc.gpsimd.memset(zp[:, :, HALF + SEQ:], 0.0).then_inc(zeroed, 1)

                    @block.tensor
                    def _(pe):
                        feature_products(pe, DK, [LAT], mm_done, evac)

                    @block.scalar
                    def _(act):
                        for j in range(DK):
                            act.wait_ge(mm_done, 2 * j + 2)
                            if j >= 2:
                                act.wait_ge(evac, 2 * (j - 1))
                            nc.scalar.activation(gate[:, j % 2, :], ps[(2 * j + 1) % NBANK][:], ACT.Sigmoid).then_inc(gated, 1)

                    @block.vector
                    def _(dve):
                        step = Chain(dve, chained)
                        dve.wait_ge(loaded, 16)
                        dve.wait_ge(zeroed, 2)
                        for j in range(DK):
                            dve.wait_ge(gated, j + 1)
                            ins = nc.vector.tensor_tensor(zp[:, j, HALF:HALF + SEQ], ps[(2 * j) % NBANK][:], gate[:, j % 2, :], ALU.mult)
                            ins.then_inc(evac, 2)
                            dve.wait_ge(evac, 2 * (j + 1))
                            step(nc.vector.tensor_scalar(zc[:, j, :], zp[:, j, 0:SEQ], taps[:, j, 0:1], taps[:, j, CONV_W:CONV_W + 1],
                                                         ALU.mult, ALU.add))
                            for i in range(1, CONV_W):
                                step(nc.vector.scalar_tensor_tensor(out=zc[:, j, :], in0=zp[:, j, i:i + SEQ], scalar=taps[:, j, i:i + 1],
                                                                    in1=zc[:, j, :], op0=ALU.mult, op1=ALU.add))
            with stage():
                cols = sb("cv_ln_columns", [P, 2, DK])
                sq = sb("squares", [P, 2, SEQ])
                mean, inv = sb("mean", [P, SEQ]), sb("inv_std", [P, SEQ])
                loaded, mm_mean, centred, squared, mm_var = sem("loaded"), sem("mean_product"), sem("centred"), sem("squared"), sem("var_product")
                chained, var_ready, root_ready, normed, applied = sem("vector_step"), sem("var_ready"), sem("root_ready"), sem("normed"), sem("silu_done")
                sq_used = sem("square_used")
                with nc.Block() as block:
                    @block.sync
                    def _(sp):
                        sp.dma_start(cols[:], dram["cv_ln"]).then_inc(loaded, 16)

                    @block.tensor
                    def _(pe):
                        for j in range(DK):
                            last = nc.tensor.matmul(ps[0][:], ones[:], zc[:, j, :], start=(j == 0), stop=(j == DK - 1))
                        last.then_inc(mm_mean, 1)
                        for j in range(DK):
                            pe.wait_ge(squared, j + 1)
                            nc.tensor.matmul(ps[1][:], ones[:], sq[:, j % 2, :], start=(j == 0), stop=(j == DK - 1)).then_inc(sq_used, 1)

                    @block.vector
                    def _(dve):
                        step = Chain(dve, chained)
                        dve.wait_ge(mm_mean, 1)
                        step(nc.vector.tensor_scalar(mean[:], ps[0][:], 1.0 / D, None, ALU.mult))
                        for j in range(DK):
                            nc.vector.tensor_tensor(zc[:, j, :], zc[:, j, :], mean[:], ALU.subtract).then_inc(centred, 1)
                        dve.wait_ge(sq_used, DK)
                        nc.vector.tensor_scalar(inv[:], ps[1][:], 1.0 / D, LN_EPS, ALU.mult, ALU.add).then_inc(var_ready, 1)
                        dve.wait_ge(root_ready, 1)
                        step(nc.vector.reciprocal(inv[:], inv[:]))
                        dve.wait_ge(centred, DK)
                        for j in range(DK):
                            nc.vector.tensor_tensor(zc[:, j, :], zc[:, j, :], inv[:], ALU.mult).then_inc(normed, 1)

                    @block.scalar
                    def _(act):
                        for j in range(DK):
                            act.wait_ge(centred, j + 1)
                            if j >= 2:
                                act.wait_ge(sq_used, j - 1)
                            nc.scalar.activation(sq[:, j % 2, :], zc[:, j, :], ACT.Square).then_inc(squared, 1)
                        act.wait_ge(var_ready, 1)
                        nc.scalar.activation(inv[:], inv[:], ACT.Sqrt).then_inc(root_ready, 1)
                        act.wait_ge(loaded, 16)
                        for j in range(DK):
                            act.wait_ge(normed, j + 1)
                            nc.scalar.activation(zc[:, j, :], zc[:, j, :], ACT.Silu, bias=cols[:, 1, j:j + 1],
                                                 scale=cols[:, 0, j:j + 1]).then_inc(applied, 1)
            out_product_ln_stage("cv_out", DK, lambda k, t: zc[:, k, (t - CTX_T) * P:(t - CTX_T + 1) * P], "mix_ln_g1", "mix_ln_b1")

    all_tiles = list(range(TOK_T))
    CTXS, HALVES = slice(0, CTX), (slice(0, BANK), slice(BANK, TOK))
    SHIFT, SCALE, GATE, FF_SHIFT, FF_SCALE, FF_GATE = (i * DK for i in range(6))

    def modulation2_stage(layer):
        ada_stage(f"ada{layer}", "b_ada", layer, mod2, silu_c2)
        with stage():
            loaded, multiplied = sem("loaded"), sem("multiplied")
            with nc.Block() as block:
                @block.sync
                def _(sp):
                    sp.dma_start(gains[:], dram["gains"][layer]).then_inc(loaded, 16)

                @block.vector
                def _(dve):
                    dve.wait_ge(loaded, 16)
                    for i, at in enumerate((SCALE, GATE, FF_SCALE, FF_GATE)):
                        for v in range(2):
                            nc.vector.tensor_tensor(mod2[:, at:at + DK, v], mod2[:, at:at + DK, v], gains[:, i, :],
                                                    ALU.mult).then_inc(multiplied, 1)

    def gates2_stage(at, streams):
        gate_row_stage([(v, [mod2[:, at + f, v:v + 1] for f in range(DK)]) for v in range(streams)])

    def modulated2_stage(at_shift, at_scale, tiles):
        to_features_stage(resid, tiles, lambda f, v: mod2[:, at_scale + f, v:v + 1],
                          lambda f, v: mod2[:, at_shift + f, v:v + 1], rms=True)

    def out_product_rms_stage(name, k_tiles, lhs, tiles, product):
        T = len(tiles)
        with stage():
            squares = sb("squares", [P, BANK])
            sums = sb("sums_of_squares", [P, T, 2])
            inv = sb("inv_rms", [P, T])
            mm_done, copied, squared = sem("mm_done"), sem("copied"), sem("squared")
            mean_ready, root_ready, chained, scaled, added = sem("mean_ready"), sem("root_ready"), sem("vector_step"), sem("scaled"), sem("added")
            with nc.Block() as block:
                @block.sync
                def _(sp):
                    weights.load(sp, name)

                @block.tensor
                def _(pe):
                    token_products(pe, k_tiles, 2, tiles, lhs, mm_done, squared)

                @block.scalar
                def _(act):
                    for n in range(2):
                        for i, t in enumerate(tiles):
                            g = n * T + i
                            act.wait_ge(mm_done, g + 1)
                            nc.scalar.copy(product[:, t, n * BANK:(n + 1) * BANK], ps[g % NBANK][:]).then_inc(copied, 1)
                            nc.scalar.activation(squares[:], ps[g % NBANK][:], ACT.Square, accum_out=sums[:, i, n:n + 1]).then_inc(squared, 1)
                            act.wait_ge(squared, g + 1)
                    act.wait_ge(mean_ready, 1)
                    nc.scalar.activation(inv[:], inv[:], ACT.Sqrt).then_inc(root_ready, 1)

                @block.vector
                def _(dve):
                    step = Chain(dve, chained)
                    dve.wait_ge(squared, 2 * T)
                    step(nc.vector.tensor_tensor(inv[:], sums[:, :, 0], sums[:, :, 1], ALU.add))
                    nc.vector.tensor_scalar(inv[:], inv[:], 1.0 / D, RMS_EPS, ALU.mult, ALU.add).then_inc(mean_ready, 1)
                    dve.wait_ge(root_ready, 1)
                    step(nc.vector.reciprocal(inv[:], inv[:]))
                    for i, t in enumerate(tiles):
                        row = gate_rows[:, 0 if t >= CTX_T else 1, :]
                        nc.vector.scalar_tensor_tensor(out=product[:, t, :], in0=product[:, t, :], scalar=inv[:, i:i + 1],
                                                       in1=row, op0=ALU.mult, op1=ALU.mult).then_inc(scaled, 1)

                @block.gpsimd
                def _(pool):
                    for i, t in enumerate(tiles):
                        pool.wait_ge(scaled, i + 1)
                        nc.gpsimd.tensor_tensor(resid[:, t, :], resid[:, t, :], product[:, t, :], ALU.add).then_inc(added, 1)

    def ffn2_stages(layer, tiles):
        segs = [CTXS, LAT] if tiles[0] == 0 else [LAT]
        FFK = DFF // P
        with stage():
            hidden = sb("ff_hidden", [P, FFK, TOK])
            with stage():
                relu = sb("relu", [P, 2, BANK])
                mm_done, relu_done, squared = sem("mm_done"), sem("relu_done"), sem("squared")
                with nc.Block() as block:
                    @block.sync
                    def _(sp):
                        weights.load(sp, f"ff1_{layer}")

                    @block.tensor
                    def _(pe):
                        feature_products(pe, FFK // 2, segs, mm_done, relu_done)

                    @block.scalar
                    def _(act):
                        for g in range(FFK * len(segs)):
                            seg = segs[g % len(segs)]
                            n = seg.stop - seg.start
                            act.wait_ge(mm_done, g + 1)
                            if g >= 2:
                                act.wait_ge(squared, g - 1)
                            nc.scalar.activation(relu[:, g % 2, 0:n], ps[g % NBANK][:, 0:n], ACT.Relu).then_inc(relu_done, 1)

                    @block.vector
                    def _(dve):
                        for g in range(FFK * len(segs)):
                            seg = segs[g % len(segs)]
                            n = seg.stop - seg.start
                            dve.wait_ge(relu_done, g + 1)
                            nc.vector.tensor_tensor(hidden[:, g // len(segs), seg], relu[:, g % 2, 0:n], relu[:, g % 2, 0:n],
                                                    ALU.mult).then_inc(squared, 1)
            flat = hT[:].rearrange("p k n -> p (k n)").rearrange("p (t d) -> p t d", d=D)
            out_product_rms_stage(f"ff2_{layer}", FFK, lambda k, t: hidden[:, k, t * P:(t + 1) * P], tiles, flat)

    def qkv_stage(qk_name, v_name, raw, n_q, vtok, q_segs):
        n_k = raw.shape[1] - n_q
        v_cols = vtok.shape[2]
        with stage():
            mm_done, copied = sem("mm_done"), sem("copied")
            segs = [(j, s) for j in range(n_q) for s in q_segs] + [(n_q + j, s) for j in range(n_k) for s in (CTXS, LAT)]
            with nc.Block() as block:
                @block.sync
                def _(sp):
                    weights.load(sp, v_name)

                @block.tensor
                def _(pe):
                    g = feature_products(pe, n_q // 2, q_segs, mm_done, copied)
                    g = feature_products(pe, n_k // 2, [CTXS, LAT], mm_done, copied, g0=g)
                    if v_cols == BANK:
                        token_products(pe, DK, 1, all_tiles, lambda k, t: hT[:, k, t * P:(t + 1) * P], mm_done, copied, g0=g)
                    else:
                        w = weights.take(pe)
                        for t in all_tiles:
                            pe.wait_ge(copied, g - NBANK + 1)
                            for k in range(DK):
                                last = nc.tensor.matmul(ps[g % NBANK][:, 0:v_cols], hT[:, k, t * P:(t + 1) * P], w[:, k, :],
                                                        start=(k == 0), stop=(k == DK - 1))
                            last.then_inc(mm_done, 1)
                            g += 1
                        weights.owed = True
                        weights.settle(pe)

                @block.scalar
                def _(act):
                    for g, (j, s) in enumerate(segs):
                        act.wait_ge(mm_done, g + 1)
                        nc.scalar.copy(raw[:, j, s], ps[g % NBANK][:, 0:s.stop - s.start]).then_inc(copied, 1)
                    for t in all_tiles:
                        g = len(segs) + t
                        act.wait_ge(mm_done, g + 1)
                        nc.scalar.copy(vtok[:, t, :], ps[g % NBANK][:, 0:v_cols]).then_inc(copied, 1)

    def qk_norm_stage(raw, n_q, q_cols):
        jobs = [(j, s) for j in range(raw.shape[1]) for s in ([q_cols] if j < n_q else HALVES)]
        with stage():
            gain = sb("head_gain", [P, 2])
            sq = sb("squares", [P, 2, BANK])
            inv = sb("inv_rms", [P, 2, BANK])
            loaded, squared, mm_done, mean_ready = sem("loaded"), sem("squared"), sem("mm_done"), sem("mean_ready")
            root_ready, chained, applied = sem("root_ready"), sem("vector_step"), sem("applied")
            with nc.Block() as block:
                @block.sync
                def _(sp):
                    sp.dma_start(gain[:], dram["d_gain"]).then_inc(loaded, 16)

                @block.scalar
                def _(act):
                    for i, (j, s) in enumerate(jobs):
                        n = s.stop - s.start
                        if i >= 2:
                            act.wait_ge(mm_done, i - 1)
                        nc.scalar.activation(sq[:, i % 2, 0:n], raw[:, j, s], ACT.Square).then_inc(squared, 1)
                        act.wait_ge(mean_ready, i + 1)
                        nc.scalar.activation(inv[:, i % 2, 0:n], inv[:, i % 2, 0:n], ACT.Sqrt).then_inc(root_ready, 1)

                @block.tensor
                def _(pe):
                    for i, (j, s) in enumerate(jobs):
                        n = s.stop - s.start
                        pe.wait_ge(squared, i + 1)
                        if i >= NBANK:
                            pe.wait_ge(mean_ready, i - NBANK + 1)
                        nc.tensor.matmul(ps[i % NBANK][:, 0:n], head_ones[:], sq[:, i % 2, 0:n], start=True, stop=True).then_inc(mm_done, 1)

                @block.vector
                def _(dve):
                    step = Chain(dve, chained)
                    dve.wait_ge(loaded, 16)
                    for i, (j, s) in enumerate(jobs):
                        n = s.stop - s.start
                        dve.wait_ge(mm_done, i + 1)
                        nc.vector.tensor_scalar(inv[:, i % 2, 0:n], ps[i % NBANK][:, 0:n], 1.0 / HD, RMS_EPS, ALU.mult, ALU.add).then_inc(mean_ready, 1)
                        dve.wait_ge(root_ready, i + 1)
                        step(nc.vector.reciprocal(inv[:, i % 2, 0:n], inv[:, i % 2, 0:n]))
                        col = gain[:, 0:1] if j < n_q else gain[:, 1:2]
                        step(nc.vector.scalar_tensor_tensor(out=raw[:, j, s], in0=raw[:, j, s], scalar=col,
                                                            in1=inv[:, i % 2, 0:n], op0=ALU.mult, op1=ALU.mult))

    def rope_stage(raw):
        n = raw.shape[1]
        with stage():
            turn, cos, sin = sb("turn", [P, P]), sb("cos", [P, SEQ]), sb("sin", [P, SEQ])
            part = sb("turned_part", [P, 2, SEQ])
            loaded, mm_done, turned, chained, added = sem("loaded"), sem("mm_done"), sem("turned"), sem("vector_step"), sem("added")
            with nc.Block() as block:
                @block.sync
                def _(sp):
                    for dst, name in ((turn, "rope_turn"), (cos, "rope_cos"), (sin, "rope_sin")):
                        sp.dma_start(dst[:], dram[name]).then_inc(loaded, 16)

                @block.tensor
                def _(pe):
                    pe.wait_ge(loaded, 48)
                    for j in range(n):
                        nc.tensor.matmul(ps[j][:], turn[:], raw[:, j, LAT], start=True, stop=True).then_inc(mm_done, 1)

                @block.vector
                def _(dve):
                    step = Chain(dve, chained)
                    dve.wait_ge(loaded, 48)
                    for j in range(n):
                        dve.wait_ge(mm_done, j + 1)
                        if j >= 2:
                            dve.wait_ge(added, j - 1)
                        step(nc.vector.tensor_tensor(part[:, j % 2, :], ps[j][:], sin[:], ALU.mult))
                        nc.vector.tensor_tensor(raw[:, j, LAT], raw[:, j, LAT], cos[:], ALU.mult).then_inc(turned, 1)

                @block.gpsimd
                def _(pool):
                    for j in range(n):
                        pool.wait_ge(turned, j + 1)
                        nc.gpsimd.tensor_tensor(raw[:, j, LAT], raw[:, j, LAT], part[:, j % 2, :], ALU.add).then_inc(added, 1)

    def spread_heads_stage(raw, n_q, k_low, k_high):
        with stage():
            zeroed, copied = sem("zeroed"), sem("copied")
            with nc.Block() as block:
                @block.gpsimd
                def _(pool):
                    nc.gpsimd.memset(k_low[HD:P], 0.0).then_inc(zeroed, 1)
                    nc.gpsimd.memset(k_high[0:HD], 0.0).then_inc(zeroed, 1)

                @block.scalar
                def _(act):
                    nc.scalar.copy(k_low[0:HD], raw[0:HD, n_q:, :]).then_inc(copied, 1)

                @block.vector
                def _(dve):
                    nc.vector.tensor_copy(k_high[HD:P], raw[HD:P, n_q:, :]).then_inc(copied, 1)

    def attention_stage(raw, k_halves, vtok, mixT, mix_at, jobs, kv_of, sink=None, mask=None, bias=None):
        items = [(job, h) for job in jobs for h in range(8)]
        N = len(items)
        with stage():
            sc = sb("scores", [P, 2, TOK])
            pr = sb("probs", [P, 2, TOK])
            pT = sb("probs_turned", [P, 2, TOK])
            o = sb("head_outputs", [P, 2, 512])
            top, total, esink, inv = (sb(n, [P, N]) for n in ("minus_max", "total", "exp_sink", "inv_total"))
            if bias is not None:
                NB = 4
                bias_ring = sb("bias_ring", [P, NB, SEQ])
                bias_landed = [sem(f"bias_landed{i}") for i in range(NB)]
            if mask is not None:
                mask_sb = sb("mask", [P, 3 * P])
            if sink is not None:
                sink_sb = sb("sink", [P, 8])
            loaded, scored, read, max_ready = sem("loaded"), sem("scored"), sem("scores_read"), sem("max_ready")
            exp_done, sink_done, turned, turn_copied, weighed, scaled = (sem(n) for n in (
                "exp_done", "sink_done", "probs_turned", "turn_copied", "weighed", "output_scaled"))
            o_turned, o_copied, chained = sem("outputs_turned"), sem("outputs_copied"), sem("vector_step")

            def spans(i):
                (qt, lat, _), h = items[i]
                n = CTX + (lat.stop - lat.start if lat else 0)
                keys = [0, 1] + ([c // P for c in range(lat.start, lat.stop, P)] if lat else [])
                return qt, h, lat, n, keys

            with nc.Block() as block:
                @block.sync
                def _(sp):
                    if mask is not None:
                        sp.dma_start(mask_sb[:], dram[mask]).then_inc(loaded, 16)
                    if sink is not None:
                        sp.dma_start(sink_sb[:], dram[sink].partition_broadcast(P)).then_inc(loaded, 16)
                    if bias is not None:
                        for i in range(N):
                            qt, h, lat, n, keys = spans(i)
                            if i >= NB:
                                sp.wait_ge(read, i - NB + 1)
                            sp.dma_start(bias_ring[:, i % NB, :], dram[bias][h, (qt - CTX_T) * P:(qt - CTX_T + 1) * P, :]).then_inc(bias_landed[i % NB], 16)

                @block.tensor
                def _(pe):
                    def score(i):
                        qt, h, lat, n, keys = spans(i)
                        if i >= 2:
                            pe.wait_ge(read, i - 1)
                        q = raw[:, h // 2, qt * P:(qt + 1) * P]
                        k = k_halves[h % 2][:, kv_of(h)[0], :]
                        b = 2 * (i % 2)
                        last = nc.tensor.matmul(ps[b][:, 0:CTX], q, k[:, 0:CTX], start=True, stop=True)
                        if lat:
                            last = nc.tensor.matmul(ps[b + 1][:, 0:n - CTX], q, k[:, lat], start=True, stop=True)
                        last.then_inc(scored, 1)

                    def turn(i):
                        qt, h, lat, n, keys = spans(i)
                        pe.wait_ge(exp_done, i + 1)
                        if i >= 1:
                            pe.wait_ge(turn_copied, i)
                        for m in range(len(keys)):
                            last = nc.tensor.transpose(ps[4 + m // 4][:, (m % 4) * P:(m % 4 + 1) * P],
                                                       pr[:, i % 2, m * P:(m + 1) * P], ident[:])
                        last.then_inc(turned, 1)

                    def weigh(i):
                        qt, h, lat, n, keys = spans(i)
                        pe.wait_ge(turn_copied, i + 1)
                        if i >= 1:
                            pe.wait_ge(scaled, i)
                        v = kv_of(h)[1]
                        for m, kt in enumerate(keys):
                            last = nc.tensor.matmul(ps[6][:, 0:HD], pT[:, i % 2, m * P:(m + 1) * P], vtok[:, kt, v],
                                                    start=(m == 0), stop=(m == len(keys) - 1))
                        last.then_inc(weighed, 1)

                    def turn_outputs(q):
                        pe.wait_ge(scaled, 8 * (q + 1))
                        if q >= 1:
                            pe.wait_ge(o_copied, q)
                        for f in range(4):
                            last = nc.tensor.transpose(ps[7][:, f * P:(f + 1) * P], o[:, q % 2, f * P:(f + 1) * P], ident[:])
                        last.then_inc(o_turned, 1)

                    for i in range(N + 3):
                        if i < N:
                            score(i)
                        if 1 <= i <= N:
                            turn(i - 1)
                        if 2 <= i <= N + 1:
                            weigh(i - 2)
                        if i >= 3 and (i - 2) % 8 == 0:
                            turn_outputs((i - 2) // 8 - 1)

                @block.vector
                def _(dve):
                    step = Chain(dve, chained)
                    if mask is not None or sink is not None:
                        dve.wait_ge(loaded, 16 * ((mask is not None) + (sink is not None)))

                    def front(i):
                        qt, h, lat, n, keys = spans(i)
                        b = 2 * (i % 2)
                        s = sc[:, i % 2, :]
                        dve.wait_ge(scored, i + 1)
                        if i >= 2:
                            dve.wait_ge(exp_done, i - 1)
                        first = nc.vector.tensor_scalar(s[:, 0:CTX], ps[b][:, 0:CTX], ATTN_SCALE, None, ALU.mult)
                        if lat:
                            step(first)
                            if bias is not None:
                                dve.wait_ge(bias_landed[i % NB], 16 * (i // NB + 1))
                                add = bias_ring[:, i % NB, :]
                            elif mask is not None:
                                add = mask_sb[:, items[i][0][2]]
                            if bias is not None or mask is not None:
                                last = nc.vector.scalar_tensor_tensor(out=s[:, CTX:n], in0=ps[b + 1][:, 0:n - CTX], scalar=ATTN_SCALE,
                                                                      in1=add, op0=ALU.mult, op1=ALU.add)
                            else:
                                last = nc.vector.tensor_scalar(s[:, CTX:n], ps[b + 1][:, 0:n - CTX], ATTN_SCALE, None, ALU.mult)
                        else:
                            last = first
                        last.then_inc(read, 1)
                        dve.wait_ge(read, i + 1)
                        step(nc.vector.tensor_reduce(top[:, i:i + 1], s[:, 0:n], AX_X, ALU.max))
                        if sink is not None:
                            step(nc.vector.tensor_tensor(top[:, i:i + 1], top[:, i:i + 1], sink_sb[:, h:h + 1], ALU.max))
                        nc.vector.tensor_scalar(top[:, i:i + 1], top[:, i:i + 1], -1.0, None, ALU.mult).then_inc(max_ready, 1)

                    def back(i):
                        qt, h, lat, n, keys = spans(i)
                        dve.wait_ge(sink_done if sink is not None else exp_done, i + 1)
                        if sink is not None:
                            step(nc.vector.tensor_tensor(total[:, i:i + 1], total[:, i:i + 1], esink[:, i:i + 1], ALU.add))
                        step(nc.vector.reciprocal(inv[:, i:i + 1], total[:, i:i + 1]))
                        q = i // 8
                        if i % 8 == 0 and q >= 2:
                            dve.wait_ge(o_turned, q - 1)
                        dve.wait_ge(weighed, i + 1)
                        nc.vector.tensor_scalar(o[:, q % 2, h * HD:(h + 1) * HD], ps[6][:, 0:HD], inv[:, i:i + 1], None,
                                                ALU.mult).then_inc(scaled, 1)

                    for i in range(N + 2):
                        if i < N:
                            front(i)
                        if i >= 2:
                            back(i - 2)

                @block.scalar
                def _(act):
                    if sink is not None:
                        act.wait_ge(loaded, 16 * ((mask is not None) + 1))

                    def exps(i):
                        qt, h, lat, n, keys = spans(i)
                        act.wait_ge(max_ready, i + 1)
                        if i >= 2:
                            act.wait_ge(turned, i - 1)
                        nc.scalar.activation(pr[:, i % 2, 0:n], sc[:, i % 2, 0:n], ACT.Exp, bias=top[:, i:i + 1],
                                             accum_out=total[:, i:i + 1]).then_inc(exp_done, 1)
                        if sink is not None:
                            nc.scalar.activation(esink[:, i:i + 1], sink_sb[:, h:h + 1], ACT.Exp, bias=top[:, i:i + 1]).then_inc(sink_done, 1)

                    def copy_turned(i):
                        qt, h, lat, n, keys = spans(i)
                        act.wait_ge(turned, i + 1)
                        if i >= 2:
                            act.wait_ge(weighed, i - 1)
                        first = nc.scalar.copy(pT[:, i % 2, 0:min(n, BANK)], ps[4][:, 0:min(n, BANK)])
                        if n > BANK:
                            nc.scalar.copy(pT[:, i % 2, BANK:n], ps[5][:, 0:n - BANK]).then_inc(turn_copied, 1)
                        else:
                            first.then_inc(turn_copied, 1)

                    def copy_outputs(q):
                        act.wait_ge(o_turned, q + 1)
                        qt = jobs[q][0]
                        nc.scalar.copy(mixT[:, mix_at:mix_at + 4, qt * P:(qt + 1) * P],
                                       ps[7][:].rearrange("p (f n) -> p f n", f=4)).then_inc(o_copied, 1)

                    for i in range(N + 3):
                        if i < N:
                            exps(i)
                        if 1 <= i <= N:
                            copy_turned(i - 1)
                        if i >= 3 and (i - 2) % 8 == 0:
                            copy_outputs((i - 2) // 8 - 1)

    def lat_cols(a, b):
        return slice(CTX + a * P, CTX + b * P)

    def windowed_attention(mixT):
        with stage():
            raw = sb("qk_b", [P, 6, TOK])
            vtok = sb("v_b", [P, TOK_T, P])
            qkv_stage("b_qk", "b_v", raw, 4, vtok, [CTXS, LAT])
            rope_stage(raw)
            k_low, k_high = sb("k_low", [P, 2, TOK]), sb("k_high", [P, 2, TOK])
            spread_heads_stage(raw, 4, k_low, k_high)
            kv = lambda h: (h // 4, slice((h // 4) * HD, (h // 4 + 1) * HD))
            jobs = [(t, None, None) for t in range(CTX_T)]
            for n in range(LAT_T):
                a, b = max(n - 1, 0), min(n + 2, LAT_T)
                jobs.append((CTX_T + n, lat_cols(a, b), slice((a - n + 1) * P, (b - n + 1) * P)))
            attention_stage(raw, (k_low, k_high), vtok, mixT, 4, jobs, kv, sink="b_sink", mask="window_mask")

    def odd_attention(mixT):
        jobs = [(CTX_T + n, LAT, None) for n in range(LAT_T)]
        with stage():
            raw = sb("qk_c", [P, 8, TOK])
            vtok = sb("v_c", [P, TOK_T, 512])
            qkv_stage("c_qk", "c_v", raw, 4, vtok, [LAT])
            k_low, k_high = sb("k_low", [P, 4, TOK]), sb("k_high", [P, 4, TOK])
            spread_heads_stage(raw, 4, k_low, k_high)
            attention_stage(raw, (k_low, k_high), vtok, mixT, 0, jobs, lambda h: (h // 2, slice(h * HD, (h + 1) * HD)), bias="rpb_table")
        with stage():
            raw = sb("qk_d", [P, 6, TOK])
            vtok = sb("v_d", [P, TOK_T, P])
            qkv_stage("d_qk", "d_v", raw, 4, vtok, [LAT])
            qk_norm_stage(raw, 4, LAT)
            rope_stage(raw)
            k_low, k_high = sb("k_low", [P, 2, TOK]), sb("k_high", [P, 2, TOK])
            spread_heads_stage(raw, 4, k_low, k_high)
            attention_stage(raw, (k_low, k_high), vtok, mixT, 4, jobs, lambda h: (h // 4, slice((h // 4) * HD, (h // 4 + 1) * HD)))

    R_MU, R_W0, R_A0, R_KK, R_KA, R_RK, R_GW, R_GB = 0, 30, 38, 46, 50, 54, 58, 62
    R_COLS = 66

    def shifted_products_stage(name, n_blocks, dests, mu_tiles, rcols, raw):
        with stage():
            keep = sb("mu_keep", [P, 15])
            mm_done, copied, chained, shifted = sem("mm_done"), sem("copied"), sem("vector_step"), sem("shifted")
            mu = rcols[:, R_MU:R_MU + 30].rearrange("p (j m) -> p j m", m=2)
            with nc.Block() as block:
                @block.sync
                def _(sp):
                    weights.load(sp, name)

                @block.tensor
                def _(pe):
                    feature_products(pe, n_blocks, [CTXS, LAT], mm_done, copied)

                @block.scalar
                def _(act):
                    for j in range(len(dests)):
                        for s, seg in enumerate((CTXS, LAT)):
                            g = 2 * j + s
                            act.wait_ge(mm_done, g + 1)
                            if j >= 2:
                                act.wait_ge(shifted, j - 1)
                            nc.scalar.copy(raw[:, j % 2, seg], ps[g % NBANK][:, 0:seg.stop - seg.start]).then_inc(copied, 1)

                @block.vector
                def _(dve):
                    step = Chain(dve, chained)
                    step(nc.vector.tensor_tensor(keep[:], mu[:, :, 0], mu[:, :, 1], ALU.add))
                    step(nc.vector.tensor_scalar(keep[:], keep[:], -1.0, 1.0, ALU.mult, ALU.add))
                    for j, (dst, m) in enumerate(zip(dests, mu_tiles)):
                        p = raw[:, j % 2, :]
                        dve.wait_ge(copied, 2 * j + 2)
                        step(nc.vector.tensor_scalar(dst, p, keep[:, m:m + 1], None, ALU.mult))
                        for seg in (CTXS, LAT):
                            a, b = seg.start, seg.stop
                            step(nc.vector.scalar_tensor_tensor(out=dst[:, a + 1:b], in0=p[:, a:b - 1], scalar=mu[:, m, 0:1],
                                                                in1=dst[:, a + 1:b], op0=ALU.mult, op1=ALU.add))
                            last = nc.vector.scalar_tensor_tensor(out=dst[:, a:b - 1], in0=p[:, a + 1:b], scalar=mu[:, m, 1:2],
                                                                  in1=dst[:, a:b - 1], op0=ALU.mult, op1=ALU.add)
                            if seg is CTXS:
                                step(last)
                        last.then_inc(shifted, 1)
                        dve.wait_ge(shifted, j + 1)

    def recurrence(mixT):
        flat = resid[:].rearrange("p t d -> p (t d)")
        flat2 = gate_rows[:].rearrange("p t d -> p (t d)")
        with stage():
            rcols = sb("recurrence_columns", [P, R_COLS])
            lora = sb("lora", [P, 3, TOK])
            with stage():
                loaded = sem("loaded")
                with nc.Block() as block:
                    @block.sync
                    def _(sp):
                        sp.dma_start(rcols[:], dram["r_cols"]).then_inc(loaded, 16)
                        sp.wait_ge(loaded, 16)
            raw = flat[:, 0:2 * TOK].rearrange("p (b n) -> p b n", b=2)
            shifted_products_stage("lora", 2, [lora[:, j, :] for j in range(3)], [12, 13, 14], rcols, raw)
            with stage():
                with nc.Block() as block:
                    @block.scalar
                    def _(act):
                        nc.scalar.activation(lora[:, 0, :], lora[:, 0, :], ACT.Tanh)
                        nc.scalar.activation(lora[:, 2, :], lora[:, 2, :], ACT.Sigmoid)
            r, k, v, kk = (sb(n, [P, 2, TOK]) for n in ("r", "k_then_y", "v", "kk"))
            iclr, kdir = sb("iclr_then_b", [P, 4, TOK]), sb("k_dir", [P, 4, TOK])
            run = sb("running_decay", [P, 4, NCH * CW])
            gam = sb("chunk_decay", [P, 3, 4, NCH])
            for half in range(2):
                shifted_products_stage(f"rkv{half}", 3, [x[:, j, :] for x in (r, k, v) for j in range(2)],
                                       [4 * x + 2 * half + j for x in range(3) for j in range(2)], rcols, raw)
                prepare_stage(half, rcols, lora, r, k, v, kk, iclr, kdir, run, gam, mixT, flat)
                if half == 0:
                    dump("kk", kk[:]); dump("kdir", kdir[:]); dump("run", run[:]); dump("bb", iclr[:]); dump("bv", mixT[:, 0:2, :])
                scan_stage(r, k, v, kk, iclr, kdir, run, gam, flat, flat2)
                if half == 0:
                    dump("y", k[:])
                head_norm_stage(half, rcols, lora, k, mixT, flat)

    def prepare_stage(half, rcols, lora, r, k, v, kk, iclr, kdir, run, gam, mixT, flat):
        f0 = 2 * half
        col = lambda at, f: rcols[:, at + f:at + f + 1]
        SW = NCH * CW
        sg = flat[:, 0:2 * SW].rearrange("p (b n) -> p b n", b=2)
        tmp = flat[:, 2 * SW:2 * SW + 2 * TOK].rearrange("p (b n) -> p b n", b=2)
        tmp2 = flat[:, 2 * SW + 2 * TOK:2 * SW + 3 * TOK]
        with stage():
            w2, a2 = sb("w2", [P, 2, 2 * P]), sb("a2", [P, 2, 2 * P])
            reset = sb("reset", [P, SW])
            omka = sb("one_minus_ka", [P, 4])
            loaded, zeroed, w_mm, w_sig, a_mm, a_sig, scanned = (sem(n) for n in (
                "loaded", "zeroed", "w_product", "w_sigmoid", "a_product", "a_sigmoid", "scanned"))
            kk_sq, kk_mm, kk_root, r_ready, r_mm, chained, kk_made = (sem(n) for n in (
                "kk_squared", "kk_product", "kk_root", "bonus_terms", "bonus_product", "vector_step", "kk_made"))
            sq_made = sem("kk_unnormed")
            tots = sem("totals")
            gam_made = sem("chunk_decays")
            with nc.Block() as block:
                @block.sync
                def _(sp):
                    sp.dma_start(w2[:], dram["w2"][half]).then_inc(loaded, 16)
                    sp.dma_start(a2[:], dram["a2"][half]).then_inc(loaded, 16)
                    sp.dma_start(reset[:], dram["reset"].partition_broadcast(P)).then_inc(loaded, 16)

                @block.gpsimd
                def _(pool):
                    for b in range(2):
                        nc.gpsimd.memset(sg[:, b, :], 0.0).then_inc(zeroed, 1)

                @block.tensor
                def _(pe):
                    pe.wait_ge(loaded, 48)
                    for i in range(4):
                        d, f = divmod(i, 2)
                        if i >= 2:
                            pe.wait_ge(w_sig, 2 * (i - 1))
                        for s, seg in enumerate(HALVES):
                            nc.tensor.matmul(ps[2 * (i % 2) + s][:, 0:seg.stop - seg.start], w2[:, d, f * P:(f + 1) * P],
                                             lora[:, 0, seg], start=True, stop=True).then_inc(w_mm, 1)
                        if i >= 2:
                            pe.wait_ge(a_sig, 2 * (i - 1))
                        for s, seg in enumerate(HALVES):
                            nc.tensor.matmul(ps[4 + 2 * (i % 2) + s][:, 0:seg.stop - seg.start], a2[:, d, f * P:(f + 1) * P],
                                             lora[:, 1, seg], start=True, stop=True).then_inc(a_mm, 1)
                    pe.wait_ge(w_sig, 8)
                    for f in range(2):
                        pe.wait_ge(kk_sq, f + 1)
                        for s, seg in enumerate(HALVES):
                            nc.tensor.matmul(ps[2 * f + s][:, 0:seg.stop - seg.start], head_ones[:], tmp[:, f, seg],
                                             start=True, stop=True).then_inc(kk_mm, 1)
                    pe.wait_ge(a_sig, 8)
                    for f in range(2):
                        pe.wait_ge(r_ready, f + 1)
                        for s, seg in enumerate(HALVES):
                            nc.tensor.matmul(ps[4 + 2 * f + s][:, 0:seg.stop - seg.start], head_ones[:], tmp[:, f, seg],
                                             start=True, stop=True).then_inc(r_mm, 1)

                @block.scalar
                def _(act):
                    act.wait_ge(zeroed, 2)
                    for i in range(4):
                        d, f = divmod(i, 2)
                        if i >= 2:
                            act.wait_ge(scanned, i - 1)
                        for s, seg in enumerate(HALVES):
                            n = (seg.stop - seg.start) // CH
                            c0 = seg.start // CH
                            to = sg[:, i % 2, :].rearrange("p (c w) -> p c w", w=CW)[:, c0:c0 + n, 1:CW]
                            act.wait_ge(w_mm, 2 * i + s + 1)
                            nc.scalar.activation(to, ps[2 * (i % 2) + s][:, 0:n * CH].rearrange("p (c w) -> p c w", w=CH), ACT.Sigmoid,
                                                 bias=rcols[:, R_W0 + 4 * d + f0 + f:R_W0 + 4 * d + f0 + f + 1]).then_inc(w_sig, 1)
                        for s, seg in enumerate(HALVES):
                            act.wait_ge(a_mm, 2 * i + s + 1)
                            nc.scalar.activation(iclr[:, i, seg], ps[4 + 2 * (i % 2) + s][:, 0:seg.stop - seg.start], ACT.Sigmoid,
                                                 bias=rcols[:, R_A0 + 4 * d + f0 + f:R_A0 + 4 * d + f0 + f + 1]).then_inc(a_sig, 1)
                    for f in range(2):
                        act.wait_ge(sq_made, f + 1)
                        nc.scalar.activation(tmp[:, f, :], kk[:, f, :], ACT.Square).then_inc(kk_sq, 1)
                    for f in range(2):
                        for s, seg in enumerate(HALVES):
                            act.wait_ge(kk_mm, 2 * f + s + 1)
                            nc.scalar.activation(tmp[:, f, seg], ps[2 * f + s][:, 0:seg.stop - seg.start], ACT.Sqrt).then_inc(kk_root, 1)
                    act.wait_ge(tots, 2)
                    nc.scalar.activation(gam[:, 0, :, :], gam[:, 1, :, :], ACT.Exp).then_inc(gam_made, 1)

                @block.vector
                def _(dve):
                    step = Chain(dve, chained)
                    for f in range(2):
                        nc.vector.tensor_scalar(kk[:, f, :], k[:, f, :], col(R_KK, f0 + f), None, ALU.mult).then_inc(sq_made, 1)
                    dve.wait_ge(loaded, 48)
                    for i in range(4):
                        dve.wait_ge(w_sig, 2 * i + 2)
                        nc.vector.tensor_tensor_scan(out=run[:, i, :], data0=reset[:], data1=sg[:, i % 2, :], initial=0.0,
                                                     op0=ALU.mult, op1=ALU.add).then_inc(scanned, 1)
                    dve.wait_ge(scanned, 4)
                    ends = run[:].rearrange("p i (c w) -> p i c w", w=CW)[:, :, :, CH]
                    nc.vector.tensor_scalar(gam[:, 1, :, :], ends, -DECAY, None, ALU.mult).then_inc(tots, 1)
                    nc.vector.tensor_scalar(gam[:, 2, :, :], ends, DECAY, None, ALU.mult).then_inc(tots, 1)
                    step(nc.vector.tensor_scalar(omka[:], rcols[:, R_KA:R_KA + 4], -1.0, 1.0, ALU.mult, ALU.add))
                    dve.wait_ge(kk_root, 4)
                    for f in range(2):
                        step(nc.vector.tensor_scalar(tmp[:, f, :], tmp[:, f, :], 1e-12, None, ALU.max))
                        step(nc.vector.reciprocal(tmp[:, f, :], tmp[:, f, :]))
                        step(nc.vector.tensor_tensor(kk[:, f, :], kk[:, f, :], tmp[:, f, :], ALU.mult))
                    dve.wait_ge(a_sig, 8)
                    for i in range(4):
                        d, f = divmod(i, 2)
                        step(nc.vector.tensor_scalar(kdir[:, i, :], iclr[:, i, :], col(R_KA, f0 + f), omka[:, f0 + f:f0 + f + 1], ALU.mult, ALU.add))
                        step(nc.vector.tensor_tensor(kdir[:, i, :], kdir[:, i, :], k[:, f, :], ALU.mult))
                        step(nc.vector.tensor_tensor(iclr[:, i, :], iclr[:, i, :], kk[:, f, :], ALU.mult))
                    for f in range(2):
                        step(nc.vector.tensor_tensor(tmp2, kdir[:, f, :], kdir[:, 2 + f, :], ALU.add))
                        nc.vector.scalar_tensor_tensor(out=tmp[:, f, :], in0=tmp2, scalar=col(R_RK, f0 + f), in1=r[:, f, :],
                                                       op0=ALU.mult, op1=ALU.mult).then_inc(r_ready, 1)
                        dve.wait_ge(r_ready, f + 1)
                    for f in range(2):
                        for s, seg in enumerate(HALVES):
                            dve.wait_ge(r_mm, 2 * f + s + 1)
                            step(nc.vector.tensor_tensor(mixT[:, f0 + f, seg], ps[4 + 2 * f + s][:, 0:seg.stop - seg.start], v[:, f, seg], ALU.mult))

    PE_MAKES = ["b_turned", "k_turned", "v_turned", "A_ab", "A_ak_T", "A_r_T", "N", "T0"] + \
        [x for l in range(1, LEVELS) for x in (f"X{l}", f"GX{l}", f"T{l}")][:-1] + ["Z", "U", "Y", "S"]
    DVE_MAKES = [f"a{d}{h}" for d in range(2) for h in range(2)] + ["r0", "r1", "A_ab", "A_ak_T", "A_r_T"] + \
        [f"G{l}" for l in range(LEVELS)] + ["Z", "Y0", "Y1", "S_sum", "S0", "S1"]
    ACT_MAKES = [f"e{j}" for j in range(9)] + ["b_turned", "k_turned", "v_turned", "T0"] + \
        [x for l in range(1, LEVELS) for x in (f"X{l}", f"T{l}")][:-1] + ["U"]
    POOL_MAKES = [f"{x}{d}{h}" for x in "bkv" for d in range(2) for h in range(2)] + ["G_init"]

    def scan_stage(r, y, v, kk, bb, kdir, run, gam, flat, flat2):
        with stage():
            def full(i):
                return flat[:, i * 512:(i + 1) * 512].rearrange("p (i n) -> p i n", i=4)
            aexp, bexp, kexp, vexp, A_ab, A_ak_T, G, T, X, Bt, Kt, V = (full(i) for i in range(12))
            U, Z, S = (flat2[:, i * 512:(i + 1) * 512].rearrange("p (i n) -> p i n", i=4) for i in range(3))
            A_r_T = flat2[:, 1536:2048].rearrange("p (m i n) -> p m i n", m=2, i=4)
            e = sb("decay_factors", [P, 3, 4, CH])
            rc = sb("r_decayed", [P, 4, CH])
            before = sb("mask_before", [P, 2, P])
            before_T = sb("mask_before_T", [P, 2, P])
            upto_T = sb("mask_upto_T", [P, 2, CH])
            level = sb("level_masks", [P, LEVELS, 2, P], U8)
            level_f32 = flat[:, 9 * 512:12 * 512]
            loaded, zeroed, levels_cast = sem("loaded"), sem("zeroed"), sem("levels_cast")
            made = {"PE": sem("product_made"), "DVE": sem("vector_made"), "ACT": sem("scalar_made"), "POOL": sem("pool_made")}
            order = {"PE": PE_MAKES, "DVE": DVE_MAKES, "ACT": ACT_MAKES, "POOL": POOL_MAKES}

            def need(eng, who, what, c):
                if c >= 0:
                    eng.wait_ge(made[who], c * len(order[who]) + order[who].index(what) + 1)

            def chunk(d, c):
                return c if d == 0 else (CTX_CH - 1 - c if c < CTX_CH else NCH + CTX_CH - 1 - c)

            def tokens(d, c):
                return slice(chunk(d, c) * CH, (chunk(d, c) + 1) * CH)

            def per_dir(mask):
                return mask.unsqueeze(2).broadcast_to([P, 2, 2, mask.shape[2]])

            def by_dir(x):
                return x.rearrange("p (d f) n -> p d f n", d=2)

            def bank(b, n=P):
                return ps[b][:, 0:4 * n].rearrange("p (i n) -> p i n", i=4)

            halves = [(slice(0, HD), slice(0, CH)), (slice(HD, P), slice(CH, P))]

            with nc.Block() as block:
                @block.sync
                def _(sp):
                    for dst, name in ((before, "mask_before"), (before_T, "mask_before_T"), (upto_T, "mask_upto_T")):
                        sp.dma_start(dst[:], dram[name]).then_inc(loaded, 16)
                    sp.dma_start(level_f32, dram["level_masks"]).then_inc(loaded, 16)

                @block.gpsimd
                def _(pool):
                    for x in (aexp, bexp, kexp, vexp, S, y[:]):
                        nc.gpsimd.memset(x, 0.0).then_inc(zeroed, 1)
                    pool.wait_ge(zeroed, 6)
                    for c in range(NCH):
                        need(pool, "PE", "A_r_T", c - 1)
                        for d in range(2):
                            need(pool, "ACT", "e2" if d == 0 else "e8", c)
                            for h, (rows_, cols) in enumerate(halves):
                                nc.gpsimd.tensor_tensor(bexp[rows_, 2 * d:2 * d + 2, cols], bb[rows_, 2 * d:2 * d + 2, tokens(d, c)],
                                                        e[rows_, 2, 2 * d:2 * d + 2, :], ALU.mult).then_inc(made["POOL"], 1)
                        for d in range(2):
                            for h, (rows_, cols) in enumerate(halves):
                                nc.gpsimd.tensor_tensor(kexp[rows_, 2 * d:2 * d + 2, cols], kdir[rows_, 2 * d:2 * d + 2, tokens(d, c)],
                                                        e[rows_, 2, 2 * d:2 * d + 2, :], ALU.mult).then_inc(made["POOL"], 1)
                        for d in range(2):
                            for h, (rows_, cols) in enumerate(halves):
                                nc.gpsimd.tensor_copy(vexp[rows_, 2 * d:2 * d + 2, cols], v[rows_, :, tokens(d, c)]).then_inc(made["POOL"], 1)
                        need(pool, "PE", "U", c - 1)
                        need(pool, "POOL", "v11", c)
                        nc.gpsimd.tensor_copy(G, ident[:].unsqueeze(1).broadcast_to([P, 4, P])).then_inc(made["POOL"], 1)
                        need(pool, "POOL", "G_init", c)

                @block.scalar
                def _(act):
                    R = run[:].rearrange("p i (c w) -> p i c w", w=CW)
                    act.wait_ge(levels_cast, 1)
                    for c in range(NCH):
                        need(act, "DVE", "r1", c - 1)
                        need(act, "POOL", "k11", c - 1)
                        x = R[:, 0:2, chunk(0, c), :]
                        for j, (lo, sign) in enumerate(((0, -DECAY), (1, -DECAY), (1, DECAY))):
                            nc.scalar.activation(e[:, j, 0:2, :], x[:, :, lo:lo + CH], ACT.Exp, scale=sign).then_inc(made["ACT"], 1)
                        cb = chunk(1, c)
                        for j, (lo, sign, total) in enumerate(((1, DECAY, 1), (0, DECAY, 1), (0, -DECAY, 2))):
                            for i in (2, 3):
                                nc.scalar.activation(e[:, j, i, :], R[:, i, cb, lo:lo + CH], ACT.Exp, scale=sign,
                                                     bias=gam[:, total, i, cb:cb + 1]).then_inc(made["ACT"], 1)
                        for name, dst, b in (("b_turned", Bt, 0), ("k_turned", Kt, 1), ("v_turned", V, 2)):
                            need(act, "PE", name, c)
                            nc.scalar.copy(dst, bank(b)).then_inc(made["ACT"], 1)
                        need(act, "PE", "T0", c)
                        nc.scalar.copy(T, bank(3)).then_inc(made["ACT"], 1)
                        for l in range(1, LEVELS):
                            need(act, "PE", f"X{l}", c)
                            nc.scalar.copy(X, bank(6)).then_inc(made["ACT"], 1)
                            if l < LEVELS - 1:
                                need(act, "PE", f"T{l}", c)
                                nc.scalar.copy(T, bank(3)).then_inc(made["ACT"], 1)
                        need(act, "PE", "U", c)
                        nc.scalar.copy(U, bank(5)).then_inc(made["ACT"], 1)

                @block.vector
                def _(dve):
                    dve.wait_ge(loaded, 64)
                    nc.vector.tensor_copy(level[:].rearrange("p l d n -> p (l d n)"), level_f32).then_inc(levels_cast, 1)
                    dve.wait_ge(levels_cast, 1)
                    dve.wait_ge(zeroed, 6)
                    for c in range(NCH):
                        need(dve, "PE", "Z", c - 1)
                        for d in range(2):
                            need(dve, "ACT", "e0" if d == 0 else "e4", c)
                            for h, (rows_, cols) in enumerate(halves):
                                nc.vector.scalar_tensor_tensor(out=aexp[rows_, 2 * d:2 * d + 2, cols], in0=kk[rows_, :, tokens(d, c)], scalar=-1.0,
                                                               in1=e[rows_, 0, 2 * d:2 * d + 2, :], op0=ALU.mult, op1=ALU.mult).then_inc(made["DVE"], 1)
                        for d in range(2):
                            need(dve, "ACT", "e1" if d == 0 else "e6", c)
                            nc.vector.tensor_tensor(rc[:, 2 * d:2 * d + 2, :], r[:, :, tokens(d, c)], e[:, 1, 2 * d:2 * d + 2, :],
                                                    ALU.mult).then_inc(made["DVE"], 1)
                        need(dve, "PE", "A_ab", c)
                        nc.vector.tensor_tensor(by_dir(A_ab), by_dir(bank(3)), per_dir(before[:]), ALU.mult).then_inc(made["DVE"], 1)
                        need(dve, "PE", "A_ak_T", c)
                        nc.vector.tensor_tensor(by_dir(A_ak_T), by_dir(bank(4)), per_dir(before_T[:]), ALU.mult).then_inc(made["DVE"], 1)
                        need(dve, "PE", "A_r_T", c)
                        for m in range(2):
                            ins = nc.vector.tensor_tensor(by_dir(A_r_T[:, m]), by_dir(ps[5][:, m * 256:(m + 1) * 256].rearrange("p (i n) -> p i n", i=4)),
                                                          per_dir(upto_T[:]), ALU.mult)
                        ins.then_inc(made["DVE"], 1)
                        for l in range(LEVELS):
                            need(dve, "POOL", "G_init", c)
                            need(dve, "PE", "N" if l == 0 else f"GX{l}", c)
                            nc.vector.copy_predicated(by_dir(G), per_dir(level[:, l]), by_dir(bank(7))).then_inc(made["DVE"], 1)
                        need(dve, "PE", "Z", c)
                        nc.vector.tensor_copy(Z, bank(4)).then_inc(made["DVE"], 1)
                        need(dve, "PE", "Y", c)
                        for d in range(2):
                            cols = tokens(d, c)
                            if d == 1:
                                need(dve, "DVE", "Y0", c)
                            nc.vector.tensor_tensor(y[:, :, cols], y[:, :, cols], bank(0, CH)[:, 2 * d:2 * d + 2, :], ALU.add).then_inc(made["DVE"], 1)
                        need(dve, "PE", "S", c)
                        nc.vector.tensor_tensor(S, S, bank(1), ALU.add).then_inc(made["DVE"], 1)
                        need(dve, "DVE", "S_sum", c)
                        for d in range(2):
                            decay = gam[:, 0, 2 * d:2 * d + 2, chunk(d, c)].unsqueeze(2).broadcast_to([P, 2, P])
                            nc.vector.tensor_tensor(S[:, 2 * d:2 * d + 2, :], S[:, 2 * d:2 * d + 2, :], decay, ALU.mult).then_inc(made["DVE"], 1)
                        need(dve, "DVE", "S1", c)

                @block.tensor
                def _(pe):
                    def four(out, lhs, rhs, start=True, stop=True):
                        for i in range(4):
                            last = nc.tensor.matmul(out[:, i, :], lhs[:, i, :], rhs[:, i, :], start=start, stop=stop)
                        return last

                    def turn(out, x):
                        for i in range(4):
                            last = nc.tensor.transpose(out[:, i, :], x[:, i, :], ident[:])
                        return last

                    def sums(out, terms):
                        for i in range(4):
                            for n, (lhs, rhs) in enumerate(terms):
                                last = nc.tensor.matmul(out[:, i, :], lhs[:, i, :], rhs[:, i, :], start=(n == 0), stop=(n == len(terms) - 1))
                        return last

                    for c in range(NCH):
                        need(pe, "POOL", "v11", c)
                        need(pe, "DVE", "S1", c - 1)
                        turn(bank(0), bexp).then_inc(made["PE"], 1)
                        turn(bank(1), kexp).then_inc(made["PE"], 1)
                        turn(bank(2), vexp).then_inc(made["PE"], 1)
                        need(pe, "DVE", "r1", c)
                        four(bank(3), aexp, bexp).then_inc(made["PE"], 1)
                        four(bank(4), kexp, aexp).then_inc(made["PE"], 1)
                        need(pe, "ACT", "U", c - 1)
                        for m, x in enumerate((bexp, kexp)):
                            last = four(ps[5][:, m * 256:(m + 1) * 256].rearrange("p (i n) -> p i n", i=4), x, rc)
                        last.then_inc(made["PE"], 1)
                        need(pe, "DVE", "A_ab", c)
                        for i in range(4):
                            last = nc.tensor.matmul(bank(7)[:, i, :], A_ab[:, i, :], ident[:], start=True, stop=True)
                        last.then_inc(made["PE"], 1)
                        need(pe, "DVE", "G0", c)
                        turn(bank(3), G).then_inc(made["PE"], 1)
                        for l in range(1, LEVELS):
                            four(bank(6), A_ab, G).then_inc(made["PE"], 1)
                            need(pe, "ACT", f"X{l}", c)
                            need(pe, "ACT", f"T{l - 1}", c)
                            four(bank(7), T, X).then_inc(made["PE"], 1)
                            need(pe, "DVE", f"G{l}", c)
                            if l < LEVELS - 1:
                                turn(bank(3), G).then_inc(made["PE"], 1)
                        need(pe, "ACT", "v_turned", c)
                        need(pe, "DVE", "A_ak_T", c)
                        sums(bank(4), [(aexp, S), (A_ak_T, V)]).then_inc(made["PE"], 1)
                        need(pe, "DVE", "Z", c)
                        four(bank(5), G, Z).then_inc(made["PE"], 1)
                        need(pe, "ACT", "U", c)
                        need(pe, "DVE", "A_r_T", c)
                        sums(bank(0, CH), [(S, rc), (U, A_r_T[:, 0]), (V, A_r_T[:, 1])]).then_inc(made["PE"], 1)
                        sums(bank(1), [(Bt, U), (Kt, V)]).then_inc(made["PE"], 1)

    def head_norm_stage(half, rcols, lora, y, mixT, flat):
        f0 = 2 * half
        inv = flat[:, 0:2 * TOK].rearrange("p (b n) -> p b n", b=2)
        jobs = [(f, s) for f in range(2) for s in HALVES]
        with stage():
            g2 = sb("g2", [P, 2 * P])
            loaded, mean_mm, centred, squared, var_mm, var_ready, root_ready, gate_mm, chained = (sem(n) for n in (
                "loaded", "mean_product", "centred", "squared", "var_product", "var_ready", "root_ready", "gate_product", "vector_step"))
            with nc.Block() as block:
                @block.sync
                def _(sp):
                    sp.dma_start(g2[:], dram["g2"][half]).then_inc(loaded, 16)

                @block.tensor
                def _(pe):
                    for i, (f, s) in enumerate(jobs):
                        nc.tensor.matmul(ps[i][:, 0:s.stop - s.start], head_ones[:], y[:, f, s], start=True, stop=True).then_inc(mean_mm, 1)
                    for i, (f, s) in enumerate(jobs):
                        pe.wait_ge(squared, i + 1)
                        nc.tensor.matmul(ps[4 + i][:, 0:s.stop - s.start], head_ones[:], inv[:, f, s], start=True, stop=True).then_inc(var_mm, 1)
                    pe.wait_ge(loaded, 16)
                    for i, (f, s) in enumerate(jobs):
                        nc.tensor.matmul(ps[i][:, 0:s.stop - s.start], g2[:, f * P:(f + 1) * P], lora[:, 2, s], start=True, stop=True).then_inc(gate_mm, 1)

                @block.scalar
                def _(act):
                    for i, (f, s) in enumerate(jobs):
                        act.wait_ge(centred, i + 1)
                        nc.scalar.activation(inv[:, f, s], y[:, f, s], ACT.Square).then_inc(squared, 1)
                    for i, (f, s) in enumerate(jobs):
                        act.wait_ge(var_ready, i + 1)
                        nc.scalar.activation(inv[:, f, s], inv[:, f, s], ACT.Sqrt).then_inc(root_ready, 1)

                @block.vector
                def _(dve):
                    step = Chain(dve, chained)
                    for i, (f, s) in enumerate(jobs):
                        dve.wait_ge(mean_mm, i + 1)
                        nc.vector.scalar_tensor_tensor(out=y[:, f, s], in0=ps[i][:, 0:s.stop - s.start], scalar=-1.0 / HD, in1=y[:, f, s],
                                                       op0=ALU.mult, op1=ALU.add).then_inc(centred, 1)
                    for i, (f, s) in enumerate(jobs):
                        dve.wait_ge(var_mm, i + 1)
                        nc.vector.tensor_scalar(inv[:, f, s], ps[4 + i][:, 0:s.stop - s.start], 1.0 / HD, GN_EPS, ALU.mult, ALU.add).then_inc(var_ready, 1)
                    dve.wait_ge(centred, 4)
                    for i, (f, s) in enumerate(jobs):
                        dve.wait_ge(root_ready, i + 1)
                        step(nc.vector.reciprocal(inv[:, f, s], inv[:, f, s]))
                        step(nc.vector.tensor_tensor(y[:, f, s], y[:, f, s], inv[:, f, s], ALU.mult))
                        step(nc.vector.tensor_scalar(y[:, f, s], y[:, f, s], rcols[:, R_GW + f0 + f:R_GW + f0 + f + 1],
                                                     rcols[:, R_GB + f0 + f:R_GB + f0 + f + 1], ALU.mult, ALU.add))
                        step(nc.vector.tensor_tensor(y[:, f, s], y[:, f, s], mixT[:, f0 + f, s], ALU.add))
                        dve.wait_ge(gate_mm, i + 1)
                        step(nc.vector.tensor_tensor(mixT[:, f0 + f, s], y[:, f, s], ps[i][:, 0:s.stop - s.start], ALU.mult))

    parked = nc.dram_tensor("parked_residual", (P, TOK_T * D), F32, kind="Internal").ap()

    def park_stage(to_dram):
        with stage():
            moved = sem("moved")
            here = resid[:].rearrange("p t d -> p (t d)")
            with nc.Block() as block:
                @block.sync
                def _(sp):
                    sp.dma_start(parked if to_dram else here, here if to_dram else parked).then_inc(moved, 16)
                    sp.wait_ge(moved, 16)

    def second_block():
        for layer in range(DEPTH):
            tiles = all_tiles if layer == 0 else lat_tiles
            streams = 2 if layer == 0 else 1
            modulation2_stage(layer)
            modulated2_stage(SHIFT, SCALE, all_tiles)
            dump(f"u{layer}", hT[:])
            with stage():
                mixT = sb("mixT", [P, DK, TOK])
                if layer == 0:
                    windowed_attention(mixT)
                    dump("battn", mixT[:, 4:8, :])
                    park_stage(True)
                    recurrence(mixT)
                    dump("rwkv", mixT[:, 0:4, :])
                    park_stage(False)
                else:
                    odd_attention(mixT)
                    dump("odd", mixT[:, :, LAT])
                gates2_stage(GATE, streams)
                product = hT[:].rearrange("p k n -> p (k n)").rearrange("p (t d) -> p t d", d=D)
                out_product_rms_stage(f"out{layer}", DK, lambda k, t: mixT[:, k, t * P:(t + 1) * P], tiles, product)
            dump(f"h{layer}", resid[:])
            gates2_stage(FF_GATE, streams)
            modulated2_stage(FF_SHIFT, FF_SCALE, tiles)
            ffn2_stages(layer, tiles)
            dump(f"g{layer}", resid[:])
        with stage():
            with nc.Block() as block:
                @block.sync
                def _(sp):
                    sp.dma_start(out_dram[0].rearrange("(t p) d -> p t d", p=P), resid[:, CTX_T:TOK_T, :]).then_inc(stored, 16)
                    sp.wait_ge(stored, 16)

    setup_stage()
    modulate1("ada_mix0", 0)
    dump("hT", hT[:, :, LAT])
    sgu_pool_mixer()
    dump("x1", resid[:])
    modulate1("ada_ffn0", 0)
    ffn1_stages(0)
    dump("x2", resid[:])
    modulate1("ada_mix1", 1)
    conformer_mixer()
    dump("x3", resid[:])
    modulate1("ada_ffn1", 1)
    ffn1_stages(1)
    dump("x4", resid[:])
    second_block()


def blocks_of(w, plan):
    w = np.asarray(w)
    parts = [w[k * P:(k + nk) * P, c:c + nc].reshape(nk, P, nc).transpose(1, 0, 2).ravel() for k, nk, c, nc in plan]
    return np.ascontiguousarray(np.concatenate(parts))


def columns(v, *shape):
    v = np.asarray(v)
    return np.ascontiguousarray(v.reshape(-1, P).T)


def interleaved(w, half):
    a, b = w[..., :half], w[..., half:]
    n = half // P
    stacked = np.stack([a.reshape(*a.shape[:-1], n, P), b.reshape(*b.shape[:-1], n, P)], axis=-2)
    return stacked.reshape(*w.shape)


def shape_constants():
    same_head = np.kron(np.eye(P // HD), np.ones((HD, HD))).astype(np.float32)
    t = np.arange(SEQ)
    counts = [np.minimum(t + w // 2, SEQ) - np.maximum(t - w // 2, 0) for w in (2, 4, 8, 16)]
    return {
        "identity": np.eye(P, dtype=np.float32),
        "head_ones": same_head,
        "inv_count": (1.0 / np.stack(counts)).astype(np.float32),
    }


def lay_out_first(i):
    plans = dict(WEIGHTS)
    i = {k: np.asarray(v) for k, v in i.items()}
    out = dict(shape_constants())
    out["x"] = i["x"][0]
    out["ctx"] = i["ctx_2"][0]
    out["c1"] = columns(i["c"][0])
    out["c2"] = np.ascontiguousarray(np.stack([columns(i["c_2"][0]), columns(i["c_ctx_2"])], axis=-1))
    out["ada_b_mix"] = np.stack([columns(b) for b in i["mix_ada_b"]])
    out["ada_b_ffn"] = np.stack([columns(b) for b in i["ffn_ada_b"]])
    w_in = i["ab_w_in"][0]
    out["ab_uv"] = blocks_of(w_in[:, :1024], plans["ab_uv"])
    out["ab_z"] = blocks_of(w_in[:, 1024:], plans["ab_z"])
    out["ab_out"] = blocks_of(i["ab_w_out"][0], plans["ab_out"])
    out["sgu_g"], out["sgu_b"] = i["ab_sgu_ln_g"][0], i["ab_sgu_ln_b"][0]
    out["wsT"] = np.ascontiguousarray(i["ab_ws"][0].transpose(2, 0, 1))
    out["bs"] = np.ascontiguousarray(i["ab_bs"][0].T)
    out["pool_w"] = np.ascontiguousarray(i["ab_pool_w"][0].transpose(1, 0, 2))
    out["pool_scale"] = columns(i["ab_pool_scale"][0])
    out["cv_in"] = blocks_of(interleaved(i["cv_w_in"][0], D), plans["cv_in"])
    out["cv_out"] = blocks_of(i["cv_w_out"][0], plans["cv_out"])
    taps = np.concatenate([i["cv_dw"][0], i["cv_dw_b"][0][None]])
    out["cv_taps"] = np.ascontiguousarray(taps.reshape(CONV_W + 1, DK, P).transpose(2, 1, 0))
    out["cv_ln"] = np.ascontiguousarray(np.stack([columns(i["cv_ln_g"][0]), columns(i["cv_ln_b"][0])], axis=1))
    ffn_taps = []
    for l in range(DEPTH):
        out[f"ada_mix{l}"] = blocks_of(i["mix_ada_w"][l], ADA1)
        out[f"ada_ffn{l}"] = blocks_of(i["ffn_ada_w"][l], ADA1)
        out[f"up{l}"] = blocks_of(interleaved(i["ffn_w_up"][l], FFN), plans[f"up{l}"])
        out[f"down{l}"] = blocks_of(i["ffn_w_down"][l], plans[f"down{l}"])
        for kind in ("mix", "ffn"):
            out[f"{kind}_ln_g{l}"], out[f"{kind}_ln_b{l}"] = i[f"{kind}_ln_g"][l], i[f"{kind}_ln_b"][l]
        taps = np.concatenate([i["ffn_dw"][l], i["ffn_dw_b"][l][None]])
        ffn_taps.append(interleaved(taps, FFN).reshape(4, 2 * FK, P).transpose(2, 1, 0))
    out["ffn_taps"] = np.ascontiguousarray(np.stack(ffn_taps))
    return out


def second_constants():
    out = {}
    t = np.arange(SEQ)
    n_freq = HD // 4
    inv_freq = 10000.0 ** (-np.arange(n_freq, dtype=np.float32) / n_freq)
    row = (t // GRID_W).astype(np.float32)[:, None] * inv_freq.astype(np.float32)
    col = (t % GRID_W).astype(np.float32)[:, None] * inv_freq.astype(np.float32)
    ang = np.concatenate([row, row, col, col], axis=-1).astype(np.float64).T
    out["rope_cos"] = np.tile(np.cos(ang), (2, 1)).astype(np.float32)
    out["rope_sin"] = np.tile(np.sin(ang), (2, 1)).astype(np.float32)
    turn = np.zeros((P, P), np.float32)
    for base in range(0, P, 2 * n_freq):
        for i in range(n_freq):
            turn[base + n_freq + i, base + i] = -1.0
            turn[base + i, base + n_freq + i] = 1.0
    out["rope_turn"] = turn
    q, k = np.arange(P)[:, None], np.arange(3 * P)[None, :]
    out["window_mask"] = np.where(np.abs(k - P - q) <= P, 0.0, NEG_INF).astype(np.float32)
    reset = np.ones((NCH, CW), np.float32)
    reset[:, 0] = 0
    out["reset"] = reset.ravel()
    i = np.arange(CH)
    earlier = (i[None, :] < i[:, None])
    both = np.stack([earlier, earlier.T])
    blocks = np.stack([np.kron(np.eye(2), m) for m in both])
    out["mask_before"] = np.ascontiguousarray(blocks.transpose(1, 0, 2)).astype(np.float32)
    out["mask_before_T"] = np.ascontiguousarray(blocks.transpose(2, 0, 1)).astype(np.float32)
    upto = both | np.eye(CH, dtype=bool)
    out["mask_upto_T"] = np.ascontiguousarray(np.tile(upto.transpose(2, 0, 1), (2, 1, 1))).astype(np.float32)
    levels = []
    for l in range(LEVELS):
        m = 1 << l
        pair = (i[:, None] // (2 * m) == i[None, :] // (2 * m))
        fwd = pair & (i[:, None] // m < i[None, :] // m)
        levels.append(np.stack([np.kron(np.eye(2), fwd), np.kron(np.eye(2), fwd.T)]))
    out["level_masks"] = np.ascontiguousarray(np.stack(levels).transpose(2, 0, 1, 3).reshape(P, -1)).astype(np.float32)
    return out


def rpb_layout(rpb):
    t = np.arange(SEQ)
    r, c = t // GRID_W, t % GRID_W
    start = np.clip(c - 8, 0, GRID_W - 16)
    ok = (c[None, :] >= start[:, None]) & (c[None, :] < start[:, None] + 16)
    dr = r[None, :] - r[:, None] + 7
    dc = np.clip(c[None, :] - c[:, None] + 15, 0, 30)
    out = rpb[:, dr, dc]
    out[:, ~ok] = NEG_INF
    return np.ascontiguousarray(out)


def lay_out(i):
    plans = dict(WEIGHTS)
    out = lay_out_first(i)
    i = {k: np.asarray(v) for k, v in i.items()}
    out.update(second_constants())
    out["b_ada"] = np.stack([columns(b) for b in i["b_ada_2"]])
    out["gains"] = np.ascontiguousarray(np.stack([np.stack([columns(i[n][l]) for n in (
        "g_pre_mix_2", "g_post_mix_2", "g_pre_ff_2", "g_post_ff_2")], axis=1) for l in range(DEPTH)]))
    for l in range(DEPTH):
        out[f"ada{l}"] = blocks_of(i["w_ada_2"][l], ADA2)
        out[f"out{l}"] = blocks_of(i["w_out_2"][l], plans[f"out{l}"])
        out[f"ff1_{l}"] = blocks_of(i["w_ff1_2"][l], plans[f"ff1_{l}"])
        out[f"ff2_{l}"] = blocks_of(i["w_ff2_2"][l], plans[f"ff2_{l}"])
    even, odd = i["w_in_even_2"][0], i["w_in_odd_2"][0]

    def grouped(w):
        k0, k1 = w[:, 512:512 + HD], w[:, 512 + HD:512 + 2 * HD]
        return np.concatenate([w[:, :512], k0, k0, k1, k1], axis=1), w[:, 640:768]

    qk, v = grouped(even[:, 1920:])
    out["b_qk"], out["b_v"] = blocks_of(qk, plans["b_qk"]), blocks_of(v, plans["b_v"])
    qk, v = grouped(odd[:, 1536:])
    out["d_qk"], out["d_v"] = blocks_of(qk, plans["d_qk"]), blocks_of(v, plans["d_v"])
    out["c_qk"], out["c_v"] = blocks_of(odd[:, :1024], plans["c_qk"]), blocks_of(odd[:, 1024:1536], plans["c_v"])
    out["lora"] = blocks_of(even[:, 1536:1920], plans["lora"])
    for h in range(2):
        cols = [even[:, x * 512 + h * 256:x * 512 + (h + 1) * 256] for x in range(3)]
        out[f"rkv{h}"] = blocks_of(np.concatenate(cols, axis=1), plans[f"rkv{h}"])
    mu = np.stack([columns(i["a_mu_prev_2"][0]), columns(i["a_mu_next_2"][0])], axis=-1).reshape(P, 30)
    two = lambda x: np.concatenate([columns(x[0]), columns(x[1])], axis=1)
    out["r_cols"] = np.ascontiguousarray(np.concatenate([
        mu, two(i["a_w0_2"][0]), two(i["a_a0_2"][0]), columns(i["a_k_k_2"][0]), columns(i["a_k_a_2"][0]),
        columns(i["a_r_k_2"][0].reshape(-1)), columns(i["a_gn_w_2"][0]), columns(i["a_gn_b_2"][0])], axis=1))
    for name, src in (("w2", i["a_w2_2"][0]), ("a2", i["a_a2_2"][0])):
        full = np.zeros((2, P, 2, 2 * P), np.float32)
        for d in range(2):
            for h in range(2):
                full[h, d * HD:(d + 1) * HD, d] = src[d][:, h * 256:(h + 1) * 256]
        out[name] = full
    out["g2"] = np.ascontiguousarray(i["a_g2_2"][0].reshape(P, 2, 2 * P).transpose(1, 0, 2))
    out["b_sink"] = i["b_sink_2"][0]
    out["rpb_table"] = rpb_layout(i["c_rpb_2"][0])
    out["d_gain"] = np.ascontiguousarray(np.stack([np.tile(i["d_q_gain_2"][0], 2), np.tile(i["d_k_gain_2"][0], 2)], axis=1))
    return out


def kernel(**inputs):
    import concourse.bacc as bacc
    from concourse.bass_utils import run_bass_kernel_spmd

    arrays = lay_out(inputs)
    nc = bacc.Bacc("TRN2", target_bir_lowering=False, num_devices=1)
    dram = {name: nc.dram_tensor(name, a.shape, mybir.dt.from_np(a.dtype), kind="ExternalInput").ap() for name, a in arrays.items()}
    out = nc.dram_tensor("out", (1, SEQ, D), F32, kind="ExternalOutput").ap()
    build(nc, dram, out)
    got = run_bass_kernel_spmd(nc, [arrays], core_ids=[0])
    return got.results[0]["out"]
```

```python
from contextlib import contextmanager

import numpy as np

import concourse.bass as bass
from concourse import mybir

ALU = mybir.AluOpType
ACT = mybir.ActivationFunctionType
AX_X = mybir.AxisListType.X
F32 = mybir.dt.float32
F32R = mybir.dt.float32r
U8 = mybir.dt.uint8

P = 128
D = 1024
DK = D // P
SEQ, CTX = 512, 256
TOK = CTX + SEQ
LAT = slice(CTX, TOK)
CTX_T, LAT_T = CTX // P, SEQ // P
TOK_T = CTX_T + LAT_T
BANK = 512
NBANK = 8

DEPTH = 2
ALPHA = (2 * DEPTH) ** 0.25
LN_EPS = 1e-5
RMS_EPS = 1e-6
GN_EPS = 64e-5
A_HEADS = 4
FFN = ((8 * D // 3 + 127) // 128) * 128
FK = FFN // P
CONV_W = 31
DFF = 4 * D
HD = 64
GRID_W = 64
NEG_INF = -1e30
ATTN_SCALE = HD ** -0.5

CH = 64
NCH = TOK // CH
CTX_CH = CTX // CH
CW = CH + 1
DECAY = float(np.exp(-0.5))
LEVELS = 6

RING = 4
BLK = 2048
PIECE = 1024
PIECES = 2
SIDE_BANK = 7
NROT = 7


def feature_plan(n_cols, k_tiles=DK, width=256):
    return [(0, k_tiles, c, min(width, n_cols - c)) for c in range(0, n_cols, width)]


def token_plan(n_cols, k_tiles):
    return [(k, min(4, k_tiles - k), c, 512) for c in range(0, n_cols, 512) for k in range(0, k_tiles, 4)]


ADA1 = feature_plan(3 * D)
ADA2 = feature_plan(6 * D)
FIRST_ADA = "ada_mix0"
MAIN = [
    ("ab_uv", token_plan(1024, DK)), ("ab_z", feature_plan(512)), ("ab_out", token_plan(D, DK)),
    ("up0", feature_plan(2 * FFN)), ("down0", token_plan(D, FK)),
    ("cv_in", feature_plan(2 * D)), ("cv_out", token_plan(D, DK)),
    ("up1", feature_plan(2 * FFN)), ("down1", token_plan(D, FK)),
    ("b_qk", feature_plan(768)), ("b_v", feature_plan(P, width=P)),
    ("lora", feature_plan(256) + [(0, DK, 256, P)]),
    ("rkv0", feature_plan(768)), ("rkv1", feature_plan(768)),
    ("out0", token_plan(D, DK)), ("ff1_0", feature_plan(DFF)), ("ff2_0", token_plan(D, DFF // P)),
    ("c_qk", feature_plan(1024)), ("c_v", token_plan(512, DK)),
    ("d_qk", feature_plan(768)), ("d_v", feature_plan(P, width=P)),
    ("out1", token_plan(D, DK)), ("ff1_1", feature_plan(DFF)), ("ff2_1", token_plan(D, DFF // P)),
]
ADAS = {"ada_mix0": ADA1, "ada_ffn0": ADA1, "ada_mix1": ADA1, "ada_ffn1": ADA1, "ada0": ADA2, "ada1": ADA2}
WEIGHTS = MAIN + list(ADAS.items())
SIDES = {
    "ab_uv": ("ada_ffn0", 0, 5), "ab_z": ("ada_ffn0", 5, 2), "ab_out": ("ada_ffn0", 7, 5),
    "up0": ("ada_mix1", 0, 12),
    "cv_in": ("ada_ffn1", 0, 8), "cv_out": ("ada_ffn1", 8, 4),
    "up1": ("ada0", 0, 24),
    "ff1_0": ("ada1", 0, 16), "ff2_0": ("ada1", 16, 8),
}


def sides_after(host, b):
    if host not in SIDES:
        return []
    m, (_, first, count) = len(dict(MAIN)[host]), SIDES[host]
    return list(range(first + b * count // m, first + (b + 1) * count // m))


class WeightStream:

    def __init__(self, nc, drams):
        self.nc = nc
        self.ring = nc.alloc_sbuf_tensor("weight_ring", [P, RING, BLK], F32)
        self.hi_buf = nc.alloc_sbuf_tensor("weight_hi", [P, PIECES, PIECE], F32R)
        self.lo_buf = nc.alloc_sbuf_tensor("weight_lo", [P, PIECES, PIECE], F32R)
        self.landed = [nc.alloc_semaphore(f"weight_landed{i}") for i in range(RING)]
        self.hi_made = nc.alloc_semaphore("weight_hi_made")
        self.lo_made = nc.alloc_semaphore("weight_lo_made")
        self.piece_used = nc.alloc_semaphore("weight_piece_used")
        self.side_used = nc.alloc_semaphore("side_block_used")
        self.blocks, self.pieces, self.end_of = [], [], {}
        self.free_when = []
        sides = 0
        offsets = {}
        for name, plan in MAIN:
            at = 0
            for b, (_, nk, _, width) in enumerate(plan):
                n = nk * width
                i = len(self.blocks)
                self.blocks.append((drams[name][at:at + P * n].rearrange("(p n) -> p n", p=P), n, width))
                at += P * n
                if width <= 256:
                    for c in range(0, width, P):
                        self.pieces.append((i, "columns", c))
                else:
                    for k in range(0, nk, 2):
                        self.pieces.append((i, "rows", k))
                self.free_when.append((self.lo_made, len(self.pieces)))
                for side in sides_after(name, b):
                    source = drams[SIDES[name][0]]
                    n = DK * 256
                    self.blocks.append((source[side * P * n:(side + 1) * P * n].rearrange("(p n) -> p n", p=P), n, 256))
                    sides += 1
                    self.free_when.append((self.side_used, sides))
            self.end_of[name] = len(self.blocks)
        self.loads = 0
        self.at = {"act": 0, "dve": 0, "pe": 0}
        self.side_blocks = [i for i, w in enumerate(self.free_when) if w[0] is self.side_used]
        self.sides = 0
        self.owed = False

    def load(self, sp, name=None):
        until = min(self.end_of.get(name, 0) + RING, len(self.blocks))
        while self.loads < until:
            i = self.loads
            if i >= RING:
                sp.wait_ge(*self.free_when[i - RING])
            source, n, _ = self.blocks[i]
            sp.dma_start(self.ring[:, i % RING, 0:n], source).then_inc(self.landed[i % RING], 16)
            self.loads += 1

    def arrived(self, engine, i):
        engine.wait_ge(self.landed[i % RING], 16 * (i // RING + 1))

    def raw_piece(self, p):
        i, kind, at = self.pieces[p]
        _, n, width = self.blocks[i]
        block = self.ring[:, i % RING, 0:n].rearrange("p (k n) -> p k n", n=width)
        raw = block[:, :, at:at + P] if kind == "columns" else block[:, at:at + 2, :]
        width = P if kind == "columns" else width
        split = [x[:, p % PIECES, 0:raw.shape[1] * width].rearrange("p (k n) -> p k n", n=width) for x in (self.hi_buf, self.lo_buf)]
        return i, raw, split

    def hi(self, act, x=None):
        p = self.at["act"]
        self.at["act"] += 1
        i, raw, (hi, _) = self.raw_piece(p)
        self.arrived(act, i)
        if p >= PIECES:
            act.wait_ge(self.piece_used, p - PIECES + 1)
        if x is not None:
            self.nc.scalar.copy(x[1], x[0])
        self.nc.scalar.copy(hi, raw).then_inc(self.hi_made, 1)

    def lo(self, dve, x=None):
        p = self.at["dve"]
        self.at["dve"] += 1
        i, raw, (hi, lo) = self.raw_piece(p)
        self.arrived(dve, i)
        dve.wait_ge(self.hi_made, p + 1)
        if x is not None:
            self.nc.vector.tensor_tensor(x[2], x[0], x[1].bitcast(F32), ALU.subtract)
        self.nc.vector.tensor_tensor(lo, raw, hi.bitcast(F32), ALU.subtract).then_inc(self.lo_made, 1)

    def take(self, pe):
        p = self.at["pe"]
        self.at["pe"] += 1
        pe.wait_ge(self.lo_made, p + 1)
        return self.raw_piece(p)[2]

    def used_by(self, product):
        if self.owed:
            product.then_inc(self.piece_used, 1)
            self.owed = False

    def settle(self, pe):
        if self.owed:
            pe.drain().then_inc(self.piece_used, 1)
            self.owed = False

    def take_side(self, pe):
        i = self.side_blocks[self.sides]
        self.sides += 1
        self.arrived(pe, i)
        return self.ring[:, i % RING, :].rearrange("p (k n) -> p k n", n=256)


class Chain:

    def __init__(self, engine, sem):
        self.engine, self.sem, self.n = engine, sem, 0

    def __call__(self, ins):
        ins.then_inc(self.sem, 1)
        self.n += 1
        self.engine.wait_ge(self.sem, self.n)


def build(nc, dram, out_dram, debug=None):
    ps = [nc.alloc_psum_tensor(f"bank{i}", [P, BANK], F32) for i in range(NBANK)]
    weights = WeightStream(nc, dram)
    stored = nc.alloc_semaphore("output_stored")

    names = {}

    def unique(name):
        names[name] = names.get(name, 0) + 1
        return f"{name}.{names[name]}"

    def sb(name, shape, dt=F32):
        return nc.alloc_sbuf_tensor(unique(name), shape, dt)

    def sem(name):
        return nc.alloc_semaphore(unique(name))

    @contextmanager
    def stage():
        with nc.cleanup_on_exit():
            yield

    def rows(name):
        return dram[name].partition_broadcast(P)

    def dump(name, ap):
        if debug is None or name not in debug:
            return
        with stage():
            done = sem("dumped")
            with nc.Block() as block:
                @block.sync
                def _(sp):
                    sp.dma_start(debug[name], ap).then_inc(done, 16)
                    sp.wait_ge(done, 16)

    ident = sb("identity", [P, P])
    ones = sb("ones", [P, P])
    head_ones = sb("head_ones", [P, P])
    silu_c1 = sb("silu_c1", [P, DK, 1])
    silu_c2 = sb("silu_c2", [P, DK, 2])
    mods = {name: sb(f"modulation_{name}", [P, len(plan) * 2, 1 if plan is ADA1 else 2]) for name, plan in ADAS.items()}
    ada_bias = {name: sb(f"bias_{name}", [P, len(plan) * 2]) for name, plan in ADAS.items()}
    gains = sb("gains", [P, 4, DK])
    resid = sb("residual", [P, TOK_T, D])
    gate_rows = sb("gate_rows", [P, 2, D])

    def three_products(out, w_hi, w_lo, x_hi, x_lo, first, last):
        nc.tensor.matmul(out, w_hi, x_hi, start=first, stop=False)
        nc.tensor.matmul(out, w_hi, x_lo, start=False, stop=False)
        return nc.tensor.matmul(out, w_lo, x_hi, start=False, stop=last)

    def side_products(pe, host, b):
        for side in sides_after(host, b):
            vec = silu_c1 if mods[SIDES[host][0]].shape[2] == 1 else silu_c2
            nv = vec.shape[2]
            w = weights.take_side(pe)
            for j in range(2):
                col = (2 * side + j) * nv
                for k in range(DK):
                    last = nc.tensor.matmul(ps[SIDE_BANK][:, col:col + nv], w[:, k, j * P:(j + 1) * P], vec[:, k, :],
                                            start=(k == 0), stop=(k == DK - 1))
                    weights.used_by(last)
            last.then_inc(weights.side_used, 1)

    def side_sums(dve, host):
        if host not in SIDES:
            return
        name, first, count = SIDES[host]
        mod = mods[name]
        nv = mod.shape[2]
        dve.wait_ge(weights.side_used, sides_until[host])
        got = ps[SIDE_BANK][:, 2 * first * nv:2 * (first + count) * nv].rearrange("p (c v) -> p c v", v=nv)
        for v in range(nv):
            nc.vector.tensor_tensor(mod[:, 2 * first:2 * (first + count), v], got[:, :, v],
                                    ada_bias[name][:, 2 * first:2 * (first + count)], ALU.add)

    sides_until, total = {}, 0
    for host, _ in MAIN:
        if host in SIDES:
            total += SIDES[host][2]
            sides_until[host] = total

    def feature_products(pe, host, hT, segments, evacuated, g0=0):
        g = g0
        piece = 0
        for b, (_, _, _, width) in enumerate(dict(MAIN)[host]):
            for _ in range(width // P):
                hi, lo = weights.take(pe)
                for seg in segments(piece) if callable(segments) else segments:
                    if g >= NROT:
                        pe.wait_ge(evacuated, g - NROT + 1)
                    for k in range(DK):
                        last = three_products(ps[g % NROT][:, 0:seg.stop - seg.start], hi[:, k, :], lo[:, k, :],
                                              hT[0][:, k, seg], hT[1][:, k, seg], k == 0, k == DK - 1)
                    g += 1
                last.then_inc(weights.piece_used, 1)
                piece += 1
            side_products(pe, host, b)
        return g

    def token_products(pe, host, tiles, x, mm_done, evacuated, g0=0):
        plan = dict(MAIN)[host]
        k_tiles = max(k + nk for k, nk, _, _ in plan)
        T = len(tiles)
        p = 0
        for b, (k0, nk, c0, _) in enumerate(plan):
            n = c0 // BANK
            for at in range(0, nk, 2):
                hi, lo = weights.take(pe)
                done = k0 + at + 2 == k_tiles
                for i in range(T):
                    g = g0 + n * T + i
                    if k0 + at == 0 and g >= NROT:
                        pe.wait_ge(evacuated, g - NROT + 1)
                    for kk in range(2):
                        k = k0 + at + kk
                        xh, xl = x(p, kk, i)
                        out = ps[g % NROT][:, :]
                        one = nc.tensor.matmul(out, xh, hi[:, kk, :], start=(k == 0), stop=False)
                        weights.used_by(one)
                        nc.tensor.matmul(out, xl, hi[:, kk, :], start=False, stop=False)
                        last = nc.tensor.matmul(out, xh, lo[:, kk, :], start=False, stop=(k == k_tiles - 1))
                    if done:
                        last.then_inc(mm_done, 1)
                if done:
                    weights.owed = True
                else:
                    last.then_inc(weights.piece_used, 1)
                p += 1
            side_products(pe, host, b)
        weights.settle(pe)
        return g0 + (n + 1) * T

    class LeftOperand:

        def __init__(self, host, source, n_tok):
            self.source = source
            self.plan = [(k0 + at) for k0, nk, _, _ in dict(MAIN)[host] for at in range(0, nk, 2)]
            self.hi = sb("left_hi", [P, PIECES, 2, n_tok], F32R)
            self.lo = sb("left_lo", [P, PIECES, 2, n_tok], F32R)
            self.first = weights.at["pe"]

        def share(self, p):
            k = self.plan[p]
            slot = (self.first + p) % PIECES
            return self.source(k), self.hi[:, slot], self.lo[:, slot]

        def __call__(self, p, kk, i):
            slot = (self.first + p) % PIECES
            cols = slice(i * P, (i + 1) * P)
            return self.hi[:, slot, kk, cols], self.lo[:, slot, kk, cols]

    def setup_stage():
        with stage():
            plan = ADAS[FIRST_ADA]
            blocks = sb("first_blocks", [P, len(plan), BLK])
            loaded, made, silu_done = sem("loaded"), sem("memset"), sem("silu_done")
            block_landed = [sem(f"block_landed{i}") for i in range(len(plan))]
            mm_done, x_loaded = sem("mm_done"), sem("x_loaded")
            small = [(silu_c1[:, :, 0], dram["c1"]), (silu_c2[:], dram["c2"]), (ident[:], dram["identity"]), (head_ones[:], dram["head_ones"])]
            small += [(ada_bias[name][:], dram["bias_" + name]) for name in ADAS]
            with nc.Block() as block:
                @block.sync
                def _(sp):
                    for dst, src in small:
                        sp.dma_start(dst, src).then_inc(loaded, 16)
                    n = DK * 256
                    for i in range(len(plan)):
                        sp.dma_start(blocks[:, i, :], dram[FIRST_ADA][i * P * n:(i + 1) * P * n].rearrange("(p n) -> p n", p=P)).then_inc(block_landed[i], 16)
                    sp.dma_start(resid[:, CTX_T:TOK_T, :], dram["x"].rearrange("(t p) d -> p t d", p=P)).then_inc(x_loaded, 16)
                    sp.dma_start(resid[:, 0:CTX_T, :], dram["ctx"].rearrange("(t p) d -> p t d", p=P)).then_inc(x_loaded, 16)
                    weights.load(sp)
                    sp.wait_ge(loaded, len(small) * 16)
                    sp.wait_ge(x_loaded, 32)

                @block.scalar
                def _(act):
                    act.wait_ge(loaded, len(small) * 16)
                    nc.scalar.activation(silu_c1[:, :, 0], silu_c1[:, :, 0], ACT.Silu).then_inc(silu_done, 1)
                    nc.scalar.activation(silu_c2[:], silu_c2[:], ACT.Silu).then_inc(silu_done, 1)

                @block.tensor
                def _(pe):
                    pe.wait_ge(silu_done, 2)
                    for i in range(len(plan)):
                        pe.wait_ge(block_landed[i], 16)
                        w = blocks[:, i, :].rearrange("p (k n) -> p k n", n=256)
                        for j in range(2):
                            for k in range(DK):
                                last = nc.tensor.matmul(ps[SIDE_BANK][:, 2 * i + j:2 * i + j + 1], w[:, k, j * P:(j + 1) * P],
                                                        silu_c1[:, k, :], start=(k == 0), stop=(k == DK - 1))
                    last.then_inc(mm_done, 1)

                @block.vector
                def _(dve):
                    nc.vector.memset(ones[:], 1.0)
                    dve.wait_ge(loaded, len(small) * 16)
                    dve.wait_ge(mm_done, 1)
                    n = 2 * len(plan)
                    nc.vector.tensor_tensor(mods[FIRST_ADA][:, :, 0], ps[SIDE_BANK][:, 0:n], ada_bias[FIRST_ADA][:], ALU.add)

    def gate_row_stage(sources, beside=None):
        with stage():
            rep = sb("gate_column_repeated", [P, 2, P])
            filled, mm_done, evac = sem("repeated"), sem("mm_done"), sem("row_copied")
            jobs = [(r, f, col) for r, cols in sources for f, col in enumerate(cols)]
            with nc.Block() as block:
                if beside is not None:
                    block.sync(beside)

                @block.vector
                def _(dve):
                    for i, (r, f, col) in enumerate(jobs):
                        if i >= 2:
                            dve.wait_ge(mm_done, i - 1)
                        nc.vector.tensor_scalar(rep[:, i % 2, :], ones[:], col, None, ALU.mult).then_inc(filled, 1)

                @block.tensor
                def _(pe):
                    for i, (r, f, col) in enumerate(jobs):
                        pe.wait_ge(filled, i + 1)
                        if i >= NBANK:
                            pe.wait_ge(evac, i - NBANK + 1)
                        nc.tensor.matmul(ps[i % NBANK][:, 0:P], rep[:, i % 2, :], ident[:],
                                         start=True, stop=True).then_inc(mm_done, 1)

                @block.scalar
                def _(act):
                    for i, (r, f, col) in enumerate(jobs):
                        act.wait_ge(mm_done, i + 1)
                        nc.scalar.copy(gate_rows[:, r, f * P:(f + 1) * P], ps[i % NBANK][:, 0:P]).then_inc(evac, 1)

    def to_features_stage(src, tiles, scale, shift, hT, t_base=0, rms=None, beside=None):
        segs = [(0, [t for t in tiles if t >= CTX_T]), (1, [t for t in tiles if t < CTX_T])]
        segs = [(v, ts) for v, ts in segs if ts]
        groups = [(f, v, ts) for f in range(DK) for v, ts in segs]
        with stage():
            mm_done, evac, chained = sem("mm_done"), sem("evacuated"), sem("vector_step")
            squared, normed, hi_made, lo_made = sem("squared"), sem("normed"), sem("hi_made"), sem("lo_made")
            act_chained = sem("scalar_step")
            if rms:
                scratch, hn, exact = rms
                stats = sb("sum_of_squares", [P, TOK_T])
                root = sb("root", [P, TOK_T])
            else:
                exact = sb("exact", [P, 4, BANK])
            x = hn if rms else src

            def place(g):
                f, v, ts = groups[g]
                cols = slice((ts[0] - t_base) * P, (ts[-1] + 1 - t_base) * P)
                return exact[:, g % 4, 0:len(ts) * P], hT[0][:, f, cols], hT[1][:, f, cols]

            with nc.Block() as block:
                if beside is not None:
                    block.sync(beside)

                @block.scalar
                def _(act):
                    if rms:
                        step = Chain(act, act_chained)
                        for t in tiles:
                            step(nc.scalar.activation(scratch[:], src[:, t, :], ACT.Square, accum_out=stats[:, t:t + 1]))
                        act.sem_inc(squared, 1)
                        act.wait_ge(squared, 2)
                        nc.scalar.activation(root[:, tiles[0]:tiles[-1] + 1], stats[:, tiles[0]:tiles[-1] + 1], ACT.Sqrt).then_inc(squared, 1)
                    for g in range(len(groups)):
                        x32, hi, _ = place(g)
                        act.wait_ge(evac, g + 1)
                        nc.scalar.copy(hi, x32).then_inc(hi_made, 1)

                @block.vector
                def _(dve):
                    step = Chain(dve, chained)
                    if rms:
                        t0, t1 = tiles[0], tiles[-1] + 1
                        dve.wait_ge(squared, 1)
                        nc.vector.tensor_scalar(stats[:, t0:t1], stats[:, t0:t1], 1.0 / D, RMS_EPS, ALU.mult, ALU.add).then_inc(squared, 1)
                        dve.wait_ge(squared, 3)
                        step(nc.vector.reciprocal(root[:, t0:t1], root[:, t0:t1]))
                        for t in tiles:
                            nc.vector.tensor_scalar(hn[:, t, :], src[:, t, :], root[:, t:t + 1], None, ALU.mult).then_inc(normed, 1)
                    for g in range(len(groups) + 2):
                        if g < len(groups):
                            f, v, ts = groups[g]
                            dve.wait_ge(mm_done, g + 1)
                            if g >= 4:
                                dve.wait_ge(lo_made, g - 3)
                            nc.vector.tensor_scalar(place(g)[0], ps[g % NBANK][:, 0:len(ts) * P],
                                                    scale(f, v), shift(f, v), ALU.mult, ALU.add).then_inc(evac, 1)
                        if g >= 2:
                            x32, hi, lo = place(g - 2)
                            dve.wait_ge(hi_made, g - 1)
                            nc.vector.tensor_tensor(lo, x32, hi.bitcast(F32), ALU.subtract).then_inc(lo_made, 1)

                @block.tensor
                def _(pe):
                    if rms:
                        pe.wait_ge(normed, len(tiles))
                    for g, (f, v, ts) in enumerate(groups):
                        if g >= NBANK:
                            pe.wait_ge(evac, g - NBANK + 1)
                        for i, t in enumerate(ts):
                            last = nc.tensor.transpose(ps[g % NBANK][:, i * P:(i + 1) * P], x[:, t, f * P:(f + 1) * P], ident[:])
                        last.then_inc(mm_done, 1)

    def out_product_ln_stage(name, source, g_row, b_row):
        tiles = list(range(CTX_T, TOK_T))
        T = len(tiles)
        n_pieces = sum(nk // 2 for _, nk, _, _ in dict(MAIN)[name])
        with stage():
            left = LeftOperand(name, source, SEQ)
            lng, lnb = sb("ln_gain", [P, D]), sb("ln_bias", [P, D])
            gated = sb("gated", [P, 2, BANK])
            stats = sb("bn_stats", [P, T, 2, 6])
            mv = sb("mean_var", [P, T, 2])
            inv = sb("inv_std", [P, T])
            nmean = sb("minus_mean_over_std", [P, T])
            loaded, mm_done, evac = sem("loaded"), sem("mm_done"), sem("evacuated")
            chained, var_ready, root_ready = sem("vector_step"), sem("var_ready"), sem("root_ready")
            inv_ready, centred = sem("inv_ready"), sem("centred")
            scaled, biased = sem("scaled"), sem("biased")
            with nc.Block() as block:
                @block.sync
                def _(sp):
                    sp.dma_start(lng[:], rows(g_row)).then_inc(loaded, 16)
                    sp.dma_start(lnb[:], rows(b_row)).then_inc(loaded, 16)
                    weights.load(sp, name)

                @block.tensor
                def _(pe):
                    token_products(pe, name, tiles, left, mm_done, evac)

                @block.vector
                def _(dve):
                    step = Chain(dve, chained)
                    for p in range(n_pieces // 2 + 1):
                        weights.lo(dve, left.share(p))
                    p += 1
                    for n in range(2):
                        cols = slice(n * BANK, (n + 1) * BANK)
                        for i, t in enumerate(tiles):
                            if n == 0 and p < n_pieces:
                                weights.lo(dve, left.share(p))
                                p += 1
                            if n == 1 and i == 0:
                                while p < n_pieces:
                                    weights.lo(dve, left.share(p))
                                    p += 1
                            g = n * T + i
                            dve.wait_ge(mm_done, g + 1)
                            ins = nc.vector.tensor_tensor(gated[:, g % 2, :], ps[g % NROT][:], gate_rows[:, 0, cols], ALU.mult)
                            ins.then_inc(evac, 1)
                            dve.wait_ge(evac, g + 1)
                            step(nc.vector.scalar_tensor_tensor(out=resid[:, t, cols], in0=resid[:, t, cols], scalar=ALPHA,
                                                                in1=gated[:, g % 2, :], op0=ALU.mult, op1=ALU.add))
                            step(nc.vector.bn_stats(stats[:, i, n, :], resid[:, t, cols]))
                            if n == 1:
                                step(nc.vector.bn_aggr(mv[:, i, :], stats[:, i, :, :].rearrange("p a b -> p (a b)")))
                                nc.vector.tensor_scalar(inv[:, i:i + 1], mv[:, i, 1:2], LN_EPS, None, ALU.add).then_inc(var_ready, 1)
                    for i, t in enumerate(tiles):
                        dve.wait_ge(root_ready, i + 1)
                        step(nc.vector.reciprocal(inv[:, i:i + 1], inv[:, i:i + 1]))
                        nc.vector.scalar_tensor_tensor(out=nmean[:, i:i + 1], in0=mv[:, i, 0:1], scalar=-1.0,
                                                       in1=inv[:, i:i + 1], op0=ALU.mult, op1=ALU.mult).then_inc(inv_ready, 1)
                    dve.wait_ge(loaded, 32)
                    for i, t in enumerate(tiles):
                        dve.wait_ge(centred, i + 1)
                        nc.vector.tensor_tensor(resid[:, t, :], resid[:, t, :], lng[:], ALU.mult).then_inc(scaled, 1)
                    side_sums(dve, name)

                @block.scalar
                def _(act):
                    for p in range(n_pieces):
                        weights.hi(act, left.share(p))
                    for i in range(T):
                        act.wait_ge(var_ready, i + 1)
                        nc.scalar.activation(inv[:, i:i + 1], inv[:, i:i + 1], ACT.Sqrt).then_inc(root_ready, 1)
                    for i, t in enumerate(tiles):
                        act.wait_ge(inv_ready, i + 1)
                        nc.scalar.activation(resid[:, t, :], resid[:, t, :], ACT.Identity, bias=nmean[:, i:i + 1],
                                             scale=inv[:, i:i + 1]).then_inc(centred, 1)

                @block.gpsimd
                def _(pool):
                    pool.wait_ge(loaded, 32)
                    for i, t in enumerate(tiles):
                        pool.wait_ge(scaled, i + 1)
                        nc.gpsimd.tensor_tensor(resid[:, t, :], resid[:, t, :], lnb[:], ALU.add).then_inc(biased, 1)

    def ffn1_stages(layer, make_hT):
        with stage():
            act_T = sb("ffn_hidden", [P, FK, SEQ])
            with stage():
                hT = make_hT()
                with stage():
                    up = f"up{layer}"
                    taps = sb("ffn_taps", [P, 2 * FK, 4])
                    conv = sb("ffn_conv", [P, 4, SEQ])
                    gel = sb("ffn_gelu", [P, 2, SEQ])
                    loaded, centre, chained = sem("loaded"), sem("centre_tap"), sem("vector_step")
                    conv_done, gelu_done, multiplied = sem("conv_done"), sem("gelu_done"), sem("multiplied")
                    first, G = weights.at["pe"], 2 * FK
                    with nc.Block() as block:
                        @block.sync
                        def _(sp):
                            sp.dma_start(taps[:], dram["ffn_taps"][layer]).then_inc(loaded, 16)
                            weights.load(sp, up)

                        @block.tensor
                        def _(pe):
                            feature_products(pe, up, hT, [slice(0, SEQ)], conv_done)

                        @block.scalar
                        def _(act):
                            act.wait_ge(loaded, 16)
                            weights.hi(act)
                            for g in range(G):
                                if g + 1 < G:
                                    weights.hi(act)
                                act.wait_ge(weights.piece_used, first + g + 1)
                                if g >= 4:
                                    act.wait_ge(multiplied, g // 2 - 1)
                                nc.scalar.activation(conv[:, g % 4, :], ps[g % NROT][:], ACT.Identity,
                                                     bias=taps[:, g, 3:4], scale=taps[:, g, 1:2]).then_inc(centre, 1)
                                if g % 2:
                                    act.wait_ge(conv_done, g)
                                    nc.scalar.activation(gel[:, g // 2 % 2, :], conv[:, (g - 1) % 4, :], ACT.Gelu_apprx_tanh).then_inc(gelu_done, 1)

                        @block.vector
                        def _(dve):
                            step = Chain(dve, chained)
                            weights.lo(dve)
                            for g in range(G):
                                if g + 1 < G:
                                    weights.lo(dve)
                                c, z = conv[:, g % 4, :], ps[g % NROT]
                                dve.wait_ge(centre, g + 1)
                                step(nc.vector.scalar_tensor_tensor(out=c[:, 1:], in0=z[:, 0:SEQ - 1], scalar=taps[:, g, 0:1],
                                                                    in1=c[:, 1:], op0=ALU.mult, op1=ALU.add))
                                nc.vector.scalar_tensor_tensor(out=c[:, 0:SEQ - 1], in0=z[:, 1:SEQ], scalar=taps[:, g, 2:3],
                                                               in1=c[:, 0:SEQ - 1], op0=ALU.mult, op1=ALU.add).then_inc(conv_done, 1)
                                if g % 2:
                                    dve.wait_ge(gelu_done, g // 2 + 1)
                                    dve.wait_ge(conv_done, g + 1)
                                    nc.vector.tensor_tensor(act_T[:, g // 2, :], gel[:, g // 2 % 2, :], c, ALU.mult).then_inc(multiplied, 1)
                            side_sums(dve, up)
            out_product_ln_stage(f"down{layer}", lambda k: act_T[:, k:k + 2, :], f"ffn_ln_g{layer}", f"ffn_ln_b{layer}")

    lat_tiles = list(range(CTX_T, TOK_T))

    def hT_pair(n_tok):
        return sb("hT_hi", [P, DK, n_tok], F32R), sb("hT_lo", [P, DK, n_tok], F32R)

    def modulate1(name):
        mod = mods[name]
        with stage():
            with nc.Block() as block:
                @block.vector
                def _(dve):
                    nc.vector.tensor_scalar(mod[:, DK:3 * DK, :], mod[:, DK:3 * DK, :], 1.0, None, ALU.add)
        gate_row_stage([(0, [mod[:, 2 * DK + f, :] for f in range(DK)])])

        def make_hT():
            hT = hT_pair(SEQ)
            to_features_stage(resid, lat_tiles, lambda f, v: mod[:, DK + f, :], lambda f, v: mod[:, f, :], hT, t_base=CTX_T)
            return hT
        return make_hT

    def sgu_pool_mixer(make_hT):
        with stage():
            u = sb("u", [P, LAT_T, 512])
            v = sb("v", [P, LAT_T, 512])
            PAD = 16
            ZW = SEQ + 2 * PAD
            z = sb("z_padded", [P, 4, ZW])
            mixT = sb("mixT", [P, DK, SEQ])
            with stage():
                hT = make_hT()
                lng, lnb = sb("sgu_gain", [P, 512]), sb("sgu_bias", [P, 512])
                stats = sb("bn_stats", [P, LAT_T, 6])
                mv = sb("mean_var", [P, LAT_T, 2])
                inv = sb("inv_std", [P, LAT_T])
                loaded, mm_done, evac = sem("loaded"), sem("mm_done"), sem("evacuated")
                chained, var_ready, root_ready, zeroed = sem("vector_step"), sem("var_ready"), sem("root_ready"), sem("zeroed")
                with nc.Block() as block:
                    @block.sync
                    def _(sp):
                        sp.dma_start(lng[:], rows("sgu_g")).then_inc(loaded, 16)
                        sp.dma_start(lnb[:], rows("sgu_b")).then_inc(loaded, 16)
                        weights.load(sp, "ab_z")

                    whole = slice(0, SEQ)
                    uv_first = weights.at["pe"]
                    uv_pieces, z_pieces = 2 * DK // 2, 4
                    k_of = lambda p, kk: 2 * (p % (DK // 2)) + kk

                    @block.tensor
                    def _(pe):
                        g = token_products(pe, "ab_uv", lat_tiles, lambda p, kk, i: tuple(
                            h[:, k_of(p, kk), i * P:(i + 1) * P] for h in hT), mm_done, evac)
                        feature_products(pe, "ab_z", hT, [whole], evac, g0=g)

                    @block.gpsimd
                    def _(pool):
                        nc.gpsimd.memset(z[:, :, 0:PAD], 0.0).then_inc(zeroed, 1)
                        nc.gpsimd.memset(z[:, :, PAD + SEQ:ZW], 0.0).then_inc(zeroed, 1)

                    @block.scalar
                    def _(act):
                        for p in range(uv_pieces // 2 + 2):
                            weights.hi(act)
                        for g in range(12):
                            if g < 8:
                                act.wait_ge(mm_done, g + 1)
                                to = (u if g < 4 else v)[:, g % 4, :]
                                nc.scalar.activation(to, ps[g % NROT][:], ACT.Gelu_apprx_tanh).then_inc(evac, 1)
                            else:
                                act.wait_ge(weights.piece_used, uv_first + uv_pieces + g - 8 + 1)
                                nc.scalar.copy(z[:, g - 8, PAD:PAD + SEQ], ps[g % NROT][:]).then_inc(evac, 1)
                            if g == 3:
                                for p in range(uv_pieces // 2 - 2 + 2):
                                    weights.hi(act)
                            if g in (8, 9):
                                weights.hi(act)
                        act.wait_ge(var_ready, 1)
                        nc.scalar.activation(inv[:], inv[:], ACT.Sqrt).then_inc(root_ready, 1)

                    @block.vector
                    def _(dve):
                        step = Chain(dve, chained)
                        for p in range(uv_pieces + z_pieces):
                            weights.lo(dve)
                        for t in range(LAT_T):
                            dve.wait_ge(evac, 4 + t + 1)
                            step(nc.vector.bn_stats(stats[:, t, :], v[:, t, :]))
                            step(nc.vector.bn_aggr(mv[:, t, :], stats[:, t, :]))
                        nc.vector.tensor_scalar(inv[:], mv[:, :, 1], LN_EPS, None, ALU.add).then_inc(var_ready, 1)
                        dve.wait_ge(root_ready, 1)
                        step(nc.vector.reciprocal(inv[:], inv[:]))
                        dve.wait_ge(loaded, 32)
                        for t in range(LAT_T):
                            step(nc.vector.tensor_scalar(v[:, t, :], v[:, t, :], mv[:, t, 0:1], inv[:, t:t + 1], ALU.subtract, ALU.mult))
                            step(nc.vector.tensor_tensor(v[:, t, :], v[:, t, :], lng[:], ALU.mult))
                            step(nc.vector.tensor_tensor(v[:, t, :], v[:, t, :], lnb[:], ALU.add))
                        side_sums(dve, "ab_z")
                        side_sums(dve, "ab_uv")
            with stage():
                wsT = sb("ws_transposed", [P, A_HEADS, P])
                bs = sb("spatial_bias", [P, A_HEADS])
                pool_w = sb("pool_w", [P, 4, P])
                pool_scale = sb("pool_scale", [P, 4])
                inv_count = sb("inv_count", [P, 4, SEQ])
                pooled = sb("pooled", [P, 4, SEQ])
                sums = sb("window_sums", [P, 2, ZW])
                loaded, mixed, gated, turned, copied = sem("loaded"), sem("mixed"), sem("gated"), sem("turned"), sem("copied")
                chained, pool_done, pool_mm = sem("vector_step"), sem("pooled"), sem("pool_product")
                n_loads = 5
                with nc.Block() as block:
                    @block.sync
                    def _(sp):
                        for dst, name in ((wsT, "wsT"), (bs, "bs"), (pool_w, "pool_w"), (pool_scale, "pool_scale")):
                            sp.dma_start(dst[:], dram[name]).then_inc(loaded, 16)
                        sp.dma_start(inv_count[:], dram["inv_count"].partition_broadcast(P)).then_inc(loaded, 16)

                    @block.tensor
                    def _(pe):
                        pe.wait_ge(loaded, 16 * n_loads)
                        for t in range(LAT_T):
                            for h in range(A_HEADS):
                                last = nc.tensor.matmul(ps[t][:, h * P:(h + 1) * P], wsT[:, h, :], v[:, t, h * P:(h + 1) * P],
                                                        start=True, stop=True)
                            last.then_inc(mixed, 1)
                        pe.wait_ge(gated, LAT_T)
                        for f in range(A_HEADS):
                            for t in range(LAT_T):
                                last = nc.tensor.transpose(ps[4 + f][:, t * P:(t + 1) * P], u[:, t, f * P:(f + 1) * P], ident[:])
                            last.then_inc(turned, 1)
                        for g in range(4):
                            pe.wait_ge(pool_done, g + 1)
                            nc.tensor.matmul(ps[g][:], pool_w[:, g, :], pooled[:, g, :], start=True, stop=True).then_inc(pool_mm, 1)

                    @block.vector
                    def _(dve):
                        step = Chain(dve, chained)
                        dve.wait_ge(loaded, 16 * n_loads)
                        for t in range(LAT_T):
                            dve.wait_ge(mixed, t + 1)
                            for h in range(A_HEADS):
                                cols = slice(h * P, (h + 1) * P)
                                last = nc.vector.scalar_tensor_tensor(out=u[:, t, cols], in0=ps[t][:, cols], scalar=bs[:, h:h + 1],
                                                                      in1=u[:, t, cols], op0=ALU.add, op1=ALU.mult)
                            last.then_inc(gated, 1)
                        for g in range(4):
                            window = 2 << g
                            src = z[:, g, :]
                            for level in range(g + 1):
                                lo, off = (2 << level) - 1, 1 << level
                                dst = sums[:, level % 2, :]
                                step(nc.vector.tensor_tensor(dst[:, lo:ZW], src[:, lo:ZW], src[:, lo - off:ZW - off], ALU.add))
                                src = dst
                            at = PAD + window // 2 - 1
                            step(nc.vector.tensor_tensor(pooled[:, g, :], src[:, at:at + SEQ], inv_count[:, g, :], ALU.mult))
                            ins = nc.vector.tensor_tensor(pooled[:, g, :], pooled[:, g, :], z[:, g, PAD:PAD + SEQ], ALU.subtract)
                            ins.then_inc(pool_done, 1)
                            dve.wait_ge(pool_done, g + 1)

                    @block.scalar
                    def _(act):
                        act.wait_ge(loaded, 16 * n_loads)
                        for f in range(A_HEADS):
                            act.wait_ge(turned, f + 1)
                            nc.scalar.copy(mixT[:, f, :], ps[4 + f][:]).then_inc(copied, 1)
                        for g in range(4):
                            act.wait_ge(pool_mm, g + 1)
                            nc.scalar.mul(mixT[:, 4 + g, :], ps[g][:], pool_scale[:, g:g + 1]).then_inc(copied, 1)
            dump("mixT", mixT[:])
            out_product_ln_stage("ab_out", lambda k: mixT[:, k:k + 2, :], "mix_ln_g0", "mix_ln_b0")

    def conformer_mixer(make_hT):
        HALF = CONV_W // 2
        with stage():
            zc = sb("conv_out", [P, DK, SEQ])
            with stage():
                hT = make_hT()
                zp = sb("glu_padded", [P, DK, SEQ + 2 * HALF])
                taps = sb("conv_taps", [P, DK, CONV_W + 1])
                gate = sb("sigmoid_gate", [P, 2, SEQ])
                loaded, zeroed, mm_done, evac = sem("loaded"), sem("zeroed"), sem("mm_done"), sem("evacuated")
                gated, chained = sem("gate_done"), sem("vector_step")
                first = weights.at["pe"]
                with nc.Block() as block:
                    @block.sync
                    def _(sp):
                        sp.dma_start(taps[:], dram["cv_taps"]).then_inc(loaded, 16)
                        weights.load(sp, "cv_in")

                    @block.gpsimd
                    def _(pool):
                        nc.gpsimd.memset(zp[:, :, 0:HALF], 0.0).then_inc(zeroed, 1)
                        nc.gpsimd.memset(zp[:, :, HALF + SEQ:], 0.0).then_inc(zeroed, 1)

                    @block.tensor
                    def _(pe):
                        feature_products(pe, "cv_in", hT, [slice(0, SEQ)], evac)

                    @block.scalar
                    def _(act):
                        weights.hi(act)
                        weights.hi(act)
                        for j in range(DK):
                            if j + 1 < DK:
                                weights.hi(act)
                                weights.hi(act)
                            act.wait_ge(weights.piece_used, first + 2 * j + 2)
                            if j >= 2:
                                act.wait_ge(evac, 2 * (j - 1))
                            nc.scalar.activation(gate[:, j % 2, :], ps[(2 * j + 1) % NROT][:], ACT.Sigmoid).then_inc(gated, 1)

                    @block.vector
                    def _(dve):
                        step = Chain(dve, chained)
                        dve.wait_ge(loaded, 16)
                        dve.wait_ge(zeroed, 2)
                        weights.lo(dve)
                        weights.lo(dve)
                        for j in range(DK):
                            if j + 1 < DK:
                                weights.lo(dve)
                                weights.lo(dve)
                            dve.wait_ge(gated, j + 1)
                            ins = nc.vector.tensor_tensor(zp[:, j, HALF:HALF + SEQ], ps[(2 * j) % NROT][:], gate[:, j % 2, :], ALU.mult)
                            ins.then_inc(evac, 2)
                            dve.wait_ge(evac, 2 * (j + 1))
                            step(nc.vector.tensor_scalar(zc[:, j, :], zp[:, j, 0:SEQ], taps[:, j, 0:1], taps[:, j, CONV_W:CONV_W + 1],
                                                         ALU.mult, ALU.add))
                            for i in range(1, CONV_W):
                                step(nc.vector.scalar_tensor_tensor(out=zc[:, j, :], in0=zp[:, j, i:i + SEQ], scalar=taps[:, j, i:i + 1],
                                                                    in1=zc[:, j, :], op0=ALU.mult, op1=ALU.add))
                        side_sums(dve, "cv_in")
            with stage():
                cols = sb("cv_ln_columns", [P, 2, DK])
                sq = sb("squares", [P, 2, SEQ])
                mean, inv = sb("mean", [P, SEQ]), sb("inv_std", [P, SEQ])
                loaded, mm_mean, centred, squared, mm_var = sem("loaded"), sem("mean_product"), sem("centred"), sem("squared"), sem("var_product")
                chained, var_ready, root_ready, normed, applied = sem("vector_step"), sem("var_ready"), sem("root_ready"), sem("normed"), sem("silu_done")
                sq_used = sem("square_used")
                with nc.Block() as block:
                    @block.sync
                    def _(sp):
                        sp.dma_start(cols[:], dram["cv_ln"]).then_inc(loaded, 16)

                    @block.tensor
                    def _(pe):
                        for j in range(DK):
                            last = nc.tensor.matmul(ps[0][:], ones[:], zc[:, j, :], start=(j == 0), stop=(j == DK - 1))
                        last.then_inc(mm_mean, 1)
                        for j in range(DK):
                            pe.wait_ge(squared, j + 1)
                            nc.tensor.matmul(ps[1][:], ones[:], sq[:, j % 2, :], start=(j == 0), stop=(j == DK - 1)).then_inc(sq_used, 1)

                    @block.vector
                    def _(dve):
                        step = Chain(dve, chained)
                        dve.wait_ge(mm_mean, 1)
                        step(nc.vector.tensor_scalar(mean[:], ps[0][:], 1.0 / D, None, ALU.mult))
                        for j in range(DK):
                            nc.vector.tensor_tensor(zc[:, j, :], zc[:, j, :], mean[:], ALU.subtract).then_inc(centred, 1)
                        dve.wait_ge(sq_used, DK)
                        nc.vector.tensor_scalar(inv[:], ps[1][:], 1.0 / D, LN_EPS, ALU.mult, ALU.add).then_inc(var_ready, 1)
                        dve.wait_ge(root_ready, 1)
                        step(nc.vector.reciprocal(inv[:], inv[:]))
                        dve.wait_ge(centred, DK)
                        for j in range(DK):
                            nc.vector.tensor_tensor(zc[:, j, :], zc[:, j, :], inv[:], ALU.mult).then_inc(normed, 1)

                    @block.scalar
                    def _(act):
                        for j in range(DK):
                            act.wait_ge(centred, j + 1)
                            if j >= 2:
                                act.wait_ge(sq_used, j - 1)
                            nc.scalar.activation(sq[:, j % 2, :], zc[:, j, :], ACT.Square).then_inc(squared, 1)
                        act.wait_ge(var_ready, 1)
                        nc.scalar.activation(inv[:], inv[:], ACT.Sqrt).then_inc(root_ready, 1)
                        act.wait_ge(loaded, 16)
                        for j in range(DK):
                            act.wait_ge(normed, j + 1)
                            nc.scalar.activation(zc[:, j, :], zc[:, j, :], ACT.Silu, bias=cols[:, 1, j:j + 1],
                                                 scale=cols[:, 0, j:j + 1]).then_inc(applied, 1)
            out_product_ln_stage("cv_out", lambda k: zc[:, k:k + 2, :], "mix_ln_g1", "mix_ln_b1")

    all_tiles = list(range(TOK_T))
    CTXS, HALVES = slice(0, CTX), (slice(0, BANK), slice(BANK, TOK))
    SHIFT, SCALE, GATE, FF_SHIFT, FF_SCALE, FF_GATE = (i * DK for i in range(6))

    parked = nc.dram_tensor("parked_residual", (P, TOK_T * D), F32, kind="Internal").ap()

    def modulation2_stage(layer):
        mod = mods[f"ada{layer}"]
        with stage():
            loaded = sem("loaded")
            with nc.Block() as block:
                @block.sync
                def _(sp):
                    sp.dma_start(gains[:], dram["gains"][layer]).then_inc(loaded, 16)

                @block.vector
                def _(dve):
                    dve.wait_ge(loaded, 16)
                    for i, (at, plus) in enumerate(((SCALE, 1.0), (GATE, 0.0), (FF_SCALE, 1.0), (FF_GATE, 0.0))):
                        for v in range(2):
                            nc.vector.scalar_tensor_tensor(out=mod[:, at:at + DK, v], in0=mod[:, at:at + DK, v], scalar=plus,
                                                           in1=gains[:, i, :], op0=ALU.add, op1=ALU.mult)

    def gates2_stage(layer, at, streams, beside=None):
        gate_row_stage([(v, [mods[f"ada{layer}"][:, at + f, v:v + 1] for f in range(DK)]) for v in range(streams)], beside)

    def modulated2_stage(layer, at_shift, at_scale, tiles, hT, t_base, buffers, beside=None):
        mod = mods[f"ada{layer}"]
        to_features_stage(resid, tiles, lambda f, v: mod[:, at_scale + f, v:v + 1],
                          lambda f, v: mod[:, at_shift + f, v:v + 1], hT, t_base, rms=buffers, beside=beside)

    def flat_of(x):
        return x[:].rearrange("p a b -> p (a b)")

    def out_product_rms_stage(name, source, tiles, bring_back=None):
        T = len(tiles)
        pieces = sum(nk // 2 for _, nk, _, _ in dict(MAIN)[name])
        with stage():
            product = sb("product", [P, T, D])
            left = LeftOperand(name, source, T * P)
            squares = sb("squares", [P, BANK])
            sums = sb("sums_of_squares", [P, T, 2])
            inv = sb("inv_rms", [P, T])
            mm_done, copied, squared = sem("mm_done"), sem("copied"), sem("squared")
            mean_ready, root_ready, chained, scaled, added = sem("mean_ready"), sem("root_ready"), sem("vector_step"), sem("scaled"), sem("added")
            brought = sem("residual_back")
            first = weights.at["pe"]
            with nc.Block() as block:
                @block.sync
                def _(sp):
                    weights.load(sp, name)
                    if bring_back is not None:
                        bring_back(sp, first, pieces, brought)

                @block.tensor
                def _(pe):
                    token_products(pe, name, tiles, left, mm_done, squared)

                @block.scalar
                def _(act):
                    for n in range(2):
                        for p in range(pieces // 2 + 1 if n == 0 else pieces // 2 - 1):
                            p += n * (pieces // 2 + 1)
                            weights.hi(act, left.share(p))
                        for i in range(T):
                            g = n * T + i
                            act.wait_ge(mm_done, g + 1)
                            nc.scalar.copy(product[:, i, n * BANK:(n + 1) * BANK], ps[g % NROT][:]).then_inc(copied, 1)
                            nc.scalar.activation(squares[:], ps[g % NROT][:], ACT.Square, accum_out=sums[:, i, n:n + 1]).then_inc(squared, 1)
                            act.wait_ge(squared, g + 1)
                    act.wait_ge(mean_ready, 1)
                    nc.scalar.activation(inv[:], inv[:], ACT.Sqrt).then_inc(root_ready, 1)

                @block.vector
                def _(dve):
                    step = Chain(dve, chained)
                    for p in range(pieces):
                        weights.lo(dve, left.share(p))
                    dve.wait_ge(squared, 2 * T)
                    step(nc.vector.tensor_tensor(inv[:], sums[:, :, 0], sums[:, :, 1], ALU.add))
                    nc.vector.tensor_scalar(inv[:], inv[:], 1.0 / D, RMS_EPS, ALU.mult, ALU.add).then_inc(mean_ready, 1)
                    dve.wait_ge(root_ready, 1)
                    step(nc.vector.reciprocal(inv[:], inv[:]))
                    for i, t in enumerate(tiles):
                        row = gate_rows[:, 0 if t >= CTX_T else 1, :]
                        nc.vector.scalar_tensor_tensor(out=product[:, i, :], in0=product[:, i, :], scalar=inv[:, i:i + 1],
                                                       in1=row, op0=ALU.mult, op1=ALU.mult).then_inc(scaled, 1)
                    side_sums(dve, name)

                @block.gpsimd
                def _(pool):
                    if bring_back is not None:
                        pool.wait_ge(brought, 16)
                    for i, t in enumerate(tiles):
                        pool.wait_ge(scaled, i + 1)
                        nc.gpsimd.tensor_tensor(resid[:, t, :], resid[:, t, :], product[:, i, :], ALU.add).then_inc(added, 1)

    def ffn2_stages(layer, tiles):
        segs = [slice(0, CTX), slice(CTX, TOK)] if tiles[0] == 0 else [slice(0, SEQ)]
        n_tok, FFK = len(tiles) * P, DFF // P
        n_borrowed = DK if tiles[0] == 0 else 0
        with stage():
            own = sb("ff_hidden", [P, FFK - n_borrowed, n_tok])
            borrowed = flat_of(resid).rearrange("p (k n) -> p k n", n=TOK)
            hidden = lambda k: borrowed[:, k:k + 2, :] if k < n_borrowed else own[:, k - n_borrowed:k - n_borrowed + 2, :]
            area = flat_of(own)
            buffers = (area[:, 0:D], area[:, D:D + TOK_T * D].rearrange("p (t d) -> p t d", d=D),
                       area[:, (TOK_T + 1) * D:(TOK_T + 3) * D].rearrange("p (b n) -> p b n", n=BANK))
            with stage():
                hT = hT_pair(n_tok)
                park = None
                moved = sem("residual_parked")
                if n_borrowed:
                    def park(sp):
                        sp.dma_start(parked, flat_of(resid)).then_inc(moved, 16)
                        sp.wait_ge(moved, 16)
                modulated2_stage(layer, FF_SHIFT, FF_SCALE, tiles, hT, tiles[0], buffers, beside=park)
                with stage():
                    relu_done = sem("relu_done")
                    first = weights.at["pe"]
                    up = f"ff1_{layer}"
                    with nc.Block() as block:
                        @block.sync
                        def _(sp):
                            weights.load(sp, up)

                        @block.tensor
                        def _(pe):
                            feature_products(pe, up, hT, segs, relu_done)

                        @block.scalar
                        def _(act):
                            weights.hi(act)
                            for j in range(FFK):
                                if j + 1 < FFK:
                                    weights.hi(act)
                                act.wait_ge(weights.piece_used, first + j + 1)
                                for s, seg in enumerate(segs):
                                    bank = ps[(j * len(segs) + s) % NROT][:, 0:seg.stop - seg.start]
                                    nc.scalar.activation(hidden(j - j % 2)[:, j % 2, seg], bank, ACT.Relu).then_inc(relu_done, 1)

                        @block.vector
                        def _(dve):
                            weights.lo(dve)
                            for j in range(FFK):
                                if j + 1 < FFK:
                                    weights.lo(dve)
                                dve.wait_ge(relu_done, (j + 1) * len(segs))
                                h = hidden(j - j % 2)[:, j % 2, :]
                                nc.vector.tensor_tensor(h, h, h, ALU.mult)
                            side_sums(dve, up)
            gates2_stage(layer, FF_GATE, 2 if n_borrowed else 1)

            def bring_back(sp, first, pieces, brought):
                sp.wait_ge(weights.lo_made, first + pieces // 2 + n_borrowed // 2)
                sp.dma_start(flat_of(resid), parked).then_inc(brought, 16)
            out_product_rms_stage(f"ff2_{layer}", hidden, tiles, bring_back if n_borrowed else None)

    def qkv_stage(qk_name, v_name, hT, raw, n_q, vtok, q_segs):
        n_k = raw.shape[1] - n_q
        v_cols = vtok.shape[2]
        wide = v_cols == BANK
        v_feat = flat_of(gate_rows)[:, 0:TOK]
        segs_of = lambda j: q_segs if j < n_q else [CTXS, LAT]
        with stage():
            mm_done, copied, turned = sem("mm_done"), sem("copied"), sem("v_turned")
            first = weights.at["pe"]
            N = n_q + n_k
            n_copies = sum(len(segs_of(j)) for j in range(N))
            with nc.Block() as block:
                @block.sync
                def _(sp):
                    weights.load(sp, v_name)

                @block.tensor
                def _(pe):
                    g = feature_products(pe, qk_name, hT, segs_of, copied)
                    if wide:
                        token_products(pe, v_name, all_tiles, lambda p, kk, i: tuple(
                            h[:, 2 * p + kk, i * P:(i + 1) * P] for h in hT), mm_done, copied, g0=g)
                    else:
                        g = feature_products(pe, v_name, hT, [CTXS, LAT], copied, g0=g)
                        pe.wait_ge(copied, g)
                        for t in all_tiles:
                            last = nc.tensor.transpose(ps[t // 4][:, (t % 4) * P:(t % 4 + 1) * P], v_feat[:, t * P:(t + 1) * P], ident[:])
                        last.then_inc(turned, 1)

                @block.scalar
                def _(act):
                    g, hi_left = 0, N + (DK // 2 if wide else 1)
                    weights.hi(act)
                    hi_left -= 1
                    for j in range(N + (0 if wide else 1)):
                        if hi_left:
                            weights.hi(act)
                            hi_left -= 1
                        act.wait_ge(weights.piece_used, first + j + 1)
                        for s in segs_of(j):
                            to = raw[:, j, s] if j < N else v_feat[:, s]
                            nc.scalar.copy(to, ps[g % NROT][:, 0:s.stop - s.start]).then_inc(copied, 1)
                            g += 1
                    if wide:
                        for _ in range(hi_left):
                            weights.hi(act)
                        for t in all_tiles:
                            act.wait_ge(mm_done, t + 1)
                            nc.scalar.copy(vtok[:, t, :], ps[(g + t) % NROT][:]).then_inc(copied, 1)
                    else:
                        act.wait_ge(turned, 1)
                        nc.scalar.copy(vtok[:, 0:4, :], ps[0][:].rearrange("p (t d) -> p t d", d=P))
                        nc.scalar.copy(vtok[:, 4:TOK_T, :], ps[1][:, 0:2 * P].rearrange("p (t d) -> p t d", d=P))

                @block.vector
                def _(dve):
                    for _ in range(N + (DK // 2 if wide else 1)):
                        weights.lo(dve)

    def qk_norm_stage(raw, n_q, q_cols):
        jobs = [(j, s) for j in range(raw.shape[1]) for s in ([q_cols] if j < n_q else HALVES)]
        with stage():
            gain = sb("head_gain", [P, 2])
            sq = sb("squares", [P, 2, BANK])
            inv = sb("inv_rms", [P, 2, BANK])
            loaded, squared, mm_done, mean_ready = sem("loaded"), sem("squared"), sem("mm_done"), sem("mean_ready")
            root_ready, chained, applied = sem("root_ready"), sem("vector_step"), sem("applied")
            with nc.Block() as block:
                @block.sync
                def _(sp):
                    sp.dma_start(gain[:], dram["d_gain"]).then_inc(loaded, 16)

                @block.scalar
                def _(act):
                    for i, (j, s) in enumerate(jobs):
                        n = s.stop - s.start
                        if i >= 2:
                            act.wait_ge(mm_done, i - 1)
                        nc.scalar.activation(sq[:, i % 2, 0:n], raw[:, j, s], ACT.Square).then_inc(squared, 1)
                        act.wait_ge(mean_ready, i + 1)
                        nc.scalar.activation(inv[:, i % 2, 0:n], inv[:, i % 2, 0:n], ACT.Sqrt).then_inc(root_ready, 1)

                @block.tensor
                def _(pe):
                    for i, (j, s) in enumerate(jobs):
                        n = s.stop - s.start
                        pe.wait_ge(squared, i + 1)
                        if i >= NBANK:
                            pe.wait_ge(mean_ready, i - NBANK + 1)
                        nc.tensor.matmul(ps[i % NBANK][:, 0:n], head_ones[:], sq[:, i % 2, 0:n], start=True, stop=True).then_inc(mm_done, 1)

                @block.vector
                def _(dve):
                    step = Chain(dve, chained)
                    dve.wait_ge(loaded, 16)
                    for i, (j, s) in enumerate(jobs):
                        n = s.stop - s.start
                        dve.wait_ge(mm_done, i + 1)
                        nc.vector.tensor_scalar(inv[:, i % 2, 0:n], ps[i % NBANK][:, 0:n], 1.0 / HD, RMS_EPS, ALU.mult, ALU.add).then_inc(mean_ready, 1)
                        dve.wait_ge(root_ready, i + 1)
                        step(nc.vector.reciprocal(inv[:, i % 2, 0:n], inv[:, i % 2, 0:n]))
                        col = gain[:, 0:1] if j < n_q else gain[:, 1:2]
                        step(nc.vector.scalar_tensor_tensor(out=raw[:, j, s], in0=raw[:, j, s], scalar=col,
                                                            in1=inv[:, i % 2, 0:n], op0=ALU.mult, op1=ALU.mult))

    def rope_stage(raw):
        n = raw.shape[1]
        with stage():
            turn, cos, sin = sb("turn", [P, P]), sb("cos", [P, SEQ]), sb("sin", [P, SEQ])
            part = sb("turned_part", [P, 2, SEQ])
            loaded, mm_done, turned, chained, added = sem("loaded"), sem("mm_done"), sem("turned"), sem("vector_step"), sem("added")
            with nc.Block() as block:
                @block.sync
                def _(sp):
                    for dst, name in ((turn, "rope_turn"), (cos, "rope_cos"), (sin, "rope_sin")):
                        sp.dma_start(dst[:], dram[name]).then_inc(loaded, 16)

                @block.tensor
                def _(pe):
                    pe.wait_ge(loaded, 48)
                    for j in range(n):
                        nc.tensor.matmul(ps[j][:], turn[:], raw[:, j, LAT], start=True, stop=True).then_inc(mm_done, 1)

                @block.vector
                def _(dve):
                    step = Chain(dve, chained)
                    dve.wait_ge(loaded, 48)
                    for j in range(n):
                        dve.wait_ge(mm_done, j + 1)
                        if j >= 2:
                            dve.wait_ge(added, j - 1)
                        step(nc.vector.tensor_tensor(part[:, j % 2, :], ps[j][:], sin[:], ALU.mult))
                        nc.vector.tensor_tensor(raw[:, j, LAT], raw[:, j, LAT], cos[:], ALU.mult).then_inc(turned, 1)

                @block.gpsimd
                def _(pool):
                    for j in range(n):
                        pool.wait_ge(turned, j + 1)
                        nc.gpsimd.tensor_tensor(raw[:, j, LAT], raw[:, j, LAT], part[:, j % 2, :], ALU.add).then_inc(added, 1)

    def spread_heads_stage(raw, n_q, k_low):
        with stage():
            copied = sem("copied")
            with nc.Block() as block:
                @block.gpsimd
                def _(pool):
                    nc.gpsimd.memset(k_low[HD:P], 0.0)

                @block.scalar
                def _(act):
                    nc.scalar.copy(k_low[0:HD], raw[0:HD, n_q:, :]).then_inc(copied, 1)

                @block.vector
                def _(dve):
                    dve.wait_ge(copied, 1)
                    nc.vector.memset(raw[0:HD, n_q:, :], 0.0)

    def attention_stage(raw, k_halves, vtok, mixT, mix_at, jobs, kv_of, mix_base=0, sink=None, mask=None, bias=None, park=False):
        items = [(job, h) for job in jobs for h in range(8)]
        N = len(items)
        with stage():
            sc = sb("scores", [P, 2, TOK])
            pr = sb("probs", [P, 2, TOK])
            pT = sb("probs_turned", [P, 2, TOK])
            o = sb("head_outputs", [P, 2, 512])
            top, total, esink, inv = (sb(n, [P, N]) for n in ("minus_max", "total", "exp_sink", "inv_total"))
            if bias is not None:
                NB = 4
                bias_ring = sb("bias_ring", [P, NB, SEQ])
                bias_landed = [sem(f"bias_landed{i}") for i in range(NB)]
            if mask is not None:
                mask_sb = sb("mask", [P, 3 * P])
            if sink is not None:
                sink_sb = sb("sink", [P, 8])
            loaded, scored, read, max_ready = sem("loaded"), sem("scored"), sem("scores_read"), sem("max_ready")
            exp_done, sink_done, turned, turn_copied, weighed, scaled = (sem(n) for n in (
                "exp_done", "sink_done", "probs_turned", "turn_copied", "weighed", "output_scaled"))
            parked_done = sem("residual_parked")
            o_turned, o_copied, chained = sem("outputs_turned"), sem("outputs_copied"), sem("vector_step")

            def spans(i):
                (qt, lat, _), h = items[i]
                n = CTX + (lat.stop - lat.start if lat else 0)
                keys = [0, 1] + ([c // P for c in range(lat.start, lat.stop, P)] if lat else [])
                return qt, h, lat, n, keys

            with nc.Block() as block:
                @block.sync
                def _(sp):
                    if park:
                        sp.dma_start(parked, flat_of(resid)).then_inc(parked_done, 16)
                    if mask is not None:
                        sp.dma_start(mask_sb[:], dram[mask]).then_inc(loaded, 16)
                    if sink is not None:
                        sp.dma_start(sink_sb[:], dram[sink].partition_broadcast(P)).then_inc(loaded, 16)
                    if bias is not None:
                        for i in range(N):
                            qt, h, lat, n, keys = spans(i)
                            if i >= NB:
                                sp.wait_ge(read, i - NB + 1)
                            sp.dma_start(bias_ring[:, i % NB, :], dram[bias][h, (qt - CTX_T) * P:(qt - CTX_T + 1) * P, :]).then_inc(bias_landed[i % NB], 16)
                    if park:
                        sp.wait_ge(parked_done, 16)

                @block.tensor
                def _(pe):
                    def score(i):
                        qt, h, lat, n, keys = spans(i)
                        if i >= 2:
                            pe.wait_ge(read, i - 1)
                        q = raw[:, h // 2, qt * P:(qt + 1) * P]
                        k = k_halves[h % 2][:, kv_of(h)[0], :]
                        b = 2 * (i % 2)
                        last = nc.tensor.matmul(ps[b][:, 0:CTX], q, k[:, 0:CTX], start=True, stop=True)
                        if lat:
                            last = nc.tensor.matmul(ps[b + 1][:, 0:n - CTX], q, k[:, lat], start=True, stop=True)
                        last.then_inc(scored, 1)

                    def turn(i):
                        qt, h, lat, n, keys = spans(i)
                        pe.wait_ge(exp_done, i + 1)
                        if i >= 1:
                            pe.wait_ge(turn_copied, i)
                        for m in range(len(keys)):
                            last = nc.tensor.transpose(ps[4 + m // 4][:, (m % 4) * P:(m % 4 + 1) * P],
                                                       pr[:, i % 2, m * P:(m + 1) * P], ident[:])
                        last.then_inc(turned, 1)

                    def weigh(i):
                        qt, h, lat, n, keys = spans(i)
                        pe.wait_ge(turn_copied, i + 1)
                        if i >= 1:
                            pe.wait_ge(scaled, i)
                        v = kv_of(h)[1]
                        for m, kt in enumerate(keys):
                            last = nc.tensor.matmul(ps[6][:, 0:HD], pT[:, i % 2, m * P:(m + 1) * P], vtok[:, kt, v],
                                                    start=(m == 0), stop=(m == len(keys) - 1))
                        last.then_inc(weighed, 1)

                    def turn_outputs(q):
                        pe.wait_ge(scaled, 8 * (q + 1))
                        if q >= 1:
                            pe.wait_ge(o_copied, q)
                        for f in range(4):
                            last = nc.tensor.transpose(ps[7][:, f * P:(f + 1) * P], o[:, q % 2, f * P:(f + 1) * P], ident[:])
                        last.then_inc(o_turned, 1)

                    for i in range(N + 3):
                        if i < N:
                            score(i)
                        if 1 <= i <= N:
                            turn(i - 1)
                        if 2 <= i <= N + 1:
                            weigh(i - 2)
                        if i >= 3 and (i - 2) % 8 == 0:
                            turn_outputs((i - 2) // 8 - 1)

                @block.vector
                def _(dve):
                    step = Chain(dve, chained)
                    if mask is not None or sink is not None:
                        dve.wait_ge(loaded, 16 * ((mask is not None) + (sink is not None)))

                    def front(i):
                        qt, h, lat, n, keys = spans(i)
                        b = 2 * (i % 2)
                        s = sc[:, i % 2, :]
                        dve.wait_ge(scored, i + 1)
                        if i >= 2:
                            dve.wait_ge(exp_done, i - 1)
                        first = nc.vector.tensor_scalar(s[:, 0:CTX], ps[b][:, 0:CTX], ATTN_SCALE, None, ALU.mult)
                        if lat:
                            step(first)
                            if bias is not None:
                                dve.wait_ge(bias_landed[i % NB], 16 * (i // NB + 1))
                                add = bias_ring[:, i % NB, :]
                            elif mask is not None:
                                add = mask_sb[:, items[i][0][2]]
                            if bias is not None or mask is not None:
                                last = nc.vector.scalar_tensor_tensor(out=s[:, CTX:n], in0=ps[b + 1][:, 0:n - CTX], scalar=ATTN_SCALE,
                                                                      in1=add, op0=ALU.mult, op1=ALU.add)
                            else:
                                last = nc.vector.tensor_scalar(s[:, CTX:n], ps[b + 1][:, 0:n - CTX], ATTN_SCALE, None, ALU.mult)
                        else:
                            last = first
                        last.then_inc(read, 1)
                        dve.wait_ge(read, i + 1)
                        step(nc.vector.tensor_reduce(top[:, i:i + 1], s[:, 0:n], AX_X, ALU.max))
                        if sink is not None:
                            step(nc.vector.tensor_tensor(top[:, i:i + 1], top[:, i:i + 1], sink_sb[:, h:h + 1], ALU.max))
                        nc.vector.tensor_scalar(top[:, i:i + 1], top[:, i:i + 1], -1.0, None, ALU.mult).then_inc(max_ready, 1)

                    def back(i):
                        qt, h, lat, n, keys = spans(i)
                        dve.wait_ge(sink_done if sink is not None else exp_done, i + 1)
                        if sink is not None:
                            step(nc.vector.tensor_tensor(total[:, i:i + 1], total[:, i:i + 1], esink[:, i:i + 1], ALU.add))
                        step(nc.vector.reciprocal(inv[:, i:i + 1], total[:, i:i + 1]))
                        q = i // 8
                        if i % 8 == 0 and q >= 2:
                            dve.wait_ge(o_turned, q - 1)
                        dve.wait_ge(weighed, i + 1)
                        nc.vector.tensor_scalar(o[:, q % 2, h * HD:(h + 1) * HD], ps[6][:, 0:HD], inv[:, i:i + 1], None,
                                                ALU.mult).then_inc(scaled, 1)

                    for i in range(N + 2):
                        if i < N:
                            front(i)
                        if i >= 2:
                            back(i - 2)

                @block.scalar
                def _(act):
                    if sink is not None:
                        act.wait_ge(loaded, 16 * ((mask is not None) + 1))

                    def exps(i):
                        qt, h, lat, n, keys = spans(i)
                        act.wait_ge(max_ready, i + 1)
                        if i >= 2:
                            act.wait_ge(turned, i - 1)
                        nc.scalar.activation(pr[:, i % 2, 0:n], sc[:, i % 2, 0:n], ACT.Exp, bias=top[:, i:i + 1],
                                             accum_out=total[:, i:i + 1]).then_inc(exp_done, 1)
                        if sink is not None:
                            nc.scalar.activation(esink[:, i:i + 1], sink_sb[:, h:h + 1], ACT.Exp, bias=top[:, i:i + 1]).then_inc(sink_done, 1)

                    def copy_turned(i):
                        qt, h, lat, n, keys = spans(i)
                        act.wait_ge(turned, i + 1)
                        if i >= 2:
                            act.wait_ge(weighed, i - 1)
                        first = nc.scalar.copy(pT[:, i % 2, 0:min(n, BANK)], ps[4][:, 0:min(n, BANK)])
                        if n > BANK:
                            nc.scalar.copy(pT[:, i % 2, BANK:n], ps[5][:, 0:n - BANK]).then_inc(turn_copied, 1)
                        else:
                            first.then_inc(turn_copied, 1)

                    def copy_outputs(q):
                        act.wait_ge(o_turned, q + 1)
                        qt = jobs[q][0]
                        nc.scalar.copy(mixT[:, mix_at:mix_at + 4, (qt - mix_base) * P:(qt - mix_base + 1) * P],
                                       ps[7][:].rearrange("p (f n) -> p f n", f=4)).then_inc(o_copied, 1)

                    for i in range(N + 3):
                        if i < N:
                            exps(i)
                        if 1 <= i <= N:
                            copy_turned(i - 1)
                        if i >= 3 and (i - 2) % 8 == 0:
                            copy_outputs((i - 2) // 8 - 1)

    def lat_cols(a, b):
        return slice(CTX + a * P, CTX + b * P)

    def windowed_attention(raw, vtok, mixT):
        rope_stage(raw)
        with stage():
            k_low = sb("k_low", [P, 2, TOK])
            spread_heads_stage(raw, 4, k_low)
            kv = lambda h: (h // 4, slice((h // 4) * HD, (h // 4 + 1) * HD))
            jobs = [(t, None, None) for t in range(CTX_T)]
            for n in range(LAT_T):
                a, b = max(n - 1, 0), min(n + 2, LAT_T)
                jobs.append((CTX_T + n, lat_cols(a, b), slice((a - n + 1) * P, (b - n + 1) * P)))
            attention_stage(raw, (k_low, raw[:, 4:6]), vtok, mixT, 4, jobs, kv, sink="b_sink", mask="window_mask", park=True)

    def odd_mixer():
        jobs = [(CTX_T + n, LAT, None) for n in range(LAT_T)]
        mixT = sb("mixT", [P, DK, SEQ])
        with stage():
            raw_d, v_d = sb("qk_d", [P, 6, TOK]), sb("v_d", [P, TOK_T, P])
            with stage():
                raw_c, v_c = sb("qk_c", [P, 8, TOK]), sb("v_c", [P, TOK_T, BANK])
                with stage():
                    hT = hT_pair(TOK)
                    buffers = (flat_of(gate_rows)[:, 0:D], flat_of(raw_c).rearrange("p (t d) -> p t d", d=D), v_c[:, 0:4, :])
                    modulated2_stage(1, SHIFT, SCALE, all_tiles, hT, 0, buffers)
                    qkv_stage("c_qk", "c_v", hT, raw_c, 4, v_c, [LAT])
                    qkv_stage("d_qk", "d_v", hT, raw_d, 4, v_d, [LAT])
                k_low = sb("k_low", [P, 4, TOK])
                spread_heads_stage(raw_c, 4, k_low)
                attention_stage(raw_c, (k_low, raw_c[:, 4:8]), v_c, mixT, 0, jobs, lambda h: (h // 2, slice(h * HD, (h + 1) * HD)),
                                mix_base=CTX_T, bias="rpb_table")
            qk_norm_stage(raw_d, 4, LAT)
            rope_stage(raw_d)
            k_low = sb("k_low", [P, 2, TOK])
            spread_heads_stage(raw_d, 4, k_low)
            attention_stage(raw_d, (k_low, raw_d[:, 4:6]), v_d, mixT, 4, jobs,
                            lambda h: (h // 4, slice((h // 4) * HD, (h // 4 + 1) * HD)), mix_base=CTX_T)
        return mixT

    R_MU, R_W0, R_A0, R_KK, R_KA, R_RK, R_GW, R_GB = 0, 30, 38, 46, 50, 54, 58, 62
    R_COLS = 66

    def shifted_products_stage(name, hT, dests, mu_tiles, rcols, raw, park=None):
        with stage():
            keep = sb("mu_keep", [P, 15])
            copied, chained, shifted, stored_tile = sem("copied"), sem("vector_step"), sem("shifted"), sem("tile_parked")
            first, J = weights.at["pe"], len(dests)
            mu = rcols[:, R_MU:R_MU + 30].rearrange("p (j m) -> p j m", m=2)
            with nc.Block() as block:
                @block.sync
                def _(sp):
                    weights.load(sp, name)

                if park is not None:
                    @block.gpsimd
                    def _(pool):
                        for j, dst in enumerate(dests):
                            pool.wait_ge(shifted, j + 1)
                            pool.dma_start(park[:, j * TOK:(j + 1) * TOK], dst).then_inc(stored_tile, 16)
                        pool.wait_ge(stored_tile, 16 * J)

                @block.tensor
                def _(pe):
                    feature_products(pe, name, hT, [CTXS, LAT], copied)

                @block.scalar
                def _(act):
                    weights.hi(act)
                    for j in range(J):
                        if j + 1 < J:
                            weights.hi(act)
                        act.wait_ge(weights.piece_used, first + j + 1)
                        if j >= 2:
                            act.wait_ge(shifted, j - 1)
                        for s, seg in enumerate((CTXS, LAT)):
                            nc.scalar.copy(raw[:, j % 2, seg], ps[(2 * j + s) % NROT][:, 0:seg.stop - seg.start]).then_inc(copied, 1)

                @block.vector
                def _(dve):
                    step = Chain(dve, chained)
                    step(nc.vector.tensor_tensor(keep[:], mu[:, :, 0], mu[:, :, 1], ALU.add))
                    step(nc.vector.tensor_scalar(keep[:], keep[:], -1.0, 1.0, ALU.mult, ALU.add))
                    weights.lo(dve)
                    for j, (dst, m) in enumerate(zip(dests, mu_tiles)):
                        if j + 1 < J:
                            weights.lo(dve)
                        p = raw[:, j % 2, :]
                        dve.wait_ge(copied, 2 * j + 2)
                        step(nc.vector.tensor_scalar(dst, p, keep[:, m:m + 1], None, ALU.mult))
                        for seg in (CTXS, LAT):
                            a, b = seg.start, seg.stop
                            step(nc.vector.scalar_tensor_tensor(out=dst[:, a + 1:b], in0=p[:, a:b - 1], scalar=mu[:, m, 0:1],
                                                                in1=dst[:, a + 1:b], op0=ALU.mult, op1=ALU.add))
                            last = nc.vector.scalar_tensor_tensor(out=dst[:, a:b - 1], in0=p[:, a + 1:b], scalar=mu[:, m, 1:2],
                                                                  in1=dst[:, a:b - 1], op0=ALU.mult, op1=ALU.add)
                            if seg is CTXS:
                                step(last)
                        last.then_inc(shifted, 1)
                        dve.wait_ge(shifted, j + 1)

    parked_rkv = nc.dram_tensor("parked_rkv", (P, 6 * TOK), F32, kind="Internal").ap()

    def even_mixer(mixT):
        flat2 = flat_of(gate_rows)
        with stage():
            rcols = sb("recurrence_columns", [P, R_COLS])
            lora = sb("lora", [P, 3, TOK])
            r, k, v = (sb(n, [P, 2, TOK]) for n in ("r", "k_then_y", "v"))
            with stage():
                raw_b, v_b = sb("qk_b", [P, 6, TOK]), sb("v_b", [P, TOK_T, P])
                with stage():
                    hT = hT_pair(TOK)
                    loaded = sem("loaded")

                    def load_columns(sp):
                        sp.dma_start(rcols[:], dram["r_cols"]).then_inc(loaded, 16)
                        sp.wait_ge(loaded, 16)
                    buffers = (flat2[:, 0:D], flat_of(mixT).rearrange("p (t d) -> p t d", d=D),
                               flat_of(raw_b)[:, 0:4 * BANK].rearrange("p (b n) -> p b n", n=BANK))
                    modulated2_stage(0, SHIFT, SCALE, all_tiles, hT, 0, buffers, beside=load_columns)
                    qkv_stage("b_qk", "b_v", hT, raw_b, 4, v_b, [CTXS, LAT])
                    raw = flat2[:, 0:2 * TOK].rearrange("p (b n) -> p b n", b=2)
                    shifted_products_stage("lora", hT, [lora[:, j, :] for j in range(3)], [12, 13, 14], rcols, raw)
                    with stage():
                        with nc.Block() as block:
                            @block.scalar
                            def _(act):
                                nc.scalar.activation(lora[:, 0, :], lora[:, 0, :], ACT.Tanh)
                                nc.scalar.activation(lora[:, 2, :], lora[:, 2, :], ACT.Sigmoid)
                    later = mixT[:, 0:6, :]
                    tiles_of = lambda half: [4 * x + 2 * half + j for x in range(3) for j in range(2)]
                    shifted_products_stage("rkv0", hT, [x[:, j, :] for x in (r, k, v) for j in range(2)], tiles_of(0), rcols, raw)
                    shifted_products_stage("rkv1", hT, [later[:, j, :] for j in range(6)], tiles_of(1), rcols, raw, park=parked_rkv)
                windowed_attention(raw_b, v_b, mixT)
            dump("battn", mixT[:, 4:8, :])
            recurrence(rcols, lora, r, k, v, mixT)

    def recurrence(rcols, lora, r, k, v, mixT):
        flat, flat2 = flat_of(resid), flat_of(gate_rows)
        with stage():
            kk = sb("kk", [P, 2, TOK])
            iclr, kdir = sb("iclr_then_b", [P, 4, TOK]), sb("k_dir", [P, 4, TOK])
            run = sb("running_decay", [P, 4, NCH * CW])
            gam = sb("chunk_decay", [P, 3, 4, NCH])
            for half in range(2):
                prepare_stage(half, rcols, lora, r, k, v, kk, iclr, kdir, run, gam, mixT, flat)
                if half == 0:
                    dump("kk", kk[:]); dump("kdir", kdir[:]); dump("run", run[:]); dump("bb", iclr[:]); dump("bv", mixT[:, 0:2, :])
                scan_stage(r, k, v, kk, iclr, kdir, run, gam, flat, flat2)
                if half == 0:
                    dump("y", k[:])
                head_norm_stage(half, rcols, lora, r, k, v, mixT, flat)
                if half == 0:
                    with stage():
                        moved = sem("k_loaded")
                        with nc.Block() as block:
                            @block.sync
                            def _(sp):
                                sp.dma_start(flat_of(k), parked_rkv[:, 2 * TOK:4 * TOK]).then_inc(moved, 16)
                                sp.wait_ge(moved, 16)

    def prepare_stage(half, rcols, lora, r, k, v, kk, iclr, kdir, run, gam, mixT, flat):
        f0 = 2 * half
        col = lambda at, f: rcols[:, at + f:at + f + 1]
        SW = NCH * CW
        sg = flat[:, 0:2 * SW].rearrange("p (b n) -> p b n", b=2)
        tmp = flat[:, 2 * SW:2 * SW + 2 * TOK].rearrange("p (b n) -> p b n", b=2)
        tmp2 = flat[:, 2 * SW + 2 * TOK:2 * SW + 3 * TOK]
        with stage():
            w2, a2 = sb("w2", [P, 2, 2 * P]), sb("a2", [P, 2, 2 * P])
            reset = sb("reset", [P, SW])
            omka = sb("one_minus_ka", [P, 4])
            loaded, zeroed, w_mm, w_sig, a_mm, a_sig, scanned = (sem(n) for n in (
                "loaded", "zeroed", "w_product", "w_sigmoid", "a_product", "a_sigmoid", "scanned"))
            kk_sq, kk_mm, kk_root, r_ready, r_mm, chained, kk_made = (sem(n) for n in (
                "kk_squared", "kk_product", "kk_root", "bonus_terms", "bonus_product", "vector_step", "kk_made"))
            sq_made = sem("kk_unnormed")
            tots = sem("totals")
            gam_made = sem("chunk_decays")
            with nc.Block() as block:
                @block.sync
                def _(sp):
                    sp.dma_start(w2[:], dram["w2"][half]).then_inc(loaded, 16)
                    sp.dma_start(a2[:], dram["a2"][half]).then_inc(loaded, 16)
                    sp.dma_start(reset[:], dram["reset"].partition_broadcast(P)).then_inc(loaded, 16)

                @block.gpsimd
                def _(pool):
                    for b in range(2):
                        nc.gpsimd.memset(sg[:, b, :], 0.0).then_inc(zeroed, 1)

                @block.tensor
                def _(pe):
                    pe.wait_ge(loaded, 48)
                    for i in range(4):
                        d, f = divmod(i, 2)
                        if i >= 2:
                            pe.wait_ge(w_sig, 2 * (i - 1))
                        for s, seg in enumerate(HALVES):
                            nc.tensor.matmul(ps[2 * (i % 2) + s][:, 0:seg.stop - seg.start], w2[:, d, f * P:(f + 1) * P],
                                             lora[:, 0, seg], start=True, stop=True).then_inc(w_mm, 1)
                        if i >= 2:
                            pe.wait_ge(a_sig, 2 * (i - 1))
                        for s, seg in enumerate(HALVES):
                            nc.tensor.matmul(ps[4 + 2 * (i % 2) + s][:, 0:seg.stop - seg.start], a2[:, d, f * P:(f + 1) * P],
                                             lora[:, 1, seg], start=True, stop=True).then_inc(a_mm, 1)
                    pe.wait_ge(w_sig, 8)
                    for f in range(2):
                        pe.wait_ge(kk_sq, f + 1)
                        for s, seg in enumerate(HALVES):
                            nc.tensor.matmul(ps[2 * f + s][:, 0:seg.stop - seg.start], head_ones[:], tmp[:, f, seg],
                                             start=True, stop=True).then_inc(kk_mm, 1)
                    pe.wait_ge(a_sig, 8)
                    for f in range(2):
                        pe.wait_ge(r_ready, f + 1)
                        for s, seg in enumerate(HALVES):
                            nc.tensor.matmul(ps[4 + 2 * f + s][:, 0:seg.stop - seg.start], head_ones[:], tmp[:, f, seg],
                                             start=True, stop=True).then_inc(r_mm, 1)

                @block.scalar
                def _(act):
                    act.wait_ge(zeroed, 2)
                    for i in range(4):
                        d, f = divmod(i, 2)
                        if i >= 2:
                            act.wait_ge(scanned, i - 1)
                        for s, seg in enumerate(HALVES):
                            n = (seg.stop - seg.start) // CH
                            c0 = seg.start // CH
                            to = sg[:, i % 2, :].rearrange("p (c w) -> p c w", w=CW)[:, c0:c0 + n, 1:CW]
                            act.wait_ge(w_mm, 2 * i + s + 1)
                            nc.scalar.activation(to, ps[2 * (i % 2) + s][:, 0:n * CH].rearrange("p (c w) -> p c w", w=CH), ACT.Sigmoid,
                                                 bias=rcols[:, R_W0 + 4 * d + f0 + f:R_W0 + 4 * d + f0 + f + 1]).then_inc(w_sig, 1)
                        for s, seg in enumerate(HALVES):
                            act.wait_ge(a_mm, 2 * i + s + 1)
                            nc.scalar.activation(iclr[:, i, seg], ps[4 + 2 * (i % 2) + s][:, 0:seg.stop - seg.start], ACT.Sigmoid,
                                                 bias=rcols[:, R_A0 + 4 * d + f0 + f:R_A0 + 4 * d + f0 + f + 1]).then_inc(a_sig, 1)
                    for f in range(2):
                        act.wait_ge(sq_made, f + 1)
                        nc.scalar.activation(tmp[:, f, :], kk[:, f, :], ACT.Square).then_inc(kk_sq, 1)
                    for f in range(2):
                        for s, seg in enumerate(HALVES):
                            act.wait_ge(kk_mm, 2 * f + s + 1)
                            nc.scalar.activation(tmp[:, f, seg], ps[2 * f + s][:, 0:seg.stop - seg.start], ACT.Sqrt).then_inc(kk_root, 1)
                    act.wait_ge(tots, 2)
                    nc.scalar.activation(gam[:, 0, :, :], gam[:, 1, :, :], ACT.Exp).then_inc(gam_made, 1)

                @block.vector
                def _(dve):
                    step = Chain(dve, chained)
                    for f in range(2):
                        nc.vector.tensor_scalar(kk[:, f, :], k[:, f, :], col(R_KK, f0 + f), None, ALU.mult).then_inc(sq_made, 1)
                    dve.wait_ge(loaded, 48)
                    for i in range(4):
                        dve.wait_ge(w_sig, 2 * i + 2)
                        nc.vector.tensor_tensor_scan(out=run[:, i, :], data0=reset[:], data1=sg[:, i % 2, :], initial=0.0,
                                                     op0=ALU.mult, op1=ALU.add).then_inc(scanned, 1)
                    dve.wait_ge(scanned, 4)
                    ends = run[:].rearrange("p i (c w) -> p i c w", w=CW)[:, :, :, CH]
                    nc.vector.tensor_scalar(gam[:, 1, :, :], ends, -DECAY, None, ALU.mult).then_inc(tots, 1)
                    nc.vector.tensor_scalar(gam[:, 2, :, :], ends, DECAY, None, ALU.mult).then_inc(tots, 1)
                    step(nc.vector.tensor_scalar(omka[:], rcols[:, R_KA:R_KA + 4], -1.0, 1.0, ALU.mult, ALU.add))
                    dve.wait_ge(kk_root, 4)
                    for f in range(2):
                        step(nc.vector.tensor_scalar(tmp[:, f, :], tmp[:, f, :], 1e-12, None, ALU.max))
                        step(nc.vector.reciprocal(tmp[:, f, :], tmp[:, f, :]))
                        step(nc.vector.tensor_tensor(kk[:, f, :], kk[:, f, :], tmp[:, f, :], ALU.mult))
                    dve.wait_ge(a_sig, 8)
                    for i in range(4):
                        d, f = divmod(i, 2)
                        step(nc.vector.tensor_scalar(kdir[:, i, :], iclr[:, i, :], col(R_KA, f0 + f), omka[:, f0 + f:f0 + f + 1], ALU.mult, ALU.add))
                        step(nc.vector.tensor_tensor(kdir[:, i, :], kdir[:, i, :], k[:, f, :], ALU.mult))
                        step(nc.vector.tensor_tensor(iclr[:, i, :], iclr[:, i, :], kk[:, f, :], ALU.mult))
                    for f in range(2):
                        step(nc.vector.tensor_tensor(tmp2, kdir[:, f, :], kdir[:, 2 + f, :], ALU.add))
                        nc.vector.scalar_tensor_tensor(out=tmp[:, f, :], in0=tmp2, scalar=col(R_RK, f0 + f), in1=r[:, f, :],
                                                       op0=ALU.mult, op1=ALU.mult).then_inc(r_ready, 1)
                        dve.wait_ge(r_ready, f + 1)
                    for f in range(2):
                        for s, seg in enumerate(HALVES):
                            dve.wait_ge(r_mm, 2 * f + s + 1)
                            step(nc.vector.tensor_tensor(mixT[:, f0 + f, seg], ps[4 + 2 * f + s][:, 0:seg.stop - seg.start], v[:, f, seg], ALU.mult))

    PE_MAKES = ["b_turned", "k_turned", "v_turned", "A_ab", "A_ak_T", "A_r_T", "N", "T0"] + \
        [x for l in range(1, LEVELS) for x in (f"X{l}", f"GX{l}", f"T{l}")][:-1] + ["Z", "U", "Y", "S"]
    DVE_MAKES = [f"a{d}{h}" for d in range(2) for h in range(2)] + ["r0", "r1", "A_ab", "A_ak_T", "A_r_T"] + \
        [f"G{l}" for l in range(LEVELS)] + ["Z", "Y0", "Y1", "S_sum", "S0", "S1"]
    ACT_MAKES = [f"e{j}" for j in range(9)] + ["b_turned", "k_turned", "v_turned", "T0"] + \
        [x for l in range(1, LEVELS) for x in (f"X{l}", f"T{l}")][:-1] + ["U"]
    POOL_MAKES = [f"{x}{d}{h}" for x in "bkv" for d in range(2) for h in range(2)] + ["G_init"]

    def scan_stage(r, y, v, kk, bb, kdir, run, gam, flat, flat2):
        with stage():
            def full(i):
                return flat[:, i * 512:(i + 1) * 512].rearrange("p (i n) -> p i n", i=4)
            aexp, bexp, kexp, vexp, A_ab, A_ak_T, G, T, X, Bt, Kt, V = (full(i) for i in range(12))
            U, Z, S = (flat2[:, i * 512:(i + 1) * 512].rearrange("p (i n) -> p i n", i=4) for i in range(3))
            A_r_T = flat2[:, 1536:2048].rearrange("p (m i n) -> p m i n", m=2, i=4)
            e = sb("decay_factors", [P, 3, 4, CH])
            rc = sb("r_decayed", [P, 4, CH])
            before = sb("mask_before", [P, 2, P])
            before_T = sb("mask_before_T", [P, 2, P])
            upto_T = sb("mask_upto_T", [P, 2, CH])
            level = sb("level_masks", [P, LEVELS, 2, P], U8)
            level_f32 = flat[:, 9 * 512:12 * 512]
            loaded, zeroed, levels_cast = sem("loaded"), sem("zeroed"), sem("levels_cast")
            made = {"PE": sem("product_made"), "DVE": sem("vector_made"), "ACT": sem("scalar_made"), "POOL": sem("pool_made")}
            order = {"PE": PE_MAKES, "DVE": DVE_MAKES, "ACT": ACT_MAKES, "POOL": POOL_MAKES}

            def need(eng, who, what, c):
                if c >= 0:
                    eng.wait_ge(made[who], c * len(order[who]) + order[who].index(what) + 1)

            def chunk(d, c):
                return c if d == 0 else (CTX_CH - 1 - c if c < CTX_CH else NCH + CTX_CH - 1 - c)

            def tokens(d, c):
                return slice(chunk(d, c) * CH, (chunk(d, c) + 1) * CH)

            def per_dir(mask):
                return mask.unsqueeze(2).broadcast_to([P, 2, 2, mask.shape[2]])

            def by_dir(x):
                return x.rearrange("p (d f) n -> p d f n", d=2)

            def bank(b, n=P):
                return ps[b][:, 0:4 * n].rearrange("p (i n) -> p i n", i=4)

            halves = [(slice(0, HD), slice(0, CH)), (slice(HD, P), slice(CH, P))]

            with nc.Block() as block:
                @block.sync
                def _(sp):
                    for dst, name in ((before, "mask_before"), (before_T, "mask_before_T"), (upto_T, "mask_upto_T")):
                        sp.dma_start(dst[:], dram[name]).then_inc(loaded, 16)
                    sp.dma_start(level_f32, dram["level_masks"]).then_inc(loaded, 16)

                @block.gpsimd
                def _(pool):
                    for x in (aexp, bexp, kexp, vexp, S, y[:]):
                        nc.gpsimd.memset(x, 0.0).then_inc(zeroed, 1)
                    pool.wait_ge(zeroed, 6)
                    for c in range(NCH):
                        need(pool, "PE", "A_r_T", c - 1)
                        for d in range(2):
                            need(pool, "ACT", "e2" if d == 0 else "e8", c)
                            for h, (rows_, cols) in enumerate(halves):
                                nc.gpsimd.tensor_tensor(bexp[rows_, 2 * d:2 * d + 2, cols], bb[rows_, 2 * d:2 * d + 2, tokens(d, c)],
                                                        e[rows_, 2, 2 * d:2 * d + 2, :], ALU.mult).then_inc(made["POOL"], 1)
                        for d in range(2):
                            for h, (rows_, cols) in enumerate(halves):
                                nc.gpsimd.tensor_tensor(kexp[rows_, 2 * d:2 * d + 2, cols], kdir[rows_, 2 * d:2 * d + 2, tokens(d, c)],
                                                        e[rows_, 2, 2 * d:2 * d + 2, :], ALU.mult).then_inc(made["POOL"], 1)
                        for d in range(2):
                            for h, (rows_, cols) in enumerate(halves):
                                nc.gpsimd.tensor_copy(vexp[rows_, 2 * d:2 * d + 2, cols], v[rows_, :, tokens(d, c)]).then_inc(made["POOL"], 1)
                        need(pool, "PE", "U", c - 1)
                        need(pool, "POOL", "v11", c)
                        nc.gpsimd.tensor_copy(G, ident[:].unsqueeze(1).broadcast_to([P, 4, P])).then_inc(made["POOL"], 1)
                        need(pool, "POOL", "G_init", c)

                @block.scalar
                def _(act):
                    R = run[:].rearrange("p i (c w) -> p i c w", w=CW)
                    act.wait_ge(levels_cast, 1)
                    for c in range(NCH):
                        need(act, "DVE", "r1", c - 1)
                        need(act, "POOL", "k11", c - 1)
                        x = R[:, 0:2, chunk(0, c), :]
                        for j, (lo, sign) in enumerate(((0, -DECAY), (1, -DECAY), (1, DECAY))):
                            nc.scalar.activation(e[:, j, 0:2, :], x[:, :, lo:lo + CH], ACT.Exp, scale=sign).then_inc(made["ACT"], 1)
                        cb = chunk(1, c)
                        for j, (lo, sign, total) in enumerate(((1, DECAY, 1), (0, DECAY, 1), (0, -DECAY, 2))):
                            for i in (2, 3):
                                nc.scalar.activation(e[:, j, i, :], R[:, i, cb, lo:lo + CH], ACT.Exp, scale=sign,
                                                     bias=gam[:, total, i, cb:cb + 1]).then_inc(made["ACT"], 1)
                        for name, dst, b in (("b_turned", Bt, 0), ("k_turned", Kt, 1), ("v_turned", V, 2)):
                            need(act, "PE", name, c)
                            nc.scalar.copy(dst, bank(b)).then_inc(made["ACT"], 1)
                        need(act, "PE", "T0", c)
                        nc.scalar.copy(T, bank(3)).then_inc(made["ACT"], 1)
                        for l in range(1, LEVELS):
                            need(act, "PE", f"X{l}", c)
                            nc.scalar.copy(X, bank(6)).then_inc(made["ACT"], 1)
                            if l < LEVELS - 1:
                                need(act, "PE", f"T{l}", c)
                                nc.scalar.copy(T, bank(3)).then_inc(made["ACT"], 1)
                        need(act, "PE", "U", c)
                        nc.scalar.copy(U, bank(5)).then_inc(made["ACT"], 1)

                @block.vector
                def _(dve):
                    dve.wait_ge(loaded, 64)
                    nc.vector.tensor_copy(level[:].rearrange("p l d n -> p (l d n)"), level_f32).then_inc(levels_cast, 1)
                    dve.wait_ge(levels_cast, 1)
                    dve.wait_ge(zeroed, 6)
                    for c in range(NCH):
                        need(dve, "PE", "Z", c - 1)
                        for d in range(2):
                            need(dve, "ACT", "e0" if d == 0 else "e4", c)
                            for h, (rows_, cols) in enumerate(halves):
                                nc.vector.scalar_tensor_tensor(out=aexp[rows_, 2 * d:2 * d + 2, cols], in0=kk[rows_, :, tokens(d, c)], scalar=-1.0,
                                                               in1=e[rows_, 0, 2 * d:2 * d + 2, :], op0=ALU.mult, op1=ALU.mult).then_inc(made["DVE"], 1)
                        for d in range(2):
                            need(dve, "ACT", "e1" if d == 0 else "e6", c)
                            nc.vector.tensor_tensor(rc[:, 2 * d:2 * d + 2, :], r[:, :, tokens(d, c)], e[:, 1, 2 * d:2 * d + 2, :],
                                                    ALU.mult).then_inc(made["DVE"], 1)
                        need(dve, "PE", "A_ab", c)
                        nc.vector.tensor_tensor(by_dir(A_ab), by_dir(bank(3)), per_dir(before[:]), ALU.mult).then_inc(made["DVE"], 1)
                        need(dve, "PE", "A_ak_T", c)
                        nc.vector.tensor_tensor(by_dir(A_ak_T), by_dir(bank(4)), per_dir(before_T[:]), ALU.mult).then_inc(made["DVE"], 1)
                        need(dve, "PE", "A_r_T", c)
                        for m in range(2):
                            ins = nc.vector.tensor_tensor(by_dir(A_r_T[:, m]), by_dir(ps[5][:, m * 256:(m + 1) * 256].rearrange("p (i n) -> p i n", i=4)),
                                                          per_dir(upto_T[:]), ALU.mult)
                        ins.then_inc(made["DVE"], 1)
                        for l in range(LEVELS):
                            need(dve, "POOL", "G_init", c)
                            need(dve, "PE", "N" if l == 0 else f"GX{l}", c)
                            nc.vector.copy_predicated(by_dir(G), per_dir(level[:, l]), by_dir(bank(7))).then_inc(made["DVE"], 1)
                        need(dve, "PE", "Z", c)
                        nc.vector.tensor_copy(Z, bank(4)).then_inc(made["DVE"], 1)
                        need(dve, "PE", "Y", c)
                        for d in range(2):
                            cols = tokens(d, c)
                            if d == 1:
                                need(dve, "DVE", "Y0", c)
                            nc.vector.tensor_tensor(y[:, :, cols], y[:, :, cols], bank(0, CH)[:, 2 * d:2 * d + 2, :], ALU.add).then_inc(made["DVE"], 1)
                        need(dve, "PE", "S", c)
                        nc.vector.tensor_tensor(S, S, bank(1), ALU.add).then_inc(made["DVE"], 1)
                        need(dve, "DVE", "S_sum", c)
                        for d in range(2):
                            decay = gam[:, 0, 2 * d:2 * d + 2, chunk(d, c)].unsqueeze(2).broadcast_to([P, 2, P])
                            nc.vector.tensor_tensor(S[:, 2 * d:2 * d + 2, :], S[:, 2 * d:2 * d + 2, :], decay, ALU.mult).then_inc(made["DVE"], 1)
                        need(dve, "DVE", "S1", c)

                @block.tensor
                def _(pe):
                    def four(out, lhs, rhs, start=True, stop=True):
                        for i in range(4):
                            last = nc.tensor.matmul(out[:, i, :], lhs[:, i, :], rhs[:, i, :], start=start, stop=stop)
                        return last

                    def turn(out, x):
                        for i in range(4):
                            last = nc.tensor.transpose(out[:, i, :], x[:, i, :], ident[:])
                        return last

                    def sums(out, terms):
                        for i in range(4):
                            for n, (lhs, rhs) in enumerate(terms):
                                last = nc.tensor.matmul(out[:, i, :], lhs[:, i, :], rhs[:, i, :], start=(n == 0), stop=(n == len(terms) - 1))
                        return last

                    for c in range(NCH):
                        need(pe, "POOL", "v11", c)
                        need(pe, "DVE", "S1", c - 1)
                        turn(bank(0), bexp).then_inc(made["PE"], 1)
                        turn(bank(1), kexp).then_inc(made["PE"], 1)
                        turn(bank(2), vexp).then_inc(made["PE"], 1)
                        need(pe, "DVE", "r1", c)
                        four(bank(3), aexp, bexp).then_inc(made["PE"], 1)
                        four(bank(4), kexp, aexp).then_inc(made["PE"], 1)
                        need(pe, "ACT", "U", c - 1)
                        for m, x in enumerate((bexp, kexp)):
                            last = four(ps[5][:, m * 256:(m + 1) * 256].rearrange("p (i n) -> p i n", i=4), x, rc)
                        last.then_inc(made["PE"], 1)
                        need(pe, "DVE", "A_ab", c)
                        for i in range(4):
                            last = nc.tensor.matmul(bank(7)[:, i, :], A_ab[:, i, :], ident[:], start=True, stop=True)
                        last.then_inc(made["PE"], 1)
                        need(pe, "DVE", "G0", c)
                        turn(bank(3), G).then_inc(made["PE"], 1)
                        for l in range(1, LEVELS):
                            four(bank(6), A_ab, G).then_inc(made["PE"], 1)
                            need(pe, "ACT", f"X{l}", c)
                            need(pe, "ACT", f"T{l - 1}", c)
                            four(bank(7), T, X).then_inc(made["PE"], 1)
                            need(pe, "DVE", f"G{l}", c)
                            if l < LEVELS - 1:
                                turn(bank(3), G).then_inc(made["PE"], 1)
                        need(pe, "ACT", "v_turned", c)
                        need(pe, "DVE", "A_ak_T", c)
                        sums(bank(4), [(aexp, S), (A_ak_T, V)]).then_inc(made["PE"], 1)
                        need(pe, "DVE", "Z", c)
                        four(bank(5), G, Z).then_inc(made["PE"], 1)
                        need(pe, "ACT", "U", c)
                        need(pe, "DVE", "A_r_T", c)
                        sums(bank(0, CH), [(S, rc), (U, A_r_T[:, 0]), (V, A_r_T[:, 1])]).then_inc(made["PE"], 1)
                        sums(bank(1), [(Bt, U), (Kt, V)]).then_inc(made["PE"], 1)

    def head_norm_stage(half, rcols, lora, r, y, v, mixT, flat):
        f0 = 2 * half
        inv = flat[:, 0:2 * TOK].rearrange("p (b n) -> p b n", b=2)
        jobs = [(f, s) for f in range(2) for s in HALVES]
        with stage():
            g2 = sb("g2", [P, 2 * P])
            brought = sem("brought_back")
            loaded, mean_mm, centred, squared, var_mm, var_ready, root_ready, gate_mm, chained = (sem(n) for n in (
                "loaded", "mean_product", "centred", "squared", "var_product", "var_ready", "root_ready", "gate_product", "vector_step"))
            with nc.Block() as block:
                @block.sync
                def _(sp):
                    sp.dma_start(g2[:], dram["g2"][half]).then_inc(loaded, 16)
                    if half == 0:
                        sp.dma_start(flat_of(r), parked_rkv[:, 0:2 * TOK]).then_inc(brought, 16)
                        sp.dma_start(flat_of(v), parked_rkv[:, 4 * TOK:6 * TOK]).then_inc(brought, 16)
                        sp.wait_ge(brought, 32)
                    else:
                        sp.dma_start(flat[:, CTX_T * D:], parked[:, CTX_T * D:]).then_inc(brought, 16)
                        sp.wait_ge(brought, 16)

                @block.tensor
                def _(pe):
                    for i, (f, s) in enumerate(jobs):
                        nc.tensor.matmul(ps[i][:, 0:s.stop - s.start], head_ones[:], y[:, f, s], start=True, stop=True).then_inc(mean_mm, 1)
                    for i, (f, s) in enumerate(jobs):
                        pe.wait_ge(squared, i + 1)
                        nc.tensor.matmul(ps[4 + i][:, 0:s.stop - s.start], head_ones[:], inv[:, f, s], start=True, stop=True).then_inc(var_mm, 1)
                    pe.wait_ge(loaded, 16)
                    for i, (f, s) in enumerate(jobs):
                        nc.tensor.matmul(ps[i][:, 0:s.stop - s.start], g2[:, f * P:(f + 1) * P], lora[:, 2, s], start=True, stop=True).then_inc(gate_mm, 1)

                @block.scalar
                def _(act):
                    for i, (f, s) in enumerate(jobs):
                        act.wait_ge(centred, i + 1)
                        nc.scalar.activation(inv[:, f, s], y[:, f, s], ACT.Square).then_inc(squared, 1)
                    for i, (f, s) in enumerate(jobs):
                        act.wait_ge(var_ready, i + 1)
                        nc.scalar.activation(inv[:, f, s], inv[:, f, s], ACT.Sqrt).then_inc(root_ready, 1)

                @block.vector
                def _(dve):
                    step = Chain(dve, chained)
                    for i, (f, s) in enumerate(jobs):
                        dve.wait_ge(mean_mm, i + 1)
                        nc.vector.scalar_tensor_tensor(out=y[:, f, s], in0=ps[i][:, 0:s.stop - s.start], scalar=-1.0 / HD, in1=y[:, f, s],
                                                       op0=ALU.mult, op1=ALU.add).then_inc(centred, 1)
                    for i, (f, s) in enumerate(jobs):
                        dve.wait_ge(var_mm, i + 1)
                        nc.vector.tensor_scalar(inv[:, f, s], ps[4 + i][:, 0:s.stop - s.start], 1.0 / HD, GN_EPS, ALU.mult, ALU.add).then_inc(var_ready, 1)
                    dve.wait_ge(centred, 4)
                    for i, (f, s) in enumerate(jobs):
                        dve.wait_ge(root_ready, i + 1)
                        step(nc.vector.reciprocal(inv[:, f, s], inv[:, f, s]))
                        step(nc.vector.tensor_tensor(y[:, f, s], y[:, f, s], inv[:, f, s], ALU.mult))
                        step(nc.vector.tensor_scalar(y[:, f, s], y[:, f, s], rcols[:, R_GW + f0 + f:R_GW + f0 + f + 1],
                                                     rcols[:, R_GB + f0 + f:R_GB + f0 + f + 1], ALU.mult, ALU.add))
                        step(nc.vector.tensor_tensor(y[:, f, s], y[:, f, s], mixT[:, f0 + f, s], ALU.add))
                        dve.wait_ge(gate_mm, i + 1)
                        step(nc.vector.tensor_tensor(mixT[:, f0 + f, s], y[:, f, s], ps[i][:, 0:s.stop - s.start], ALU.mult))

    def second_block():
        for layer in range(DEPTH):
            tiles = all_tiles if layer == 0 else lat_tiles
            streams = 2 if layer == 0 else 1
            modulation2_stage(layer)
            with stage():
                bring = None
                if layer == 0:
                    mixT = sb("mixT", [P, DK, TOK])
                    even_mixer(mixT)
                    dump("rwkv", mixT[:, 0:4, :])
                    back = sem("residual_back")

                    def bring(sp):
                        sp.dma_start(flat_of(resid)[:, 0:CTX_T * D], parked[:, 0:CTX_T * D]).then_inc(back, 16)
                        sp.wait_ge(back, 16)
                else:
                    mixT = odd_mixer()
                    dump("odd", mixT[:])
                gates2_stage(layer, GATE, streams, beside=bring)
                out_product_rms_stage(f"out{layer}", lambda k: mixT[:, k:k + 2, :], tiles)
            dump(f"h{layer}", resid[:])
            ffn2_stages(layer, tiles)
            dump(f"g{layer}", resid[:])
        with stage():
            with nc.Block() as block:
                @block.sync
                def _(sp):
                    sp.dma_start(out_dram[0].rearrange("(t p) d -> p t d", p=P), resid[:, CTX_T:TOK_T, :]).then_inc(stored, 16)
                    sp.wait_ge(stored, 16)

    setup_stage()
    sgu_pool_mixer(modulate1("ada_mix0"))
    dump("x1", resid[:])
    ffn1_stages(0, modulate1("ada_ffn0"))
    dump("x2", resid[:])
    conformer_mixer(modulate1("ada_mix1"))
    dump("x3", resid[:])
    ffn1_stages(1, modulate1("ada_ffn1"))
    dump("x4", resid[:])
    second_block()


def blocks_of(w, plan):
    w = np.asarray(w)
    parts = [w[k * P:(k + nk) * P, c:c + nc].reshape(nk, P, nc).transpose(1, 0, 2).ravel() for k, nk, c, nc in plan]
    return np.ascontiguousarray(np.concatenate(parts))


def columns(v, *shape):
    v = np.asarray(v)
    return np.ascontiguousarray(v.reshape(-1, P).T)


def interleaved(w, half):
    a, b = w[..., :half], w[..., half:]
    n = half // P
    stacked = np.stack([a.reshape(*a.shape[:-1], n, P), b.reshape(*b.shape[:-1], n, P)], axis=-2)
    return stacked.reshape(*w.shape)


def shape_constants():
    same_head = np.kron(np.eye(P // HD), np.ones((HD, HD))).astype(np.float32)
    t = np.arange(SEQ)
    counts = [np.minimum(t + w // 2, SEQ) - np.maximum(t - w // 2, 0) for w in (2, 4, 8, 16)]
    return {
        "identity": np.eye(P, dtype=np.float32),
        "head_ones": same_head,
        "inv_count": (1.0 / np.stack(counts)).astype(np.float32),
    }


def lay_out_first(i):
    plans = dict(WEIGHTS)
    i = {k: np.asarray(v) for k, v in i.items()}
    out = dict(shape_constants())
    out["x"] = i["x"][0]
    out["ctx"] = i["ctx_2"][0]
    out["c1"] = columns(i["c"][0])
    out["c2"] = np.ascontiguousarray(np.stack([columns(i["c_2"][0]), columns(i["c_ctx_2"])], axis=-1))
    for l in range(DEPTH):
        out[f"bias_ada_mix{l}"], out[f"bias_ada_ffn{l}"] = columns(i["mix_ada_b"][l]), columns(i["ffn_ada_b"][l])
        out[f"bias_ada{l}"] = columns(i["b_ada_2"][l])
    w_in = i["ab_w_in"][0]
    out["ab_uv"] = blocks_of(w_in[:, :1024], plans["ab_uv"])
    out["ab_z"] = blocks_of(w_in[:, 1024:], plans["ab_z"])
    out["ab_out"] = blocks_of(i["ab_w_out"][0], plans["ab_out"])
    out["sgu_g"], out["sgu_b"] = i["ab_sgu_ln_g"][0], i["ab_sgu_ln_b"][0]
    out["wsT"] = np.ascontiguousarray(i["ab_ws"][0].transpose(2, 0, 1))
    out["bs"] = np.ascontiguousarray(i["ab_bs"][0].T)
    out["pool_w"] = np.ascontiguousarray(i["ab_pool_w"][0].transpose(1, 0, 2))
    out["pool_scale"] = columns(i["ab_pool_scale"][0])
    out["cv_in"] = blocks_of(interleaved(i["cv_w_in"][0], D), plans["cv_in"])
    out["cv_out"] = blocks_of(i["cv_w_out"][0], plans["cv_out"])
    taps = np.concatenate([i["cv_dw"][0], i["cv_dw_b"][0][None]])
    out["cv_taps"] = np.ascontiguousarray(taps.reshape(CONV_W + 1, DK, P).transpose(2, 1, 0))
    out["cv_ln"] = np.ascontiguousarray(np.stack([columns(i["cv_ln_g"][0]), columns(i["cv_ln_b"][0])], axis=1))
    ffn_taps = []
    for l in range(DEPTH):
        out[f"ada_mix{l}"] = blocks_of(i["mix_ada_w"][l], ADA1)
        out[f"ada_ffn{l}"] = blocks_of(i["ffn_ada_w"][l], ADA1)
        out[f"up{l}"] = blocks_of(interleaved(i["ffn_w_up"][l], FFN), plans[f"up{l}"])
        out[f"down{l}"] = blocks_of(i["ffn_w_down"][l], plans[f"down{l}"])
        for kind in ("mix", "ffn"):
            out[f"{kind}_ln_g{l}"], out[f"{kind}_ln_b{l}"] = i[f"{kind}_ln_g"][l], i[f"{kind}_ln_b"][l]
        taps = np.concatenate([i["ffn_dw"][l], i["ffn_dw_b"][l][None]])
        ffn_taps.append(interleaved(taps, FFN).reshape(4, 2 * FK, P).transpose(2, 1, 0))
    out["ffn_taps"] = np.ascontiguousarray(np.stack(ffn_taps))
    return out


def second_constants():
    out = {}
    t = np.arange(SEQ)
    n_freq = HD // 4
    inv_freq = 10000.0 ** (-np.arange(n_freq, dtype=np.float32) / n_freq)
    row = (t // GRID_W).astype(np.float32)[:, None] * inv_freq.astype(np.float32)
    col = (t % GRID_W).astype(np.float32)[:, None] * inv_freq.astype(np.float32)
    ang = np.concatenate([row, row, col, col], axis=-1).astype(np.float64).T
    out["rope_cos"] = np.tile(np.cos(ang), (2, 1)).astype(np.float32)
    out["rope_sin"] = np.tile(np.sin(ang), (2, 1)).astype(np.float32)
    turn = np.zeros((P, P), np.float32)
    for base in range(0, P, 2 * n_freq):
        for i in range(n_freq):
            turn[base + n_freq + i, base + i] = -1.0
            turn[base + i, base + n_freq + i] = 1.0
    out["rope_turn"] = turn
    q, k = np.arange(P)[:, None], np.arange(3 * P)[None, :]
    out["window_mask"] = np.where(np.abs(k - P - q) <= P, 0.0, NEG_INF).astype(np.float32)
    reset = np.ones((NCH, CW), np.float32)
    reset[:, 0] = 0
    out["reset"] = reset.ravel()
    i = np.arange(CH)
    earlier = (i[None, :] < i[:, None])
    both = np.stack([earlier, earlier.T])
    blocks = np.stack([np.kron(np.eye(2), m) for m in both])
    out["mask_before"] = np.ascontiguousarray(blocks.transpose(1, 0, 2)).astype(np.float32)
    out["mask_before_T"] = np.ascontiguousarray(blocks.transpose(2, 0, 1)).astype(np.float32)
    upto = both | np.eye(CH, dtype=bool)
    out["mask_upto_T"] = np.ascontiguousarray(np.tile(upto.transpose(2, 0, 1), (2, 1, 1))).astype(np.float32)
    levels = []
    for l in range(LEVELS):
        m = 1 << l
        pair = (i[:, None] // (2 * m) == i[None, :] // (2 * m))
        fwd = pair & (i[:, None] // m < i[None, :] // m)
        levels.append(np.stack([np.kron(np.eye(2), fwd), np.kron(np.eye(2), fwd.T)]))
    out["level_masks"] = np.ascontiguousarray(np.stack(levels).transpose(2, 0, 1, 3).reshape(P, -1)).astype(np.float32)
    return out


def rpb_layout(rpb):
    t = np.arange(SEQ)
    r, c = t // GRID_W, t % GRID_W
    start = np.clip(c - 8, 0, GRID_W - 16)
    ok = (c[None, :] >= start[:, None]) & (c[None, :] < start[:, None] + 16)
    dr = r[None, :] - r[:, None] + 7
    dc = np.clip(c[None, :] - c[:, None] + 15, 0, 30)
    out = rpb[:, dr, dc]
    out[:, ~ok] = NEG_INF
    return np.ascontiguousarray(out)


def lay_out(i):
    plans = dict(WEIGHTS)
    out = lay_out_first(i)
    i = {k: np.asarray(v) for k, v in i.items()}
    out.update(second_constants())
    out["gains"] = np.ascontiguousarray(np.stack([np.stack([columns(i[n][l]) for n in (
        "g_pre_mix_2", "g_post_mix_2", "g_pre_ff_2", "g_post_ff_2")], axis=1) for l in range(DEPTH)]))
    for l in range(DEPTH):
        out[f"ada{l}"] = blocks_of(i["w_ada_2"][l], ADA2)
        out[f"out{l}"] = blocks_of(i["w_out_2"][l], plans[f"out{l}"])
        out[f"ff1_{l}"] = blocks_of(i["w_ff1_2"][l], plans[f"ff1_{l}"])
        out[f"ff2_{l}"] = blocks_of(i["w_ff2_2"][l], plans[f"ff2_{l}"])
    even, odd = i["w_in_even_2"][0], i["w_in_odd_2"][0]

    def grouped(w):
        k0, k1 = w[:, 512:512 + HD], w[:, 512 + HD:512 + 2 * HD]
        return np.concatenate([w[:, :512], k0, k0, k1, k1], axis=1), w[:, 640:768]

    qk, v = grouped(even[:, 1920:])
    out["b_qk"], out["b_v"] = blocks_of(qk, plans["b_qk"]), blocks_of(v, plans["b_v"])
    qk, v = grouped(odd[:, 1536:])
    out["d_qk"], out["d_v"] = blocks_of(qk, plans["d_qk"]), blocks_of(v, plans["d_v"])
    out["c_qk"], out["c_v"] = blocks_of(odd[:, :1024], plans["c_qk"]), blocks_of(odd[:, 1024:1536], plans["c_v"])
    out["lora"] = blocks_of(even[:, 1536:1920], plans["lora"])
    for h in range(2):
        cols = [even[:, x * 512 + h * 256:x * 512 + (h + 1) * 256] for x in range(3)]
        out[f"rkv{h}"] = blocks_of(np.concatenate(cols, axis=1), plans[f"rkv{h}"])
    mu = np.stack([columns(i["a_mu_prev_2"][0]), columns(i["a_mu_next_2"][0])], axis=-1).reshape(P, 30)
    two = lambda x: np.concatenate([columns(x[0]), columns(x[1])], axis=1)
    out["r_cols"] = np.ascontiguousarray(np.concatenate([
        mu, two(i["a_w0_2"][0]), two(i["a_a0_2"][0]), columns(i["a_k_k_2"][0]), columns(i["a_k_a_2"][0]),
        columns(i["a_r_k_2"][0].reshape(-1)), columns(i["a_gn_w_2"][0]), columns(i["a_gn_b_2"][0])], axis=1))
    for name, src in (("w2", i["a_w2_2"][0]), ("a2", i["a_a2_2"][0])):
        full = np.zeros((2, P, 2, 2 * P), np.float32)
        for d in range(2):
            for h in range(2):
                full[h, d * HD:(d + 1) * HD, d] = src[d][:, h * 256:(h + 1) * 256]
        out[name] = full
    out["g2"] = np.ascontiguousarray(i["a_g2_2"][0].reshape(P, 2, 2 * P).transpose(1, 0, 2))
    out["b_sink"] = i["b_sink_2"][0]
    out["rpb_table"] = rpb_layout(i["c_rpb_2"][0])
    out["d_gain"] = np.ascontiguousarray(np.stack([np.tile(i["d_q_gain_2"][0], 2), np.tile(i["d_k_gain_2"][0], 2)], axis=1))
    return out


def kernel(**inputs):
    import concourse.bacc as bacc
    from concourse.bass_utils import run_bass_kernel_spmd

    arrays = lay_out(inputs)
    nc = bacc.Bacc("TRN2", target_bir_lowering=False, num_devices=1)
    dram = {name: nc.dram_tensor(name, a.shape, mybir.dt.from_np(a.dtype), kind="ExternalInput").ap() for name, a in arrays.items()}
    out = nc.dram_tensor("out", (1, SEQ, D), F32, kind="ExternalOutput").ap()
    build(nc, dram, out)
    got = run_bass_kernel_spmd(nc, [arrays], core_ids=[0])
    return got.results[0]["out"]
```

```python
from contextlib import contextmanager

import numpy as np

import concourse.bass as bass
from concourse import mybir

ALU = mybir.AluOpType
ACT = mybir.ActivationFunctionType
AX_X = mybir.AxisListType.X
F32 = mybir.dt.float32
F32R = mybir.dt.float32r
U8 = mybir.dt.uint8

P = 128
D = 1024
DK = D // P
SEQ, CTX = 512, 256
TOK = CTX + SEQ
LAT = slice(CTX, TOK)
CTX_T, LAT_T = CTX // P, SEQ // P
TOK_T = CTX_T + LAT_T
BANK = 512
NBANK = 8

DEPTH = 2
ALPHA = (2 * DEPTH) ** 0.25
LN_EPS = 1e-5
RMS_EPS = 1e-6
GN_EPS = 64e-5
A_HEADS = 4
FFN = ((8 * D // 3 + 127) // 128) * 128
FK = FFN // P
CONV_W = 31
PE_TAPS = [8] * 6 + [11, 18]
DFF = 4 * D
HD = 64
GRID_W = 64
NEG_INF = -1e30
ATTN_SCALE = HD ** -0.5

CH = 64
NCH = TOK // CH
CTX_CH = CTX // CH
CW = CH + 1
DECAY = float(np.exp(-0.5))
LEVELS = 6

RING = 4
BLK = 2048
PIECE = 1024
PIECES = 2
SIDE_BANK = 7
NROT = 7


def feature_plan(n_cols, k_tiles=DK, width=256):
    return [(0, k_tiles, c, min(width, n_cols - c)) for c in range(0, n_cols, width)]


def token_plan(n_cols, k_tiles):
    return [(k, min(4, k_tiles - k), c, 512) for c in range(0, n_cols, 512) for k in range(0, k_tiles, 4)]


ADA1 = feature_plan(3 * D)
ADA2 = feature_plan(6 * D)
FIRST_ADA = "ada_mix0"
MAIN = [
    ("ab_uv", token_plan(1024, DK)), ("ab_z", feature_plan(512)), ("ab_out", token_plan(D, DK)),
    ("up0", feature_plan(2 * FFN)), ("down0", token_plan(D, FK)),
    ("cv_in", feature_plan(2 * D)), ("cv_out", token_plan(D, DK)),
    ("up1", feature_plan(2 * FFN)), ("down1", token_plan(D, FK)),
    ("b_qk", feature_plan(768)), ("b_v", feature_plan(P, width=P)),
    ("lora", feature_plan(256) + [(0, DK, 256, P)]),
    ("rkv0", feature_plan(768)), ("rkv1", feature_plan(768)),
    ("out0", token_plan(D, DK)), ("ff1_0", feature_plan(DFF)), ("ff2_0", token_plan(D, DFF // P)),
    ("c_qk", feature_plan(1024)), ("c_v", token_plan(512, DK)),
    ("d_qk", feature_plan(768)), ("d_v", feature_plan(P, width=P)),
    ("out1", token_plan(D, DK)), ("ff1_1", feature_plan(DFF)), ("ff2_1", token_plan(D, DFF // P)),
]
ADAS = {"ada_mix0": ADA1, "ada_ffn0": ADA1, "ada_mix1": ADA1, "ada_ffn1": ADA1, "ada0": ADA2, "ada1": ADA2}
WEIGHTS = MAIN + list(ADAS.items())
SIDES = {
    "ab_uv": [("ada_ffn0", 0, 5)], "ab_z": [("ada_ffn0", 5, 2)], "ab_out": [("ada_ffn0", 7, 5)],
    "up0": [("ada_mix1", 0, 12), ("ada_ffn1", 0, 8)], "down0": [("ada_ffn1", 8, 4)], "up1": [("ada0", 0, 12)],
    "b_qk": [("ada0", 12, 3)], "lora": [("ada0", 15, 2)], "rkv0": [("ada0", 17, 3)], "rkv1": [("ada0", 20, 3)],
    "out0": [("ada0", 23, 1)], "ff1_0": [("ada1", 0, 12)],
    "c_qk": [("ada1", 12, 4)], "c_v": [("ada1", 16, 2)], "d_qk": [("ada1", 18, 3)], "out1": [("ada1", 21, 3)],
}


SPREAD = ["up1"]


def sides_after(host, b):
    plan = dict(MAIN)[host]
    sides = [(name, first + n) for name, first, count in SIDES.get(host, []) for n in range(count)]
    m = sum(c == 0 for _, _, c, _ in plan) if plan[0][3] == 512 else len(plan)
    return sides[b * len(sides) // m:(b + 1) * len(sides) // m]


class WeightStream:

    def __init__(self, nc, drams, vectors):
        self.nc = nc
        self.vectors = vectors
        self.side_sum = nc.alloc_sbuf_tensor("side_sum", [P, 2, 256], F32)
        self.side_step = nc.alloc_semaphore("side_sum_step")
        self.ring = nc.alloc_sbuf_tensor("weight_ring", [P, RING, BLK], F32)
        self.hi_buf = nc.alloc_sbuf_tensor("weight_hi", [P, PIECES, PIECE], F32R)
        self.lo_buf = nc.alloc_sbuf_tensor("weight_lo", [P, PIECES, PIECE], F32R)
        self.landed = [nc.alloc_semaphore(f"weight_landed{i}") for i in range(RING)]
        self.hi_made = nc.alloc_semaphore("weight_hi_made")
        self.lo_made = nc.alloc_semaphore("weight_lo_made")
        self.piece_used = nc.alloc_semaphore("weight_piece_used")
        self.side_used = nc.alloc_semaphore("side_block_used")
        self.blocks, self.pieces, self.end_of = [], [], {}
        self.free_when = []
        sides = 0
        self.sums_after, self.products_after = {}, {}
        self.matrix_of = []
        self.side_steps = []
        for name, plan in MAIN:
            at = 0
            waiting = []
            for b, (_, nk, _, width) in enumerate(plan):
                n = nk * width
                i = len(self.blocks)
                piece_before = len(self.pieces)
                self.blocks.append((drams[name][at:at + P * n].rearrange("(p n) -> p n", p=P), n, width))
                at += P * n
                if width <= 256:
                    for c in range(0, width, P):
                        self.pieces.append((i, "columns", c))
                else:
                    for k in range(0, nk, 2):
                        self.pieces.append((i, "rows", k))
                self.free_when.append((self.lo_made, len(self.pieces)))
                following = sides_after(name, b)
                for n, (matrix, side) in enumerate(following):
                    nv = vectors[matrix].shape[2]
                    self.matrix_of.append(matrix)
                    self.side_steps.append((self.side_steps or [0])[-1] + DK * nv)
                    shares = [(len(self.blocks) + n, sides + n, nv, k) for k in (0, DK // 2)]
                    waiting += [(shares[0], None), (shares[1], (matrix, side, len(self.blocks) + n, nv))]
                for piece in range(piece_before, len(self.pieces)):
                    ready = len(waiting) if piece == len(self.pieces) - 1 else len(waiting) - 2 * len(following)
                    everything = b == len(plan) - 1 and piece == len(self.pieces) - 1
                    for share, product in [waiting.pop(0) for _ in range(ready if everything else -(-ready // (2 if name in SPREAD else 1)))]:
                        self.sums_after.setdefault(piece, []).append(share)
                        if product is not None:
                            self.products_after.setdefault(piece, []).append(product)
                for matrix, side in following:
                    source = drams[matrix]
                    n = DK * 256
                    self.blocks.append((source[side * P * n:(side + 1) * P * n].rearrange("(p n) -> p n", p=P), n, 256))
                    sides += 1
                    self.free_when.append((self.side_used, sides))
            self.end_of[name] = len(self.blocks)
        self.loads = 0
        self.at = {"act": 0, "dve": 0, "pe": 0}
        self.side_blocks = [i for i, w in enumerate(self.free_when) if w[0] is self.side_used]
        self.sides, self.steps = 0, 0
        self.owed = False

    def load(self, sp, name=None):
        until = min(self.end_of.get(name, 0) + RING, len(self.blocks))
        while self.loads < until:
            i = self.loads
            if i >= RING:
                sp.wait_ge(*self.free_when[i - RING])
            source, n, _ = self.blocks[i]
            sp.dma_start(self.ring[:, i % RING, 0:n], source).then_inc(self.landed[i % RING], 16)
            self.loads += 1

    def arrived(self, engine, i):
        engine.wait_ge(self.landed[i % RING], 16 * (i // RING + 1))

    def raw_piece(self, p):
        i, kind, at = self.pieces[p]
        _, n, width = self.blocks[i]
        block = self.ring[:, i % RING, 0:n].rearrange("p (k n) -> p k n", n=width)
        raw = block[:, :, at:at + P] if kind == "columns" else block[:, at:at + 2, :]
        width = P if kind == "columns" else width
        split = [x[:, p % PIECES, 0:raw.shape[1] * width].rearrange("p (k n) -> p k n", n=width) for x in (self.hi_buf, self.lo_buf)]
        return i, raw, split

    def hi(self, act, x=None):
        p = self.at["act"]
        self.at["act"] += 1
        i, raw, (hi, _) = self.raw_piece(p)
        self.arrived(act, i)
        if p >= PIECES:
            act.wait_ge(self.piece_used, p - PIECES + 1)
        if x is not None:
            self.nc.scalar.copy(x[1], x[0])
        self.nc.scalar.copy(hi, raw).then_inc(self.hi_made, 1)

    def lo(self, dve, x=None):
        p = self.at["dve"]
        self.at["dve"] += 1
        i, raw, (hi, lo) = self.raw_piece(p)
        self.arrived(dve, i)
        dve.wait_ge(self.hi_made, p + 1)
        if x is not None:
            self.nc.vector.tensor_tensor(x[2], x[0], x[1].bitcast(F32), ALU.subtract)
        self.nc.vector.tensor_tensor(lo, raw, hi.bitcast(F32), ALU.subtract).then_inc(self.lo_made, 1)
        for part in self.sums_after.get(p, []):
            self.sum_side(dve, *part)

    def sum_place(self, i, n, v, nv):
        return self.ring[:, i % RING, 0:256] if v == nv - 1 else self.side_sum[:, n % 2, :]

    def sum_side(self, dve, i, n, nv, k0):
        vec = self.vectors[self.matrix_of[n]]
        w = self.ring[:, i % RING, :].rearrange("p (k n) -> p k n", n=256)
        self.arrived(dve, i)
        if nv == 2 and n >= 2:
            dve.wait_ge(self.side_used, n - 1)
        for k in range(k0, k0 + DK // 2):
            for v in range(nv):
                to = self.sum_place(i, n, v, nv)
                if k > 0:
                    dve.wait_ge(self.side_step, self.steps - nv + 1)
                elif v > 0:
                    dve.wait_ge(self.side_step, self.steps)
                if k == 0:
                    ins = self.nc.vector.tensor_scalar(to, w[:, k, :], vec[:, k, v:v + 1], None, ALU.mult)
                else:
                    ins = self.nc.vector.scalar_tensor_tensor(out=to, in0=w[:, k, :], scalar=vec[:, k, v:v + 1], in1=to,
                                                              op0=ALU.mult, op1=ALU.add)
                ins.then_inc(self.side_step, 1)
                self.steps += 1

    def take(self, pe):
        p = self.at["pe"]
        self.at["pe"] += 1
        pe.wait_ge(self.lo_made, p + 1)
        return self.raw_piece(p)[2]

    def used_by(self, product):
        if self.owed:
            product.then_inc(self.piece_used, 1)
            self.owed = False

    def settle(self, pe):
        if self.owed:
            pe.drain().then_inc(self.piece_used, 1)
            self.owed = False

    def take_side(self, pe):
        pe.wait_ge(self.side_step, self.side_steps[self.sides])
        self.sides += 1
        return self.sides - 1


class Chain:

    def __init__(self, engine, sem):
        self.engine, self.sem, self.n = engine, sem, 0

    def __call__(self, ins):
        ins.then_inc(self.sem, 1)
        self.n += 1
        self.engine.wait_ge(self.sem, self.n)


def build(nc, dram, out_dram, debug=None):
    ps = [nc.alloc_psum_tensor(f"bank{i}", [P, BANK], F32) for i in range(NBANK)]
    stored = nc.alloc_semaphore("output_stored")

    names = {}

    def unique(name):
        names[name] = names.get(name, 0) + 1
        return f"{name}.{names[name]}"

    def sb(name, shape, dt=F32):
        return nc.alloc_sbuf_tensor(unique(name), shape, dt)

    def sem(name):
        return nc.alloc_semaphore(unique(name))

    @contextmanager
    def stage():
        with nc.cleanup_on_exit():
            yield

    def rows(name):
        return dram[name].partition_broadcast(P)

    def dump(name, ap):
        if debug is None or name not in debug:
            return
        with stage():
            done = sem("dumped")
            with nc.Block() as block:
                @block.sync
                def _(sp):
                    sp.dma_start(debug[name], ap).then_inc(done, 16)
                    sp.wait_ge(done, 16)

    ident = sb("identity", [P, P])
    ones = sb("ones", [P, P])
    head_ones = sb("head_ones", [P, P])
    silu_c1 = sb("silu_c1", [P, DK, 1])
    silu_c2 = sb("silu_c2", [P, DK, 2])
    weights = WeightStream(nc, dram, {name: silu_c1 if plan is ADA1 else silu_c2 for name, plan in ADAS.items()})
    mods = {name: sb(f"modulation_{name}", [P, len(plan) * 2, 1 if plan is ADA1 else 2]) for name, plan in ADAS.items()}
    ada_bias = {name: mods[name][:, :, 0] if plan is ADA1 else sb(f"bias_{name}", [P, len(plan) * 2])[:] for name, plan in ADAS.items()}
    gains = sb("gains", [P, 4, DK])
    resid = sb("residual", [P, TOK_T, D])
    gate_rows = sb("gate_rows", [P, 2, D])

    def three_products(out, w_hi, w_lo, x_hi, x_lo, first, last):
        nc.tensor.matmul(out, w_hi, x_hi, start=first, stop=False)
        nc.tensor.matmul(out, w_hi, x_lo, start=False, stop=False)
        return nc.tensor.matmul(out, w_lo, x_hi, start=False, stop=last)

    def side_products(pe):
        for name, side, i, nv in weights.products_after.get(weights.at["pe"] - 1, []):
            n = weights.take_side(pe)
            for j in range(2):
                for v in range(nv):
                    col = side_base[name] + (2 * side + j) * nv + v
                    last = nc.tensor.matmul(ps[SIDE_BANK][:, col:col + 1], weights.sum_place(i, n, v, nv)[:, j * P:(j + 1) * P],
                                            ones[:, 0:1], start=True, stop=True)
                    weights.used_by(last)
            last.then_inc(weights.side_used, 1)

    def side_sums(dve, *hosts):
        hosts = [h for h in hosts if h in SIDES]
        if not hosts:
            return
        dve.wait_ge(weights.side_used, max(sides_until[h] for h in hosts))
        for name, first, count in [x for h in hosts for x in SIDES[h]]:
            mod = mods[name]
            nv = mod.shape[2]
            at = side_base[name]
            got = ps[SIDE_BANK][:, at + 2 * first * nv:at + 2 * (first + count) * nv].rearrange("p (c v) -> p c v", v=nv)
            for v in range(nv):
                nc.vector.tensor_tensor(mod[:, 2 * first:2 * (first + count), v], got[:, :, v],
                                        ada_bias[name][:, 2 * first:2 * (first + count)], ALU.add)

    side_base, base = {}, 0
    for name, plan in ADAS.items():
        side_base[name] = base
        base += 2 * len(plan) * mods[name].shape[2]

    sides_until, total = {}, 0
    for host, _ in MAIN:
        if host in SIDES:
            total += sum(count for _, _, count in SIDES[host])
            sides_until[host] = total

    def feature_products(pe, host, hT, segments, evacuated, g0=0, after_piece=None):
        g = g0
        piece = 0
        for b, (_, _, _, width) in enumerate(dict(MAIN)[host]):
            for _ in range(width // P):
                hi, lo = weights.take(pe)
                for seg in segments(piece) if callable(segments) else segments:
                    if g >= NROT:
                        pe.wait_ge(evacuated, g - NROT + 1)
                    for k in range(DK):
                        last = three_products(ps[g % NROT][:, 0:seg.stop - seg.start], hi[:, k, :], lo[:, k, :],
                                              hT[0][:, k, seg], hT[1][:, k, seg], k == 0, k == DK - 1)
                    g += 1
                last.then_inc(weights.piece_used, 1)
                side_products(pe)
                if after_piece is not None:
                    after_piece(piece)
                piece += 1
        return g

    def token_products(pe, host, tiles, x, mm_done, evacuated, g0=0):
        plan = dict(MAIN)[host]
        k_tiles = max(k + nk for k, nk, _, _ in plan)
        T = len(tiles)
        p = 0
        for b, (k0, nk, c0, _) in enumerate(plan):
            n = c0 // BANK
            for at in range(0, nk, 2):
                hi, lo = weights.take(pe)
                done = k0 + at + 2 == k_tiles
                for i in range(T):
                    g = g0 + n * T + i
                    if k0 + at == 0 and g >= NROT:
                        pe.wait_ge(evacuated, g - NROT + 1)
                    for kk in range(2):
                        k = k0 + at + kk
                        xh, xl = x(p, kk, i)
                        out = ps[g % NROT][:, :]
                        one = nc.tensor.matmul(out, xh, hi[:, kk, :], start=(k == 0), stop=False)
                        weights.used_by(one)
                        nc.tensor.matmul(out, xl, hi[:, kk, :], start=False, stop=False)
                        last = nc.tensor.matmul(out, xh, lo[:, kk, :], start=False, stop=(k == k_tiles - 1))
                    if done:
                        last.then_inc(mm_done, 1)
                if done:
                    weights.owed = True
                else:
                    last.then_inc(weights.piece_used, 1)
                side_products(pe)
                p += 1
        weights.settle(pe)
        return g0 + (n + 1) * T

    class LeftOperand:

        def __init__(self, host, source, n_tok):
            self.source = source
            self.plan = [(k0 + at) for k0, nk, _, _ in dict(MAIN)[host] for at in range(0, nk, 2)]
            self.hi = sb("left_hi", [P, PIECES, 2, n_tok], F32R)
            self.lo = sb("left_lo", [P, PIECES, 2, n_tok], F32R)
            self.first = weights.at["pe"]

        def share(self, p):
            k = self.plan[p]
            slot = (self.first + p) % PIECES
            return self.source(k), self.hi[:, slot], self.lo[:, slot]

        def __call__(self, p, kk, i):
            slot = (self.first + p) % PIECES
            cols = slice(i * P, (i + 1) * P)
            return self.hi[:, slot, kk, cols], self.lo[:, slot, kk, cols]

    def setup_stage():
        with stage():
            plan = ADAS[FIRST_ADA]
            blocks = sb("first_blocks", [P, len(plan), BLK])
            loaded, made, silu_done = sem("loaded"), sem("memset"), sem("silu_done")
            block_landed = [sem(f"block_landed{i}") for i in range(len(plan))]
            mm_done, x_loaded, ones_made, summed = sem("mm_done"), sem("x_loaded"), sem("ones_made"), sem("block_summed")
            small = [(silu_c1[:, :, 0], dram["c1"]), (silu_c2[:], dram["c2"]), (ident[:], dram["identity"]), (head_ones[:], dram["head_ones"])]
            small += [(ada_bias[name], dram["bias_" + name]) for name in ADAS]
            with nc.Block() as block:
                @block.sync
                def _(sp):
                    for dst, src in small:
                        sp.dma_start(dst, src).then_inc(loaded, 16)
                    n = DK * 256
                    for i in range(len(plan)):
                        sp.dma_start(blocks[:, i, :], dram[FIRST_ADA][i * P * n:(i + 1) * P * n].rearrange("(p n) -> p n", p=P)).then_inc(block_landed[i], 16)
                    sp.dma_start(resid[:, CTX_T:TOK_T, :], dram["x"].rearrange("(t p) d -> p t d", p=P)).then_inc(x_loaded, 16)
                    sp.dma_start(resid[:, 0:CTX_T, :], dram["ctx"].rearrange("(t p) d -> p t d", p=P)).then_inc(x_loaded, 16)
                    weights.load(sp)
                    sp.wait_ge(loaded, len(small) * 16)
                    sp.wait_ge(x_loaded, 32)

                @block.scalar
                def _(act):
                    act.wait_ge(loaded, len(small) * 16)
                    nc.scalar.activation(silu_c1[:, :, 0], silu_c1[:, :, 0], ACT.Silu).then_inc(silu_done, 1)
                    nc.scalar.activation(silu_c2[:], silu_c2[:], ACT.Silu).then_inc(silu_done, 1)

                @block.tensor
                def _(pe):
                    pe.wait_ge(ones_made, 1)
                    for i in range(len(plan)):
                        pe.wait_ge(summed, DK * (i + 1))
                        for j in range(2):
                            for h in range(2):
                                last = nc.tensor.matmul(ps[SIDE_BANK][:, 2 * i + j:2 * i + j + 1], blocks[:, i, h * 256 + j * P:h * 256 + (j + 1) * P],
                                                        ones[:, 0:1], start=(h == 0), stop=(h == 1))
                    last.then_inc(mm_done, 1)

                @block.vector
                def _(dve):
                    nc.vector.memset(ones[:], 1.0).then_inc(ones_made, 1)
                    dve.wait_ge(silu_done, 2)
                    for i in range(len(plan)):
                        dve.wait_ge(block_landed[i], 16)
                        w = blocks[:, i, :].rearrange("p (k n) -> p k n", n=256)
                        for k in range(DK):
                            if k < 2:
                                ins = nc.vector.tensor_scalar(w[:, k, :], w[:, k, :], silu_c1[:, k, :], None, ALU.mult)
                            else:
                                dve.wait_ge(summed, DK * i + k - 1)
                                ins = nc.vector.scalar_tensor_tensor(out=w[:, k % 2, :], in0=w[:, k, :], scalar=silu_c1[:, k, :], in1=w[:, k % 2, :],
                                                                     op0=ALU.mult, op1=ALU.add)
                            ins.then_inc(summed, 1)
                    dve.wait_ge(mm_done, 1)
                    n = 2 * len(plan)
                    nc.vector.tensor_tensor(mods[FIRST_ADA][:, :, 0], ps[SIDE_BANK][:, 0:n], ada_bias[FIRST_ADA], ALU.add)

    def gate_row_stage(sources, beside=None):
        with stage():
            diag = sb("gate_diagonals", [P, DK, P])
            filled, mm_done, evac = sem("diagonals"), sem("mm_done"), sem("row_copied")
            with nc.Block() as block:
                if beside is not None:
                    block.sync(beside)

                @block.vector
                def _(dve):
                    for i, (r, cols) in enumerate(sources):
                        if i:
                            dve.wait_ge(mm_done, 2 * i)
                        nc.vector.tensor_tensor(diag[:], ident[:].unsqueeze(1).broadcast_to([P, DK, P]),
                                                cols.unsqueeze(2).broadcast_to([P, DK, P]), ALU.mult).then_inc(filled, 1)

                @block.tensor
                def _(pe):
                    for i in range(len(sources)):
                        pe.wait_ge(filled, i + 1)
                        for n in range(2):
                            nc.tensor.matmul(ps[2 * i + n][:], ones[:], diag[:, 4 * n:4 * n + 4, :].rearrange("p f n -> p (f n)"),
                                             start=True, stop=True).then_inc(mm_done, 1)

                @block.scalar
                def _(act):
                    for i, (r, cols) in enumerate(sources):
                        for n in range(2):
                            act.wait_ge(mm_done, 2 * i + n + 1)
                            nc.scalar.copy(gate_rows[:, r, n * BANK:(n + 1) * BANK], ps[2 * i + n][:]).then_inc(evac, 1)

    def to_features_stage(src, tiles, scale, shift, hT, t_base=0, rms=None, beside=None):
        segs = [(0, [t for t in tiles if t >= CTX_T]), (1, [t for t in tiles if t < CTX_T])]
        segs = [(v, ts) for v, ts in segs if ts]
        groups = [(f, v, ts) for f in range(DK) for v, ts in segs]
        with stage():
            mm_done, evac, chained = sem("mm_done"), sem("evacuated"), sem("vector_step")
            squared, normed, hi_made, lo_made = sem("squared"), sem("normed"), sem("hi_made"), sem("lo_made")
            act_chained, normed_act = sem("scalar_step"), sem("normed_by_scalar")
            if rms:
                scratch, hn, exact = rms
                stats = sb("sum_of_squares", [P, TOK_T])
                root = sb("root", [P, TOK_T])
            else:
                exact = sb("exact", [P, 4, BANK])
            x = hn if rms else src

            def place(g):
                f, v, ts = groups[g]
                cols = slice((ts[0] - t_base) * P, (ts[-1] + 1 - t_base) * P)
                return exact[:, g % 4, 0:len(ts) * P], hT[0][:, f, cols], hT[1][:, f, cols]

            with nc.Block() as block:
                if beside is not None:
                    block.sync(beside)

                @block.scalar
                def _(act):
                    if rms:
                        step = Chain(act, act_chained)
                        for t in tiles:
                            step(nc.scalar.activation(scratch[:], src[:, t, :], ACT.Square, accum_out=stats[:, t:t + 1]))
                        act.sem_inc(squared, 1)
                        act.wait_ge(squared, 2)
                        nc.scalar.activation(root[:, tiles[0]:tiles[-1] + 1], stats[:, tiles[0]:tiles[-1] + 1], ACT.Sqrt).then_inc(squared, 1)
                        act.wait_ge(chained, 1)
                        for t in tiles[1::2]:
                            nc.scalar.mul(hn[:, t, :], src[:, t, :], root[:, t:t + 1]).then_inc(normed_act, 1)
                    for g in range(len(groups)):
                        x32, hi, _ = place(g)
                        act.wait_ge(evac, g + 1)
                        nc.scalar.copy(hi, x32).then_inc(hi_made, 1)

                @block.vector
                def _(dve):
                    step = Chain(dve, chained)
                    if rms:
                        t0, t1 = tiles[0], tiles[-1] + 1
                        dve.wait_ge(squared, 1)
                        nc.vector.tensor_scalar(stats[:, t0:t1], stats[:, t0:t1], 1.0 / D, RMS_EPS, ALU.mult, ALU.add).then_inc(squared, 1)
                        dve.wait_ge(squared, 3)
                        step(nc.vector.reciprocal(root[:, t0:t1], root[:, t0:t1]))
                        for t in tiles[::2]:
                            nc.vector.tensor_scalar(hn[:, t, :], src[:, t, :], root[:, t:t + 1], None, ALU.mult).then_inc(normed, 1)
                    for g in range(len(groups) + 2):
                        if g < len(groups):
                            f, v, ts = groups[g]
                            dve.wait_ge(mm_done, g + 1)
                            if g >= 4:
                                dve.wait_ge(lo_made, g - 3)
                            nc.vector.tensor_scalar(place(g)[0], ps[g % NBANK][:, 0:len(ts) * P],
                                                    scale(f, v), shift(f, v), ALU.mult, ALU.add).then_inc(evac, 1)
                        if g >= 2:
                            x32, hi, lo = place(g - 2)
                            dve.wait_ge(hi_made, g - 1)
                            nc.vector.tensor_tensor(lo, x32, hi.bitcast(F32), ALU.subtract).then_inc(lo_made, 1)

                @block.tensor
                def _(pe):
                    if rms:
                        pe.wait_ge(normed, len(tiles[::2]))
                        pe.wait_ge(normed_act, len(tiles[1::2]))
                    for g, (f, v, ts) in enumerate(groups):
                        if g >= NBANK:
                            pe.wait_ge(evac, g - NBANK + 1)
                        for i, t in enumerate(ts):
                            last = nc.tensor.transpose(ps[g % NBANK][:, i * P:(i + 1) * P], x[:, t, f * P:(f + 1) * P], ident[:])
                        last.then_inc(mm_done, 1)

    def out_product_ln_stage(name, source, g_row, b_row):
        tiles = list(range(CTX_T, TOK_T))
        T = len(tiles)
        n_pieces = sum(nk // 2 for _, nk, _, _ in dict(MAIN)[name])
        with stage():
            left = LeftOperand(name, source, SEQ)
            lng, lnb = sb("ln_gain", [P, D]), sb("ln_bias", [P, D])
            gated = sb("gated", [P, 2, BANK])
            stats = sb("bn_stats", [P, T, 2, 6])
            mv = sb("mean_var", [P, T, 2])
            inv = sb("inv_std", [P, T])
            nmean = sb("minus_mean_over_std", [P, T])
            loaded, mm_done, evac = sem("loaded"), sem("mm_done"), sem("evacuated")
            chained, var_ready, root_ready = sem("vector_step"), sem("var_ready"), sem("root_ready")
            inv_ready, centred = sem("inv_ready"), sem("centred")
            scaled, biased = sem("scaled"), sem("biased")
            with nc.Block() as block:
                @block.sync
                def _(sp):
                    sp.dma_start(lng[:], rows(g_row)).then_inc(loaded, 16)
                    sp.dma_start(lnb[:], rows(b_row)).then_inc(loaded, 16)
                    weights.load(sp, name)

                @block.tensor
                def _(pe):
                    token_products(pe, name, tiles, left, mm_done, evac)

                @block.vector
                def _(dve):
                    step = Chain(dve, chained)
                    for p in range(n_pieces // 2 + 1):
                        weights.lo(dve, left.share(p))
                    p += 1
                    for n in range(2):
                        cols = slice(n * BANK, (n + 1) * BANK)
                        for i, t in enumerate(tiles):
                            if n == 0 and p < n_pieces:
                                weights.lo(dve, left.share(p))
                                p += 1
                            if n == 1 and i == 0:
                                while p < n_pieces:
                                    weights.lo(dve, left.share(p))
                                    p += 1
                            g = n * T + i
                            dve.wait_ge(mm_done, g + 1)
                            ins = nc.vector.tensor_tensor(gated[:, g % 2, :], ps[g % NROT][:], gate_rows[:, 0, cols], ALU.mult)
                            ins.then_inc(evac, 1)
                            dve.wait_ge(evac, g + 1)
                            step(nc.vector.scalar_tensor_tensor(out=resid[:, t, cols], in0=resid[:, t, cols], scalar=ALPHA,
                                                                in1=gated[:, g % 2, :], op0=ALU.mult, op1=ALU.add))
                            step(nc.vector.bn_stats(stats[:, i, n, :], resid[:, t, cols]))
                            if n == 1:
                                step(nc.vector.bn_aggr(mv[:, i, :], stats[:, i, :, :].rearrange("p a b -> p (a b)")))
                                nc.vector.tensor_scalar(inv[:, i:i + 1], mv[:, i, 1:2], LN_EPS, None, ALU.add).then_inc(var_ready, 1)
                    for i, t in enumerate(tiles):
                        dve.wait_ge(root_ready, i + 1)
                        step(nc.vector.reciprocal(inv[:, i:i + 1], inv[:, i:i + 1]))
                        nc.vector.scalar_tensor_tensor(out=nmean[:, i:i + 1], in0=mv[:, i, 0:1], scalar=-1.0,
                                                       in1=inv[:, i:i + 1], op0=ALU.mult, op1=ALU.mult).then_inc(inv_ready, 1)
                    dve.wait_ge(loaded, 32)
                    for i, t in enumerate(tiles):
                        dve.wait_ge(centred, i + 1)
                        nc.vector.tensor_tensor(resid[:, t, :], resid[:, t, :], lng[:], ALU.mult).then_inc(scaled, 1)
                        if i % 2:
                            dve.wait_ge(scaled, i + 1)
                            nc.vector.tensor_tensor(resid[:, t, :], resid[:, t, :], lnb[:], ALU.add)
                    side_sums(dve, name)

                @block.scalar
                def _(act):
                    for p in range(n_pieces):
                        weights.hi(act, left.share(p))
                    for i in range(T):
                        act.wait_ge(var_ready, i + 1)
                        nc.scalar.activation(inv[:, i:i + 1], inv[:, i:i + 1], ACT.Sqrt).then_inc(root_ready, 1)
                    for i, t in enumerate(tiles):
                        act.wait_ge(inv_ready, i + 1)
                        nc.scalar.activation(resid[:, t, :], resid[:, t, :], ACT.Identity, bias=nmean[:, i:i + 1],
                                             scale=inv[:, i:i + 1]).then_inc(centred, 1)

                @block.gpsimd
                def _(pool):
                    pool.wait_ge(loaded, 32)
                    for i, t in enumerate(tiles[::2]):
                        pool.wait_ge(scaled, 2 * i + 1)
                        nc.gpsimd.tensor_tensor(resid[:, t, :], resid[:, t, :], lnb[:], ALU.add).then_inc(biased, 1)

    def ffn1_stages(layer, make_hT):
        with stage():
            act_T = sb("ffn_hidden", [P, FK, SEQ])
            with stage():
                hT = make_hT()
                with stage():
                    up = f"up{layer}"
                    taps = sb("ffn_taps", [P, 2 * FK, 4])
                    conv = sb("ffn_conv", [P, 4, SEQ])
                    gel = sb("ffn_gelu", [P, 2, SEQ])
                    loaded, centre, chained = sem("loaded"), sem("centre_tap"), sem("vector_step")
                    conv_done, gelu_done, multiplied = sem("conv_done"), sem("gelu_done"), sem("multiplied")
                    first, G = weights.at["pe"], 2 * FK
                    with nc.Block() as block:
                        @block.sync
                        def _(sp):
                            sp.dma_start(taps[:], dram["ffn_taps"][layer]).then_inc(loaded, 16)
                            weights.load(sp, up)

                        @block.tensor
                        def _(pe):
                            feature_products(pe, up, hT, [slice(0, SEQ)], conv_done)

                        @block.scalar
                        def _(act):
                            act.wait_ge(loaded, 16)
                            weights.hi(act)
                            for g in range(G):
                                if g + 1 < G:
                                    weights.hi(act)
                                act.wait_ge(weights.piece_used, first + g + 1)
                                if g >= 4:
                                    act.wait_ge(multiplied, g // 2 - 1)
                                nc.scalar.activation(conv[:, g % 4, :], ps[g % NROT][:], ACT.Identity,
                                                     bias=taps[:, g, 3:4], scale=taps[:, g, 1:2]).then_inc(centre, 1)
                                if g % 2:
                                    act.wait_ge(conv_done, g)
                                    nc.scalar.activation(gel[:, g // 2 % 2, :], conv[:, (g - 1) % 4, :], ACT.Gelu_apprx_tanh).then_inc(gelu_done, 1)

                        @block.vector
                        def _(dve):
                            step = Chain(dve, chained)
                            weights.lo(dve)
                            for g in range(G):
                                if g + 1 < G:
                                    weights.lo(dve)
                                c, z = conv[:, g % 4, :], ps[g % NROT]
                                dve.wait_ge(centre, g + 1)
                                step(nc.vector.scalar_tensor_tensor(out=c[:, 1:], in0=z[:, 0:SEQ - 1], scalar=taps[:, g, 0:1],
                                                                    in1=c[:, 1:], op0=ALU.mult, op1=ALU.add))
                                nc.vector.scalar_tensor_tensor(out=c[:, 0:SEQ - 1], in0=z[:, 1:SEQ], scalar=taps[:, g, 2:3],
                                                               in1=c[:, 0:SEQ - 1], op0=ALU.mult, op1=ALU.add).then_inc(conv_done, 1)
                                if g % 2:
                                    dve.wait_ge(gelu_done, g // 2 + 1)
                                    dve.wait_ge(conv_done, g + 1)
                                    nc.vector.tensor_tensor(act_T[:, g // 2, :], gel[:, g // 2 % 2, :], c, ALU.mult).then_inc(multiplied, 1)
                            side_sums(dve, up)
            out_product_ln_stage(f"down{layer}", lambda k: act_T[:, k:k + 2, :], f"ffn_ln_g{layer}", f"ffn_ln_b{layer}")

    lat_tiles = list(range(CTX_T, TOK_T))

    def hT_pair(n_tok):
        return sb("hT_hi", [P, DK, n_tok], F32R), sb("hT_lo", [P, DK, n_tok], F32R)

    def modulate1(name):
        mod = mods[name]
        with stage():
            with nc.Block() as block:
                @block.vector
                def _(dve):
                    nc.vector.tensor_scalar(mod[:, DK:3 * DK, :], mod[:, DK:3 * DK, :], 1.0, None, ALU.add)
        gate_row_stage([(0, mod[:, 2 * DK:3 * DK, 0])])

        def make_hT():
            hT = hT_pair(SEQ)
            to_features_stage(resid, lat_tiles, lambda f, v: mod[:, DK + f, :], lambda f, v: mod[:, f, :], hT, t_base=CTX_T)
            return hT
        return make_hT

    def sgu_pool_mixer(make_hT):
        with stage():
            u = sb("u", [P, LAT_T, 512])
            v = sb("v", [P, LAT_T, 512])
            PAD = 16
            ZW = SEQ + 2 * PAD
            z = sb("z_padded", [P, 4, ZW])
            mixT = sb("mixT", [P, DK, SEQ])
            with stage():
                hT = make_hT()
                lng, lnb = sb("sgu_gain", [P, 512]), sb("sgu_bias", [P, 512])
                stats = sb("bn_stats", [P, LAT_T, 6])
                mv = sb("mean_var", [P, LAT_T, 2])
                inv = sb("inv_std", [P, LAT_T])
                loaded, mm_done, evac = sem("loaded"), sem("mm_done"), sem("evacuated")
                chained, var_ready, root_ready, zeroed = sem("vector_step"), sem("var_ready"), sem("root_ready"), sem("zeroed")
                with nc.Block() as block:
                    @block.sync
                    def _(sp):
                        sp.dma_start(lng[:], rows("sgu_g")).then_inc(loaded, 16)
                        sp.dma_start(lnb[:], rows("sgu_b")).then_inc(loaded, 16)
                        weights.load(sp, "ab_z")

                    whole = slice(0, SEQ)
                    uv_first = weights.at["pe"]
                    uv_pieces, z_pieces = 2 * DK // 2, 4
                    k_of = lambda p, kk: 2 * (p % (DK // 2)) + kk

                    @block.tensor
                    def _(pe):
                        g = token_products(pe, "ab_uv", lat_tiles, lambda p, kk, i: tuple(
                            h[:, k_of(p, kk), i * P:(i + 1) * P] for h in hT), mm_done, evac)
                        feature_products(pe, "ab_z", hT, [whole], evac, g0=g)

                    @block.gpsimd
                    def _(pool):
                        nc.gpsimd.memset(z[:, :, 0:PAD], 0.0).then_inc(zeroed, 1)
                        nc.gpsimd.memset(z[:, :, PAD + SEQ:ZW], 0.0).then_inc(zeroed, 1)

                    @block.scalar
                    def _(act):
                        for p in range(uv_pieces // 2 + 2):
                            weights.hi(act)
                        for g in range(12):
                            if g < 8:
                                act.wait_ge(mm_done, g + 1)
                                to = (u if g < 4 else v)[:, g % 4, :]
                                nc.scalar.activation(to, ps[g % NROT][:], ACT.Gelu_apprx_tanh).then_inc(evac, 1)
                            else:
                                act.wait_ge(weights.piece_used, uv_first + uv_pieces + g - 8 + 1)
                                nc.scalar.copy(z[:, g - 8, PAD:PAD + SEQ], ps[g % NROT][:]).then_inc(evac, 1)
                            if g == 3:
                                for p in range(uv_pieces // 2 - 2 + 2):
                                    weights.hi(act)
                            if g in (8, 9):
                                weights.hi(act)
                        act.wait_ge(var_ready, 1)
                        nc.scalar.activation(inv[:], inv[:], ACT.Sqrt).then_inc(root_ready, 1)

                    @block.vector
                    def _(dve):
                        step = Chain(dve, chained)
                        for p in range(uv_pieces + z_pieces):
                            weights.lo(dve)
                        for t in range(LAT_T):
                            dve.wait_ge(evac, 4 + t + 1)
                            step(nc.vector.bn_stats(stats[:, t, :], v[:, t, :]))
                            step(nc.vector.bn_aggr(mv[:, t, :], stats[:, t, :]))
                        nc.vector.tensor_scalar(inv[:], mv[:, :, 1], LN_EPS, None, ALU.add).then_inc(var_ready, 1)
                        dve.wait_ge(root_ready, 1)
                        step(nc.vector.reciprocal(inv[:], inv[:]))
                        dve.wait_ge(loaded, 32)
                        for t in range(LAT_T):
                            step(nc.vector.tensor_scalar(v[:, t, :], v[:, t, :], mv[:, t, 0:1], inv[:, t:t + 1], ALU.subtract, ALU.mult))
                            step(nc.vector.tensor_tensor(v[:, t, :], v[:, t, :], lng[:], ALU.mult))
                            step(nc.vector.tensor_tensor(v[:, t, :], v[:, t, :], lnb[:], ALU.add))
                        side_sums(dve, "ab_uv", "ab_z")
            with stage():
                wsT = sb("ws_transposed", [P, A_HEADS, P])
                bs = sb("spatial_bias", [P, A_HEADS])
                pool_w = sb("pool_w", [P, 4, P])
                pool_scale = sb("pool_scale", [P, 4])
                inv_count = sb("inv_count", [P, 4, SEQ])
                pooled = sb("pooled", [P, 4, SEQ])
                sums = sb("window_sums", [P, 2, ZW])
                loaded, mixed, gated, turned, copied = sem("loaded"), sem("mixed"), sem("gated"), sem("turned"), sem("copied")
                chained, pool_done, pool_mm = sem("vector_step"), sem("pooled"), sem("pool_product")
                n_loads = 5
                with nc.Block() as block:
                    @block.sync
                    def _(sp):
                        for dst, name in ((wsT, "wsT"), (bs, "bs"), (pool_w, "pool_w"), (pool_scale, "pool_scale")):
                            sp.dma_start(dst[:], dram[name]).then_inc(loaded, 16)
                        sp.dma_start(inv_count[:], dram["inv_count"].partition_broadcast(P)).then_inc(loaded, 16)

                    @block.tensor
                    def _(pe):
                        pe.wait_ge(loaded, 16 * n_loads)
                        for t in range(LAT_T):
                            for h in range(A_HEADS):
                                last = nc.tensor.matmul(ps[t][:, h * P:(h + 1) * P], wsT[:, h, :], v[:, t, h * P:(h + 1) * P],
                                                        start=True, stop=True)
                            last.then_inc(mixed, 1)
                        pe.wait_ge(gated, LAT_T)
                        for f in range(A_HEADS):
                            for t in range(LAT_T):
                                last = nc.tensor.transpose(ps[4 + f][:, t * P:(t + 1) * P], u[:, t, f * P:(f + 1) * P], ident[:])
                            last.then_inc(turned, 1)
                        for g in range(4):
                            pe.wait_ge(pool_done, g + 1)
                            nc.tensor.matmul(ps[g][:], pool_w[:, g, :], pooled[:, g, :], start=True, stop=True).then_inc(pool_mm, 1)

                    @block.vector
                    def _(dve):
                        step = Chain(dve, chained)
                        dve.wait_ge(loaded, 16 * n_loads)
                        for t in range(LAT_T):
                            dve.wait_ge(mixed, t + 1)
                            for h in range(A_HEADS):
                                cols = slice(h * P, (h + 1) * P)
                                last = nc.vector.scalar_tensor_tensor(out=u[:, t, cols], in0=ps[t][:, cols], scalar=bs[:, h:h + 1],
                                                                      in1=u[:, t, cols], op0=ALU.add, op1=ALU.mult)
                            last.then_inc(gated, 1)
                        for g in range(4):
                            window = 2 << g
                            src = z[:, g, :]
                            for level in range(g + 1):
                                lo, off = (2 << level) - 1, 1 << level
                                dst = sums[:, level % 2, :]
                                step(nc.vector.tensor_tensor(dst[:, lo:ZW], src[:, lo:ZW], src[:, lo - off:ZW - off], ALU.add))
                                src = dst
                            at = PAD + window // 2 - 1
                            step(nc.vector.tensor_tensor(pooled[:, g, :], src[:, at:at + SEQ], inv_count[:, g, :], ALU.mult))
                            ins = nc.vector.tensor_tensor(pooled[:, g, :], pooled[:, g, :], z[:, g, PAD:PAD + SEQ], ALU.subtract)
                            ins.then_inc(pool_done, 1)
                            dve.wait_ge(pool_done, g + 1)

                    @block.scalar
                    def _(act):
                        act.wait_ge(loaded, 16 * n_loads)
                        for f in range(A_HEADS):
                            act.wait_ge(turned, f + 1)
                            nc.scalar.copy(mixT[:, f, :], ps[4 + f][:]).then_inc(copied, 1)
                        for g in range(4):
                            act.wait_ge(pool_mm, g + 1)
                            nc.scalar.mul(mixT[:, 4 + g, :], ps[g][:], pool_scale[:, g:g + 1]).then_inc(copied, 1)
            dump("mixT", mixT[:])
            out_product_ln_stage("ab_out", lambda k: mixT[:, k:k + 2, :], "mix_ln_g0", "mix_ln_b0")

    def conformer_mixer(make_hT):
        HALF = CONV_W // 2
        with stage():
            zc = sb("conv_out", [P, DK, SEQ])
            with stage():
                hT = make_hT()
                zp = sb("glu_padded", [P, DK, SEQ + 2 * HALF])
                taps = sb("conv_taps", [P, DK, CONV_W + 1])
                gate = sb("sigmoid_gate", [P, 2, SEQ])
                second = sb("second_sum", [P, SEQ])
                tapped, tap_steps = sem("tap_added"), [0]
                diag = sb("tap_diagonals", [P, 2, max(PE_TAPS), P])
                loaded, zeroed, mm_done, evac = sem("loaded"), sem("zeroed"), sem("mm_done"), sem("evacuated")
                gated, chained, diag_made = sem("gate_done"), sem("vector_step"), sem("diagonals_made")
                taps_mm, started = sem("tap_products"), sem("conv_started")
                first = weights.at["pe"]
                with nc.Block() as block:
                    @block.sync
                    def _(sp):
                        sp.dma_start(taps[:], dram["cv_taps"]).then_inc(loaded, 16)
                        weights.load(sp, "cv_in")

                    @block.gpsimd
                    def _(pool):
                        nc.gpsimd.memset(zp[:, :, 0:HALF], 0.0).then_inc(zeroed, 1)
                        nc.gpsimd.memset(zp[:, :, HALF + SEQ:], 0.0).then_inc(zeroed, 1)

                    @block.tensor
                    def _(pe):
                        def tap_products(j):
                            pe.wait_ge(diag_made, j + 1)
                            pe.wait_ge(evac, 2 * (j + 1))
                            if j >= 1:
                                pe.wait_ge(started, j)
                            for i in range(PE_TAPS[j]):
                                last = nc.tensor.matmul(ps[SIDE_BANK][:], diag[:, j % 2, i, :], zp[:, j, i:i + SEQ],
                                                        start=(i == 0), stop=(i == PE_TAPS[j] - 1))
                            last.then_inc(taps_mm, 1)

                        def after_piece(piece):
                            if piece % 2 and piece > 1:
                                tap_products(piece // 2 - 1)
                        feature_products(pe, "cv_in", hT, [slice(0, SEQ)], evac, after_piece=after_piece)
                        tap_products(DK - 1)

                    @block.scalar
                    def _(act):
                        def conv_start(j):
                            act.wait_ge(taps_mm, j + 1)
                            nc.scalar.activation(zc[:, j, :], ps[SIDE_BANK][:], ACT.Identity, bias=taps[:, j, CONV_W:CONV_W + 1]).then_inc(started, 1)

                        weights.hi(act)
                        weights.hi(act)
                        act.wait_ge(loaded, 16)
                        for j in range(DK):
                            if j + 1 < DK:
                                weights.hi(act)
                                weights.hi(act)
                            act.wait_ge(weights.piece_used, first + 2 * j + 2)
                            if j >= 2:
                                act.wait_ge(evac, 2 * (j - 1))
                            nc.scalar.activation(gate[:, j % 2, :], ps[(2 * j + 1) % NROT][:], ACT.Sigmoid).then_inc(gated, 1)
                            if j >= 2:
                                act.wait_ge(taps_mm, j - 1)
                            for i in range(PE_TAPS[j]):
                                last = nc.scalar.mul(diag[:, j % 2, i, :], ident[:], taps[:, j, i:i + 1])
                            last.then_inc(diag_made, 1)
                            if j >= 1:
                                conv_start(j - 1)
                        conv_start(DK - 1)

                    @block.vector
                    def _(dve):
                        step = Chain(dve, chained)

                        def conv(j):
                            for i in range(PE_TAPS[j], CONV_W):
                                n = i - PE_TAPS[j]
                                x, w, to = zp[:, j, i:i + SEQ], taps[:, j, i:i + 1], (second[:], zc[:, j, :])[n % 2]
                                if n == 1:
                                    dve.wait_ge(started, j + 1)
                                if n >= 2:
                                    dve.wait_ge(tapped, tap_steps[0] - 1)
                                if n == 0:
                                    if j > 0:
                                        dve.wait_ge(chained, step.n)
                                    ins = nc.vector.tensor_scalar(to, x, w, None, ALU.mult)
                                else:
                                    ins = nc.vector.scalar_tensor_tensor(out=to, in0=x, scalar=w, in1=to, op0=ALU.mult, op1=ALU.add)
                                ins.then_inc(tapped, 1)
                                tap_steps[0] += 1
                            dve.wait_ge(tapped, tap_steps[0])
                            nc.vector.tensor_tensor(zc[:, j, :], zc[:, j, :], second[:], ALU.add).then_inc(chained, 1)
                            step.n += 1

                        dve.wait_ge(loaded, 16)
                        dve.wait_ge(zeroed, 2)
                        weights.lo(dve)
                        weights.lo(dve)
                        for j in range(DK):
                            if j + 1 < DK:
                                weights.lo(dve)
                                weights.lo(dve)
                            dve.wait_ge(gated, j + 1)
                            ins = nc.vector.tensor_tensor(zp[:, j, HALF:HALF + SEQ], ps[(2 * j) % NROT][:], gate[:, j % 2, :], ALU.mult)
                            ins.then_inc(evac, 2)
                            dve.wait_ge(evac, 2 * (j + 1))
                            if j >= 2:
                                conv(j - 2)
                        conv(DK - 2)
                        conv(DK - 1)
                        side_sums(dve, "cv_in")
            with stage():
                cols = sb("cv_ln_columns", [P, 2, DK])
                sq = sb("squares", [P, 2, SEQ])
                mean, inv = sb("mean", [P, SEQ]), sb("inv_std", [P, SEQ])
                loaded, mm_mean, centred, squared, mm_var = sem("loaded"), sem("mean_product"), sem("centred"), sem("squared"), sem("var_product")
                chained, var_ready, root_ready, normed, applied = sem("vector_step"), sem("var_ready"), sem("root_ready"), sem("normed"), sem("silu_done")
                sq_used = sem("square_used")
                with nc.Block() as block:
                    @block.sync
                    def _(sp):
                        sp.dma_start(cols[:], dram["cv_ln"]).then_inc(loaded, 16)

                    @block.tensor
                    def _(pe):
                        for j in range(DK):
                            last = nc.tensor.matmul(ps[0][:], ones[:], zc[:, j, :], start=(j == 0), stop=(j == DK - 1))
                        last.then_inc(mm_mean, 1)
                        for j in range(DK):
                            pe.wait_ge(squared, j + 1)
                            nc.tensor.matmul(ps[1][:], ones[:], sq[:, j % 2, :], start=(j == 0), stop=(j == DK - 1)).then_inc(sq_used, 1)

                    @block.vector
                    def _(dve):
                        step = Chain(dve, chained)
                        dve.wait_ge(mm_mean, 1)
                        step(nc.vector.tensor_scalar(mean[:], ps[0][:], 1.0 / D, None, ALU.mult))
                        for j in range(DK):
                            nc.vector.tensor_tensor(zc[:, j, :], zc[:, j, :], mean[:], ALU.subtract).then_inc(centred, 1)
                        dve.wait_ge(sq_used, DK)
                        nc.vector.tensor_scalar(inv[:], ps[1][:], 1.0 / D, LN_EPS, ALU.mult, ALU.add).then_inc(var_ready, 1)
                        dve.wait_ge(root_ready, 1)
                        step(nc.vector.reciprocal(inv[:], inv[:]))
                        dve.wait_ge(centred, DK)
                        for j in range(DK):
                            nc.vector.tensor_tensor(zc[:, j, :], zc[:, j, :], inv[:], ALU.mult).then_inc(normed, 1)

                    @block.scalar
                    def _(act):
                        for j in range(DK):
                            act.wait_ge(centred, j + 1)
                            if j >= 2:
                                act.wait_ge(sq_used, j - 1)
                            nc.scalar.activation(sq[:, j % 2, :], zc[:, j, :], ACT.Square).then_inc(squared, 1)
                        act.wait_ge(var_ready, 1)
                        nc.scalar.activation(inv[:], inv[:], ACT.Sqrt).then_inc(root_ready, 1)
                        act.wait_ge(loaded, 16)
                        for j in range(DK):
                            act.wait_ge(normed, j + 1)
                            nc.scalar.activation(zc[:, j, :], zc[:, j, :], ACT.Silu, bias=cols[:, 1, j:j + 1],
                                                 scale=cols[:, 0, j:j + 1]).then_inc(applied, 1)
            out_product_ln_stage("cv_out", lambda k: zc[:, k:k + 2, :], "mix_ln_g1", "mix_ln_b1")

    all_tiles = list(range(TOK_T))
    CTXS, HALVES = slice(0, CTX), (slice(0, BANK), slice(BANK, TOK))
    SHIFT, SCALE, GATE, FF_SHIFT, FF_SCALE, FF_GATE = (i * DK for i in range(6))

    parked = nc.dram_tensor("parked_residual", (P, TOK_T * D), F32, kind="Internal").ap()

    def modulation2_stage(layer, part):
        mod = mods[f"ada{layer}"]
        with stage():
            loaded = sem("loaded")
            with nc.Block() as block:
                @block.sync
                def _(sp):
                    sp.dma_start(gains[:], dram["gains"][layer]).then_inc(loaded, 16)

                @block.vector
                def _(dve):
                    dve.wait_ge(loaded, 16)
                    for i, at, plus in ((2 * part, (FF_SCALE if part else SCALE), 1.0), (2 * part + 1, (FF_GATE if part else GATE), 0.0)):
                        for v in range(2):
                            nc.vector.scalar_tensor_tensor(out=mod[:, at:at + DK, v], in0=mod[:, at:at + DK, v], scalar=plus,
                                                           in1=gains[:, i, :], op0=ALU.add, op1=ALU.mult)

    def gates2_stage(layer, at, streams, beside=None):
        gate_row_stage([(v, mods[f"ada{layer}"][:, at:at + DK, v]) for v in range(streams)], beside)

    def modulated2_stage(layer, at_shift, at_scale, tiles, hT, t_base, buffers, beside=None):
        mod = mods[f"ada{layer}"]
        to_features_stage(resid, tiles, lambda f, v: mod[:, at_scale + f, v:v + 1],
                          lambda f, v: mod[:, at_shift + f, v:v + 1], hT, t_base, rms=buffers, beside=beside)

    def flat_of(x):
        return x[:].rearrange("p a b -> p (a b)")

    def out_product_rms_stage(name, source, tiles, bring_back=None):
        T = len(tiles)
        pieces = sum(nk // 2 for _, nk, _, _ in dict(MAIN)[name])
        with stage():
            product = sb("product", [P, T, D])
            left = LeftOperand(name, source, T * P)
            sums = sb("sums_of_squares", [P, T, 2])
            inv = sb("inv_rms", [P, T])
            mm_done, copied, squared = sem("mm_done"), sem("copied"), sem("squared")
            mean_ready, root_ready, chained, gated, added = sem("mean_ready"), sem("root_ready"), sem("vector_step"), sem("times_gate"), sem("added")
            brought = sem("residual_back")
            first = weights.at["pe"]
            with nc.Block() as block:
                @block.sync
                def _(sp):
                    weights.load(sp, name)
                    if bring_back is not None:
                        bring_back(sp, first, pieces, brought)

                @block.tensor
                def _(pe):
                    token_products(pe, name, tiles, left, mm_done, copied)

                @block.scalar
                def _(act):
                    for n in range(2):
                        for p in range(pieces // 2 + 1 if n == 0 else pieces // 2 - 1):
                            p += n * (pieces // 2 + 1)
                            weights.hi(act, left.share(p))
                        for i in range(T):
                            g = n * T + i
                            act.wait_ge(mm_done, g + 1)
                            to = product[:, i, n * BANK:(n + 1) * BANK]
                            nc.scalar.activation(to, ps[g % NROT][:], ACT.Square, accum_out=sums[:, i, n:n + 1]).then_inc(squared, 1)
                            act.wait_ge(squared, g + 1)
                            nc.scalar.copy(to, ps[g % NROT][:]).then_inc(copied, 1)
                    act.wait_ge(mean_ready, 1)
                    nc.scalar.activation(inv[:], inv[:], ACT.Sqrt).then_inc(root_ready, 1)

                @block.vector
                def _(dve):
                    step = Chain(dve, chained)
                    def times_gate(g):
                        n, i = divmod(g, T)
                        cols = slice(n * BANK, (n + 1) * BANK)
                        dve.wait_ge(copied, g + 1)
                        nc.vector.tensor_tensor(product[:, i, cols], product[:, i, cols], gate_rows[:, 0 if tiles[i] >= CTX_T else 1, cols],
                                                ALU.mult).then_inc(gated, 1)

                    g = 0
                    for p in range(pieces):
                        weights.lo(dve, left.share(p))
                        for _ in range(2):
                            if p > pieces // 2 and g < T:
                                times_gate(g)
                                g += 1
                    while g < 2 * T:
                        times_gate(g)
                        g += 1
                    step(nc.vector.tensor_tensor(inv[:], sums[:, :, 0], sums[:, :, 1], ALU.add))
                    nc.vector.tensor_scalar(inv[:], inv[:], 1.0 / D, RMS_EPS, ALU.mult, ALU.add).then_inc(mean_ready, 1)
                    dve.wait_ge(root_ready, 1)
                    step(nc.vector.reciprocal(inv[:], inv[:]))
                    dve.wait_ge(gated, 2 * T)
                    if bring_back is not None:
                        dve.wait_ge(brought, 16)
                    for i, t in enumerate(tiles):
                        nc.vector.scalar_tensor_tensor(out=resid[:, t, :], in0=product[:, i, :], scalar=inv[:, i:i + 1],
                                                       in1=resid[:, t, :], op0=ALU.mult, op1=ALU.add).then_inc(added, 1)
                    side_sums(dve, name)

    def ffn2_stages(layer, tiles):
        segs = [slice(0, CTX), slice(CTX, TOK)] if tiles[0] == 0 else [slice(0, SEQ)]
        n_tok, FFK = len(tiles) * P, DFF // P
        n_borrowed = DK if tiles[0] == 0 else 0
        with stage():
            own = sb("ff_hidden", [P, FFK - n_borrowed, n_tok])
            borrowed = flat_of(resid).rearrange("p (k n) -> p k n", n=TOK)
            hidden = lambda k: borrowed[:, k:k + 2, :] if k < n_borrowed else own[:, k - n_borrowed:k - n_borrowed + 2, :]
            area = flat_of(own)
            buffers = (area[:, 0:D], area[:, D:D + TOK_T * D].rearrange("p (t d) -> p t d", d=D),
                       area[:, (TOK_T + 1) * D:(TOK_T + 3) * D].rearrange("p (b n) -> p b n", n=BANK))
            with stage():
                hT = hT_pair(n_tok)
                park = None
                moved = sem("residual_parked")
                if n_borrowed:
                    def park(sp):
                        sp.dma_start(parked, flat_of(resid)).then_inc(moved, 16)
                        sp.wait_ge(moved, 16)
                modulated2_stage(layer, FF_SHIFT, FF_SCALE, tiles, hT, tiles[0], buffers, beside=park)
                with stage():
                    relu_done = sem("relu_done")
                    first = weights.at["pe"]
                    up = f"ff1_{layer}"
                    with nc.Block() as block:
                        @block.sync
                        def _(sp):
                            weights.load(sp, up)

                        @block.tensor
                        def _(pe):
                            feature_products(pe, up, hT, segs, relu_done)

                        @block.scalar
                        def _(act):
                            weights.hi(act)
                            for j in range(FFK):
                                if j + 1 < FFK:
                                    weights.hi(act)
                                act.wait_ge(weights.piece_used, first + j + 1)
                                for s, seg in enumerate(segs):
                                    bank = ps[(j * len(segs) + s) % NROT][:, 0:seg.stop - seg.start]
                                    nc.scalar.activation(hidden(j - j % 2)[:, j % 2, seg], bank, ACT.Relu).then_inc(relu_done, 1)

                        @block.vector
                        def _(dve):
                            weights.lo(dve)
                            for j in range(FFK):
                                if j + 1 < FFK:
                                    weights.lo(dve)
                                dve.wait_ge(relu_done, (j + 1) * len(segs))
                                h = hidden(j - j % 2)[:, j % 2, :]
                                nc.vector.tensor_tensor(h, h, h, ALU.mult)
                            side_sums(dve, up)
            gates2_stage(layer, FF_GATE, 2 if n_borrowed else 1)

            def bring_back(sp, first, pieces, brought):
                sp.wait_ge(weights.lo_made, first + pieces // 2 + n_borrowed // 2)
                sp.dma_start(flat_of(resid), parked).then_inc(brought, 16)
            out_product_rms_stage(f"ff2_{layer}", hidden, tiles, bring_back if n_borrowed else None)

    def qkv_stage(qk_name, v_name, hT, raw, n_q, vtok, q_segs):
        n_k = raw.shape[1] - n_q
        v_cols = vtok.shape[2]
        wide = v_cols == BANK
        v_feat = flat_of(gate_rows)[:, 0:TOK]
        segs_of = lambda j: q_segs if j < n_q else [CTXS, LAT]
        with stage():
            mm_done, copied, turned = sem("mm_done"), sem("copied"), sem("v_turned")
            first = weights.at["pe"]
            N = n_q + n_k
            n_copies = sum(len(segs_of(j)) for j in range(N))
            with nc.Block() as block:
                @block.sync
                def _(sp):
                    weights.load(sp, v_name)

                @block.tensor
                def _(pe):
                    g = feature_products(pe, qk_name, hT, segs_of, copied)
                    if wide:
                        token_products(pe, v_name, all_tiles, lambda p, kk, i: tuple(
                            h[:, 2 * p + kk, i * P:(i + 1) * P] for h in hT), mm_done, copied, g0=g)
                    else:
                        g = feature_products(pe, v_name, hT, [CTXS, LAT], copied, g0=g)
                        pe.wait_ge(copied, g)
                        for t in all_tiles:
                            last = nc.tensor.transpose(ps[t // 4][:, (t % 4) * P:(t % 4 + 1) * P], v_feat[:, t * P:(t + 1) * P], ident[:])
                        last.then_inc(turned, 1)

                @block.scalar
                def _(act):
                    g, hi_left = 0, N + (DK // 2 if wide else 1)
                    weights.hi(act)
                    hi_left -= 1
                    for j in range(N + (0 if wide else 1)):
                        if hi_left:
                            weights.hi(act)
                            hi_left -= 1
                        act.wait_ge(weights.piece_used, first + j + 1)
                        for s in segs_of(j):
                            to = raw[:, j, s] if j < N else v_feat[:, s]
                            nc.scalar.copy(to, ps[g % NROT][:, 0:s.stop - s.start]).then_inc(copied, 1)
                            g += 1
                    if wide:
                        for _ in range(hi_left):
                            weights.hi(act)
                        for t in all_tiles:
                            act.wait_ge(mm_done, t + 1)
                            nc.scalar.copy(vtok[:, t, :], ps[(g + t) % NROT][:]).then_inc(copied, 1)
                    else:
                        act.wait_ge(turned, 1)
                        nc.scalar.copy(vtok[:, 0:4, :], ps[0][:].rearrange("p (t d) -> p t d", d=P))
                        nc.scalar.copy(vtok[:, 4:TOK_T, :], ps[1][:, 0:2 * P].rearrange("p (t d) -> p t d", d=P))

                @block.vector
                def _(dve):
                    for _ in range(N + (DK // 2 if wide else 1)):
                        weights.lo(dve)
                    side_sums(dve, qk_name, v_name)

    def qk_norm_stage(raw, n_q, q_cols):
        jobs = [(j, s) for j in range(raw.shape[1]) for s in ([q_cols] if j < n_q else HALVES)]
        with stage():
            gain = sb("head_gain", [P, 2])
            sq = sb("squares", [P, 2, BANK])
            inv = sb("inv_rms", [P, 2, BANK])
            loaded, squared, mm_done, mean_ready = sem("loaded"), sem("squared"), sem("mm_done"), sem("mean_ready")
            root_ready, chained, applied = sem("root_ready"), sem("vector_step"), sem("applied")
            with nc.Block() as block:
                @block.sync
                def _(sp):
                    sp.dma_start(gain[:], dram["d_gain"]).then_inc(loaded, 16)

                @block.scalar
                def _(act):
                    def square(i):
                        j, s = jobs[i]
                        if i >= 2:
                            act.wait_ge(mm_done, i - 1)
                        nc.scalar.activation(sq[:, i % 2, 0:s.stop - s.start], raw[:, j, s], ACT.Square).then_inc(squared, 1)

                    square(0)
                    for i, (j, s) in enumerate(jobs):
                        n = s.stop - s.start
                        if i + 1 < len(jobs):
                            square(i + 1)
                        act.wait_ge(mean_ready, i + 1)
                        nc.scalar.activation(inv[:, i % 2, 0:n], inv[:, i % 2, 0:n], ACT.Sqrt).then_inc(root_ready, 1)

                @block.tensor
                def _(pe):
                    for i, (j, s) in enumerate(jobs):
                        n = s.stop - s.start
                        pe.wait_ge(squared, i + 1)
                        if i >= NBANK:
                            pe.wait_ge(mean_ready, i - NBANK + 1)
                        nc.tensor.matmul(ps[i % NBANK][:, 0:n], head_ones[:], sq[:, i % 2, 0:n], start=True, stop=True).then_inc(mm_done, 1)

                @block.vector
                def _(dve):
                    step = Chain(dve, chained)
                    dve.wait_ge(loaded, 16)
                    def mean(i):
                        n = jobs[i][1].stop - jobs[i][1].start
                        dve.wait_ge(mm_done, i + 1)
                        nc.vector.tensor_scalar(inv[:, i % 2, 0:n], ps[i % NBANK][:, 0:n], 1.0 / HD, RMS_EPS, ALU.mult, ALU.add).then_inc(mean_ready, 1)

                    mean(0)
                    for i, (j, s) in enumerate(jobs):
                        n = s.stop - s.start
                        if i + 1 < len(jobs):
                            mean(i + 1)
                        dve.wait_ge(root_ready, i + 1)
                        step(nc.vector.reciprocal(inv[:, i % 2, 0:n], inv[:, i % 2, 0:n]))
                        col = gain[:, 0:1] if j < n_q else gain[:, 1:2]
                        step(nc.vector.scalar_tensor_tensor(out=raw[:, j, s], in0=raw[:, j, s], scalar=col,
                                                            in1=inv[:, i % 2, 0:n], op0=ALU.mult, op1=ALU.mult))

    def rope_stage(raw):
        n = raw.shape[1]
        with stage():
            turn, cos, sin = sb("turn", [P, P]), sb("cos", [P, SEQ]), sb("sin", [P, SEQ])
            part = sb("turned_part", [P, 2, SEQ])
            loaded, mm_done, turned, chained, added = sem("loaded"), sem("mm_done"), sem("turned"), sem("vector_step"), sem("added")
            with nc.Block() as block:
                @block.sync
                def _(sp):
                    for dst, name in ((turn, "rope_turn"), (cos, "rope_cos"), (sin, "rope_sin")):
                        sp.dma_start(dst[:], dram[name]).then_inc(loaded, 16)

                @block.tensor
                def _(pe):
                    pe.wait_ge(loaded, 48)
                    for j in range(n):
                        nc.tensor.matmul(ps[j][:], turn[:], raw[:, j, LAT], start=True, stop=True).then_inc(mm_done, 1)

                @block.vector
                def _(dve):
                    step = Chain(dve, chained)
                    dve.wait_ge(loaded, 48)
                    for j in range(n):
                        dve.wait_ge(mm_done, j + 1)
                        if j >= 2:
                            dve.wait_ge(added, j - 1)
                        step(nc.vector.tensor_tensor(part[:, j % 2, :], ps[j][:], sin[:], ALU.mult))
                        nc.vector.tensor_tensor(raw[:, j, LAT], raw[:, j, LAT], cos[:], ALU.mult).then_inc(turned, 1)

                @block.gpsimd
                def _(pool):
                    for j in range(n):
                        pool.wait_ge(turned, j + 1)
                        nc.gpsimd.tensor_tensor(raw[:, j, LAT], raw[:, j, LAT], part[:, j % 2, :], ALU.add).then_inc(added, 1)

    def spread_heads_stage(raw, n_q, k_low):
        with stage():
            copied = sem("copied")
            with nc.Block() as block:
                @block.gpsimd
                def _(pool):
                    nc.gpsimd.memset(k_low[HD:P], 0.0)

                @block.scalar
                def _(act):
                    nc.scalar.copy(k_low[0:HD], raw[0:HD, n_q:, :]).then_inc(copied, 1)

                @block.vector
                def _(dve):
                    dve.wait_ge(copied, 1)
                    nc.vector.memset(raw[0:HD, n_q:, :], 0.0)

    def attention_stage(raw, k_halves, vtok, mixT, mix_at, jobs, kv_of, mix_base=0, sink=None, mask=None, bias=None, park=False):
        items = [(job, h) for job in jobs for h in range(8)]
        N = len(items)
        with stage():
            sc = sb("scores", [P, 2, TOK])
            pr = sb("probs", [P, 2, TOK])
            pT = sb("probs_turned", [P, 2, TOK])
            o = sb("head_outputs", [P, 2, 512])
            top, total, esink, inv = (sb(n, [P, N]) for n in ("minus_max", "total", "exp_sink", "inv_total"))
            if bias is not None:
                NB = 4
                bias_ring = sb("bias_ring", [P, NB, SEQ])
                bias_landed = [sem(f"bias_landed{i}") for i in range(NB)]
            if mask is not None:
                mask_sb = sb("mask", [P, 3 * P])
            if sink is not None:
                sink_sb = sb("sink", [P, 8])
            loaded, scored, read, max_ready = sem("loaded"), sem("scored"), sem("scores_read"), sem("max_ready")
            exp_done, sink_done, turned, turn_copied, weighed, scaled = (sem(n) for n in (
                "exp_done", "sink_done", "probs_turned", "turn_copied", "weighed", "output_scaled"))
            parked_done = sem("residual_parked")
            o_turned, o_copied, chained = sem("outputs_turned"), sem("outputs_copied"), sem("vector_step")

            def spans(i):
                (qt, lat, _), h = items[i]
                n = CTX + (lat.stop - lat.start if lat else 0)
                keys = [0, 1] + ([c // P for c in range(lat.start, lat.stop, P)] if lat else [])
                return qt, h, lat, n, keys

            with nc.Block() as block:
                @block.sync
                def _(sp):
                    if park:
                        sp.dma_start(parked, flat_of(resid)).then_inc(parked_done, 16)
                    if mask is not None:
                        sp.dma_start(mask_sb[:], dram[mask]).then_inc(loaded, 16)
                    if sink is not None:
                        sp.dma_start(sink_sb[:], dram[sink].partition_broadcast(P)).then_inc(loaded, 16)
                    if bias is not None:
                        for i in range(N):
                            qt, h, lat, n, keys = spans(i)
                            if i >= NB:
                                sp.wait_ge(read, i - NB + 1)
                            sp.dma_start(bias_ring[:, i % NB, :], dram[bias][h, (qt - CTX_T) * P:(qt - CTX_T + 1) * P, :]).then_inc(bias_landed[i % NB], 16)
                    if park:
                        sp.wait_ge(parked_done, 16)

                @block.tensor
                def _(pe):
                    def score(i):
                        qt, h, lat, n, keys = spans(i)
                        if i >= 2:
                            pe.wait_ge(read, i - 1)
                        q = raw[:, h // 2, qt * P:(qt + 1) * P]
                        k = k_halves[h % 2][:, kv_of(h)[0], :]
                        b = 2 * (i % 2)
                        last = nc.tensor.matmul(ps[b][:, 0:CTX], q, k[:, 0:CTX], start=True, stop=True)
                        if lat:
                            last = nc.tensor.matmul(ps[b + 1][:, 0:n - CTX], q, k[:, lat], start=True, stop=True)
                        last.then_inc(scored, 1)

                    def turn(i):
                        qt, h, lat, n, keys = spans(i)
                        pe.wait_ge(exp_done, i + 1)
                        if i >= 1:
                            pe.wait_ge(turn_copied, i)
                        for m in range(len(keys)):
                            last = nc.tensor.transpose(ps[4 + m // 4][:, (m % 4) * P:(m % 4 + 1) * P],
                                                       pr[:, i % 2, m * P:(m + 1) * P], ident[:])
                        last.then_inc(turned, 1)

                    def weigh(i):
                        qt, h, lat, n, keys = spans(i)
                        pe.wait_ge(turn_copied, i + 1)
                        if i >= 1:
                            pe.wait_ge(scaled, i)
                        v = kv_of(h)[1]
                        for m, kt in enumerate(keys):
                            last = nc.tensor.matmul(ps[6][:, 0:HD], pT[:, i % 2, m * P:(m + 1) * P], vtok[:, kt, v],
                                                    start=(m == 0), stop=(m == len(keys) - 1))
                        last.then_inc(weighed, 1)

                    def turn_outputs(q):
                        pe.wait_ge(scaled, 8 * (q + 1))
                        if q >= 1:
                            pe.wait_ge(o_copied, q)
                        for f in range(4):
                            last = nc.tensor.transpose(ps[7][:, f * P:(f + 1) * P], o[:, q % 2, f * P:(f + 1) * P], ident[:])
                        last.then_inc(o_turned, 1)

                    for i in range(N + 5):
                        if i < N:
                            score(i)
                        if 0 <= i - 2 < N:
                            turn(i - 2)
                        if 0 <= i - 3 < N:
                            weigh(i - 3)
                        if i > 4 and (i - 4) % 8 == 0:
                            turn_outputs((i - 4) // 8 - 1)

                @block.vector
                def _(dve):
                    step = Chain(dve, chained)
                    if mask is not None or sink is not None:
                        dve.wait_ge(loaded, 16 * ((mask is not None) + (sink is not None)))

                    def front(i):
                        qt, h, lat, n, keys = spans(i)
                        b = 2 * (i % 2)
                        s = sc[:, i % 2, :]
                        dve.wait_ge(scored, i + 1)
                        if i >= 2:
                            dve.wait_ge(exp_done, i - 1)
                        first = nc.vector.tensor_scalar(s[:, 0:CTX], ps[b][:, 0:CTX], ATTN_SCALE, None, ALU.mult)
                        if lat:
                            if bias is not None:
                                dve.wait_ge(bias_landed[i % NB], 16 * (i // NB + 1))
                                add = bias_ring[:, i % NB, :]
                            elif mask is not None:
                                add = mask_sb[:, items[i][0][2]]
                            if bias is not None or mask is not None:
                                last = nc.vector.scalar_tensor_tensor(out=s[:, CTX:n], in0=ps[b + 1][:, 0:n - CTX], scalar=ATTN_SCALE,
                                                                      in1=add, op0=ALU.mult, op1=ALU.add)
                            else:
                                last = nc.vector.tensor_scalar(s[:, CTX:n], ps[b + 1][:, 0:n - CTX], ATTN_SCALE, None, ALU.mult)
                        else:
                            last = first
                        last.then_inc(read, 1)
                        dve.wait_ge(read, i + 1)
                        step(nc.vector.tensor_reduce(top[:, i:i + 1], s[:, 0:n], AX_X, ALU.max))
                        if sink is not None:
                            nc.vector.tensor_scalar(top[:, i:i + 1], top[:, i:i + 1], sink_sb[:, h:h + 1], -1.0, ALU.max, ALU.mult).then_inc(max_ready, 1)
                        else:
                            nc.vector.tensor_scalar(top[:, i:i + 1], top[:, i:i + 1], -1.0, None, ALU.mult).then_inc(max_ready, 1)

                    def back(i):
                        qt, h, lat, n, keys = spans(i)
                        dve.wait_ge(sink_done if sink is not None else exp_done, i + 1)
                        if sink is not None:
                            step(nc.vector.tensor_tensor(total[:, i:i + 1], total[:, i:i + 1], esink[:, i:i + 1], ALU.add))
                        step(nc.vector.reciprocal(inv[:, i:i + 1], total[:, i:i + 1]))
                        q = i // 8
                        if i % 8 == 0 and q >= 2:
                            dve.wait_ge(o_turned, q - 1)
                        dve.wait_ge(weighed, i + 1)
                        nc.vector.tensor_scalar(o[:, q % 2, h * HD:(h + 1) * HD], ps[6][:, 0:HD], inv[:, i:i + 1], None,
                                                ALU.mult).then_inc(scaled, 1)

                    for i in range(N + 4):
                        if i >= 4:
                            back(i - 4)
                        if i < N:
                            front(i)

                @block.scalar
                def _(act):
                    if sink is not None:
                        act.wait_ge(loaded, 16 * ((mask is not None) + 1))

                    def exps(i):
                        qt, h, lat, n, keys = spans(i)
                        act.wait_ge(max_ready, i + 1)
                        if i >= 2:
                            act.wait_ge(turned, i - 1)
                        nc.scalar.activation(pr[:, i % 2, 0:n], sc[:, i % 2, 0:n], ACT.Exp, bias=top[:, i:i + 1],
                                             accum_out=total[:, i:i + 1]).then_inc(exp_done, 1)
                        if sink is not None:
                            nc.scalar.activation(esink[:, i:i + 1], sink_sb[:, h:h + 1], ACT.Exp, bias=top[:, i:i + 1]).then_inc(sink_done, 1)

                    def copy_turned(i):
                        qt, h, lat, n, keys = spans(i)
                        act.wait_ge(turned, i + 1)
                        if i >= 2:
                            act.wait_ge(weighed, i - 1)
                        first = nc.scalar.copy(pT[:, i % 2, 0:min(n, BANK)], ps[4][:, 0:min(n, BANK)])
                        if n > BANK:
                            nc.scalar.copy(pT[:, i % 2, BANK:n], ps[5][:, 0:n - BANK]).then_inc(turn_copied, 1)
                        else:
                            first.then_inc(turn_copied, 1)

                    def copy_outputs(q):
                        act.wait_ge(o_turned, q + 1)
                        qt = jobs[q][0]
                        nc.scalar.copy(mixT[:, mix_at:mix_at + 4, (qt - mix_base) * P:(qt - mix_base + 1) * P],
                                       ps[7][:].rearrange("p (f n) -> p f n", f=4)).then_inc(o_copied, 1)

                    for i in range(N + 5):
                        if 0 <= i - 1 < N:
                            exps(i - 1)
                        if 0 <= i - 2 < N:
                            copy_turned(i - 2)
                        if i > 4 and (i - 4) % 8 == 0:
                            copy_outputs((i - 4) // 8 - 1)

    def lat_cols(a, b):
        return slice(CTX + a * P, CTX + b * P)

    def windowed_attention(raw, vtok, mixT):
        rope_stage(raw)
        with stage():
            k_low = sb("k_low", [P, 2, TOK])
            spread_heads_stage(raw, 4, k_low)
            kv = lambda h: (h // 4, slice((h // 4) * HD, (h // 4 + 1) * HD))
            jobs = [(t, None, None) for t in range(CTX_T)]
            for n in range(LAT_T):
                a, b = max(n - 1, 0), min(n + 2, LAT_T)
                jobs.append((CTX_T + n, lat_cols(a, b), slice((a - n + 1) * P, (b - n + 1) * P)))
            attention_stage(raw, (k_low, raw[:, 4:6]), vtok, mixT, 4, jobs, kv, sink="b_sink", mask="window_mask", park=True)

    def odd_mixer():
        jobs = [(CTX_T + n, LAT, None) for n in range(LAT_T)]
        mixT = sb("mixT", [P, DK, SEQ])
        with stage():
            raw_d = sb("qk_d", [P, 6, TOK])
            v_d = gate_rows[:, 1, 0:TOK_T * P].rearrange("p (t d) -> p t d", d=P)
            with stage():
                raw_c, v_c = sb("qk_c", [P, 8, TOK]), sb("v_c", [P, TOK_T, BANK])
                with stage():
                    hT = hT_pair(TOK)
                    buffers = (flat_of(gate_rows)[:, 0:D], flat_of(raw_c).rearrange("p (t d) -> p t d", d=D), v_c[:, 0:4, :])
                    modulated2_stage(1, SHIFT, SCALE, all_tiles, hT, 0, buffers)
                    qkv_stage("c_qk", "c_v", hT, raw_c, 4, v_c, [LAT])
                    qkv_stage("d_qk", "d_v", hT, raw_d, 4, v_d, [LAT])
                k_low = sb("k_low", [P, 4, TOK])
                spread_heads_stage(raw_c, 4, k_low)
                attention_stage(raw_c, (k_low, raw_c[:, 4:8]), v_c, mixT, 0, jobs, lambda h: (h // 2, slice(h * HD, (h + 1) * HD)),
                                mix_base=CTX_T, bias="rpb_table")
            qk_norm_stage(raw_d, 4, LAT)
            rope_stage(raw_d)
            k_low = sb("k_low", [P, 2, TOK])
            spread_heads_stage(raw_d, 4, k_low)
            attention_stage(raw_d, (k_low, raw_d[:, 4:6]), v_d, mixT, 4, jobs,
                            lambda h: (h // 4, slice((h // 4) * HD, (h // 4 + 1) * HD)), mix_base=CTX_T)
        return mixT

    R_MU, R_W0, R_A0, R_KK, R_KA, R_RK, R_GW, R_GB = 0, 30, 38, 46, 50, 54, 58, 62
    R_COLS = 66

    def shifted_products_stage(name, hT, dests, mu_tiles, rcols, raw, park=None, meanwhile=None):
        with stage():
            keep = sb("mu_keep", [P, 15])
            copied, chained, shifted, stored_tile = sem("copied"), sem("vector_step"), sem("shifted"), sem("tile_parked")
            first, J = weights.at["pe"], len(dests)
            mu = rcols[:, R_MU:R_MU + 30].rearrange("p (j m) -> p j m", m=2)
            with nc.Block() as block:
                @block.sync
                def _(sp):
                    weights.load(sp, name)

                if park is not None:
                    @block.gpsimd
                    def _(pool):
                        for j, dst in enumerate(dests):
                            pool.wait_ge(shifted, j + 1)
                            pool.dma_start(park[:, j * TOK:(j + 1) * TOK], dst).then_inc(stored_tile, 16)
                        pool.wait_ge(stored_tile, 16 * J)

                @block.tensor
                def _(pe):
                    feature_products(pe, name, hT, [CTXS, LAT], copied)

                @block.scalar
                def _(act):
                    weights.hi(act)
                    for j in range(J):
                        if j + 1 < J:
                            weights.hi(act)
                        if j == 0 and meanwhile is not None:
                            meanwhile()
                        act.wait_ge(weights.piece_used, first + j + 1)
                        if j >= 2:
                            act.wait_ge(shifted, j - 1)
                        for s, seg in enumerate((CTXS, LAT)):
                            nc.scalar.copy(raw[:, j % 2, seg], ps[(2 * j + s) % NROT][:, 0:seg.stop - seg.start]).then_inc(copied, 1)

                @block.vector
                def _(dve):
                    step = Chain(dve, chained)
                    step(nc.vector.tensor_tensor(keep[:], mu[:, :, 0], mu[:, :, 1], ALU.add))
                    step(nc.vector.tensor_scalar(keep[:], keep[:], -1.0, 1.0, ALU.mult, ALU.add))
                    weights.lo(dve)
                    for j, (dst, m) in enumerate(zip(dests, mu_tiles)):
                        if j + 1 < J:
                            weights.lo(dve)
                        p = raw[:, j % 2, :]
                        dve.wait_ge(copied, 2 * j + 2)
                        step(nc.vector.tensor_scalar(dst, p, keep[:, m:m + 1], None, ALU.mult))
                        for seg in (CTXS, LAT):
                            a, b = seg.start, seg.stop
                            step(nc.vector.scalar_tensor_tensor(out=dst[:, a + 1:b], in0=p[:, a:b - 1], scalar=mu[:, m, 0:1],
                                                                in1=dst[:, a + 1:b], op0=ALU.mult, op1=ALU.add))
                            last = nc.vector.scalar_tensor_tensor(out=dst[:, a:b - 1], in0=p[:, a + 1:b], scalar=mu[:, m, 1:2],
                                                                  in1=dst[:, a:b - 1], op0=ALU.mult, op1=ALU.add)
                            if seg is CTXS:
                                step(last)
                        last.then_inc(shifted, 1)
                        dve.wait_ge(shifted, j + 1)
                    side_sums(dve, name)

    parked_rkv = nc.dram_tensor("parked_rkv", (P, 6 * TOK), F32, kind="Internal").ap()

    def even_mixer(mixT):
        flat2 = flat_of(gate_rows)
        with stage():
            rcols = sb("recurrence_columns", [P, R_COLS])
            lora = sb("lora", [P, 3, TOK])
            r, k, v = (sb(n, [P, 2, TOK]) for n in ("r", "k_then_y", "v"))
            with stage():
                raw_b, v_b = sb("qk_b", [P, 6, TOK]), sb("v_b", [P, TOK_T, P])
                with stage():
                    hT = hT_pair(TOK)
                    loaded = sem("loaded")

                    def load_columns(sp):
                        sp.dma_start(rcols[:], dram["r_cols"]).then_inc(loaded, 16)
                        sp.wait_ge(loaded, 16)
                    buffers = (flat2[:, 0:D], flat_of(mixT).rearrange("p (t d) -> p t d", d=D),
                               flat_of(raw_b)[:, 0:4 * BANK].rearrange("p (b n) -> p b n", n=BANK))
                    modulated2_stage(0, SHIFT, SCALE, all_tiles, hT, 0, buffers, beside=load_columns)
                    qkv_stage("b_qk", "b_v", hT, raw_b, 4, v_b, [CTXS, LAT])
                    raw = flat2[:, 0:2 * TOK].rearrange("p (b n) -> p b n", b=2)
                    shifted_products_stage("lora", hT, [lora[:, j, :] for j in range(3)], [12, 13, 14], rcols, raw)

                    def lora_activations():
                        nc.scalar.activation(lora[:, 0, :], lora[:, 0, :], ACT.Tanh)
                        nc.scalar.activation(lora[:, 2, :], lora[:, 2, :], ACT.Sigmoid)
                    later = mixT[:, 0:6, :]
                    tiles_of = lambda half: [4 * x + 2 * half + j for x in range(3) for j in range(2)]
                    shifted_products_stage("rkv0", hT, [x[:, j, :] for x in (r, k, v) for j in range(2)], tiles_of(0), rcols, raw,
                                           meanwhile=lora_activations)
                    shifted_products_stage("rkv1", hT, [later[:, j, :] for j in range(6)], tiles_of(1), rcols, raw, park=parked_rkv)
                windowed_attention(raw_b, v_b, mixT)
            dump("battn", mixT[:, 4:8, :])
            recurrence(rcols, lora, r, k, v, mixT)

    def recurrence(rcols, lora, r, k, v, mixT):
        flat, flat2 = flat_of(resid), flat_of(gate_rows)
        with stage():
            kk = sb("kk", [P, 2, TOK])
            iclr, kdir = sb("iclr_then_b", [P, 4, TOK]), sb("k_dir", [P, 4, TOK])
            run = sb("running_decay", [P, 4, NCH * CW])
            gam = sb("chunk_decay", [P, 3, 4, NCH])
            for half in range(2):
                prepare_stage(half, rcols, lora, r, k, v, kk, iclr, kdir, run, gam, mixT, flat)
                if half == 0:
                    dump("kk", kk[:]); dump("kdir", kdir[:]); dump("run", run[:]); dump("bb", iclr[:]); dump("bv", mixT[:, 0:2, :])
                scan_stage(r, k, v, kk, iclr, kdir, run, gam, flat, flat2)
                if half == 0:
                    dump("y", k[:])
                head_norm_stage(half, rcols, lora, r, k, v, mixT, flat)
                if half == 0:
                    with stage():
                        moved = sem("k_loaded")
                        with nc.Block() as block:
                            @block.sync
                            def _(sp):
                                sp.dma_start(flat_of(k), parked_rkv[:, 2 * TOK:4 * TOK]).then_inc(moved, 16)
                                sp.wait_ge(moved, 16)

    def prepare_stage(half, rcols, lora, r, k, v, kk, iclr, kdir, run, gam, mixT, flat):
        f0 = 2 * half
        col = lambda at, f: rcols[:, at + f:at + f + 1]
        SW = NCH * CW
        sg = flat[:, 0:2 * SW].rearrange("p (b n) -> p b n", b=2)
        tmp = flat[:, 2 * SW:2 * SW + 2 * TOK].rearrange("p (b n) -> p b n", b=2)
        tmp2 = flat[:, 2 * SW + 2 * TOK:2 * SW + 3 * TOK]
        with stage():
            w2, a2 = sb("w2", [P, 2, 2 * P]), sb("a2", [P, 2, 2 * P])
            reset = sb("reset", [P, SW])
            omka = sb("one_minus_ka", [P, 4])
            loaded, zeroed, w_mm, w_sig, a_mm, a_sig, scanned = (sem(n) for n in (
                "loaded", "zeroed", "w_product", "w_sigmoid", "a_product", "a_sigmoid", "scanned"))
            kk_sq, kk_mm, kk_root, r_ready, r_mm, chained, kk_made = (sem(n) for n in (
                "kk_squared", "kk_product", "kk_root", "bonus_terms", "bonus_product", "vector_step", "kk_made"))
            sq_made = sem("kk_unnormed")
            tots = sem("totals")
            gam_made = sem("chunk_decays")
            with nc.Block() as block:
                @block.sync
                def _(sp):
                    sp.dma_start(w2[:], dram["w2"][half]).then_inc(loaded, 16)
                    sp.dma_start(a2[:], dram["a2"][half]).then_inc(loaded, 16)
                    sp.dma_start(reset[:], dram["reset"].partition_broadcast(P)).then_inc(loaded, 16)

                @block.gpsimd
                def _(pool):
                    for b in range(2):
                        nc.gpsimd.memset(sg[:, b, :], 0.0).then_inc(zeroed, 1)

                @block.tensor
                def _(pe):
                    for f in range(2):
                        pe.wait_ge(kk_sq, f + 1)
                        for s, seg in enumerate(HALVES):
                            nc.tensor.matmul(ps[2 * f + s][:, 0:seg.stop - seg.start], head_ones[:], tmp[:, f, seg],
                                             start=True, stop=True).then_inc(kk_mm, 1)
                    pe.wait_ge(loaded, 48)
                    for i in range(4):
                        d, f = divmod(i, 2)
                        if i < 2:
                            pe.wait_ge(kk_root, 2 * i + 2)
                        else:
                            pe.wait_ge(w_sig, 2 * (i - 1))
                        for s, seg in enumerate(HALVES):
                            nc.tensor.matmul(ps[2 * (i % 2) + s][:, 0:seg.stop - seg.start], w2[:, d, f * P:(f + 1) * P],
                                             lora[:, 0, seg], start=True, stop=True).then_inc(w_mm, 1)
                        if i >= 2:
                            pe.wait_ge(a_sig, 2 * (i - 1))
                        for s, seg in enumerate(HALVES):
                            nc.tensor.matmul(ps[4 + 2 * (i % 2) + s][:, 0:seg.stop - seg.start], a2[:, d, f * P:(f + 1) * P],
                                             lora[:, 1, seg], start=True, stop=True).then_inc(a_mm, 1)
                    pe.wait_ge(a_sig, 8)
                    for f in range(2):
                        pe.wait_ge(r_ready, f + 1)
                        for s, seg in enumerate(HALVES):
                            nc.tensor.matmul(ps[4 + 2 * f + s][:, 0:seg.stop - seg.start], head_ones[:], tmp[:, f, seg],
                                             start=True, stop=True).then_inc(r_mm, 1)

                @block.scalar
                def _(act):
                    for f in range(2):
                        act.wait_ge(sq_made, f + 1)
                        nc.scalar.activation(tmp[:, f, :], kk[:, f, :], ACT.Square).then_inc(kk_sq, 1)
                    for f in range(2):
                        for s, seg in enumerate(HALVES):
                            act.wait_ge(kk_mm, 2 * f + s + 1)
                            nc.scalar.activation(tmp[:, f, seg], ps[2 * f + s][:, 0:seg.stop - seg.start], ACT.Sqrt).then_inc(kk_root, 1)
                    act.wait_ge(zeroed, 2)
                    for i in range(4):
                        d, f = divmod(i, 2)
                        if i >= 2:
                            act.wait_ge(scanned, i - 1)
                        for s, seg in enumerate(HALVES):
                            n = (seg.stop - seg.start) // CH
                            c0 = seg.start // CH
                            to = sg[:, i % 2, :].rearrange("p (c w) -> p c w", w=CW)[:, c0:c0 + n, 1:CW]
                            act.wait_ge(w_mm, 2 * i + s + 1)
                            nc.scalar.activation(to, ps[2 * (i % 2) + s][:, 0:n * CH].rearrange("p (c w) -> p c w", w=CH), ACT.Sigmoid,
                                                 bias=rcols[:, R_W0 + 4 * d + f0 + f:R_W0 + 4 * d + f0 + f + 1]).then_inc(w_sig, 1)
                        for s, seg in enumerate(HALVES):
                            act.wait_ge(a_mm, 2 * i + s + 1)
                            nc.scalar.activation(iclr[:, i, seg], ps[4 + 2 * (i % 2) + s][:, 0:seg.stop - seg.start], ACT.Sigmoid,
                                                 bias=rcols[:, R_A0 + 4 * d + f0 + f:R_A0 + 4 * d + f0 + f + 1]).then_inc(a_sig, 1)
                    act.wait_ge(tots, 2)
                    nc.scalar.activation(gam[:, 0, :, :], gam[:, 1, :, :], ACT.Exp).then_inc(gam_made, 1)

                @block.vector
                def _(dve):
                    step = Chain(dve, chained)
                    for f in range(2):
                        nc.vector.tensor_scalar(kk[:, f, :], k[:, f, :], col(R_KK, f0 + f), None, ALU.mult).then_inc(sq_made, 1)
                    dve.wait_ge(kk_root, 4)
                    for f in range(2):
                        step(nc.vector.tensor_scalar(tmp[:, f, :], tmp[:, f, :], 1e-12, None, ALU.max))
                        step(nc.vector.reciprocal(tmp[:, f, :], tmp[:, f, :]))
                        step(nc.vector.tensor_tensor(kk[:, f, :], kk[:, f, :], tmp[:, f, :], ALU.mult))
                    dve.wait_ge(loaded, 48)
                    for i in range(4):
                        dve.wait_ge(w_sig, 2 * i + 2)
                        nc.vector.tensor_tensor_scan(out=run[:, i, :], data0=reset[:], data1=sg[:, i % 2, :], initial=0.0,
                                                     op0=ALU.mult, op1=ALU.add).then_inc(scanned, 1)
                    dve.wait_ge(scanned, 4)
                    ends = run[:].rearrange("p i (c w) -> p i c w", w=CW)[:, :, :, CH]
                    nc.vector.tensor_scalar(gam[:, 1, :, :], ends, -DECAY, None, ALU.mult).then_inc(tots, 1)
                    nc.vector.tensor_scalar(gam[:, 2, :, :], ends, DECAY, None, ALU.mult).then_inc(tots, 1)
                    step(nc.vector.tensor_scalar(omka[:], rcols[:, R_KA:R_KA + 4], -1.0, 1.0, ALU.mult, ALU.add))
                    dve.wait_ge(a_sig, 8)
                    for i in range(4):
                        d, f = divmod(i, 2)
                        step(nc.vector.tensor_scalar(kdir[:, i, :], iclr[:, i, :], col(R_KA, f0 + f), omka[:, f0 + f:f0 + f + 1], ALU.mult, ALU.add))
                        step(nc.vector.tensor_tensor(kdir[:, i, :], kdir[:, i, :], k[:, f, :], ALU.mult))
                        step(nc.vector.tensor_tensor(iclr[:, i, :], iclr[:, i, :], kk[:, f, :], ALU.mult))
                    for f in range(2):
                        step(nc.vector.tensor_tensor(tmp2, kdir[:, f, :], kdir[:, 2 + f, :], ALU.add))
                        nc.vector.scalar_tensor_tensor(out=tmp[:, f, :], in0=tmp2, scalar=col(R_RK, f0 + f), in1=r[:, f, :],
                                                       op0=ALU.mult, op1=ALU.mult).then_inc(r_ready, 1)
                        dve.wait_ge(r_ready, f + 1)
                    for f in range(2):
                        for s, seg in enumerate(HALVES):
                            dve.wait_ge(r_mm, 2 * f + s + 1)
                            step(nc.vector.tensor_tensor(mixT[:, f0 + f, seg], ps[4 + 2 * f + s][:, 0:seg.stop - seg.start], v[:, f, seg], ALU.mult))

    def recurrence_orders():
        def both(*names):
            return [(n, d) for n in names for d in range(2)]

        e_of = [[("e0", 0), ("e1", 0), ("e2", 0)], [(f"e{j}{i}", 1) for j in range(3) for i in range(2)]]
        ahead = lambda names: [("ahead",) + x for x in names]
        pe = both("N", "bk_turned", "v_A_r")
        for l in range(1, LEVELS):
            pe += [x for d in range(2) for x in ((f"X{l}", d), (f"T{l - 1}", d))[:1 if l == 1 else 2]]
            pe += {2: [("Z", 0)], 3: [("Z", 1)], 4: ahead([("A", 0)]), 5: ahead([("A", 1)])}.get(l, [])
            pe += both(f"GX{l}")
        pe += both("U", "Y", "S")
        dve = both("G0", "A_r", "T0", "G1", "G2") + [("Z", 0)]
        dve += ahead([("a", 0), ("r", 0)]) + both("G3") + [("Z", 1)] + ahead([("a", 1), ("r", 1)]) + both("G4", "G5")
        dve += ahead([x for d in range(2) for x in (("A_ab", d), ("A_ak", d))])
        dve += [x for d in range(2) for x in (("Y", d), ("S_sum", d), ("S", d))]
        act = both("bk", "v")
        for l in range(1, LEVELS):
            act += [x for d in range(2) for x in ((f"X{l}", d), (f"T{l - 1}", d))[:1 if l == 1 else 2]]
            act += ahead({1: e_of[0], 2: e_of[1][:3], 3: e_of[1][3:]}.get(l, []))
        act += both("U") + ahead(both("G_init", "T_init"))
        pool = ahead([x for d in range(2) for x in (("b", d), ("k", d), ("v", d))])
        places = {}
        for who, period in (("PE", pe), ("DVE", dve), ("ACT", act), ("POOL", pool)):
            place = {}
            for c in range(-1, NCH):
                for x in period:
                    step = c + 1 if x[0] == "ahead" else c
                    if 0 <= step < NCH:
                        place[x[-2:] + (step,)] = len(place) + 1
            places[who] = place
        return places

    def scan_stage(r, y, v, kk, bb, kdir, run, gam, flat, flat2):
        with stage():
            def full(i):
                return flat[:, i * 512:(i + 1) * 512].rearrange("p (i n) -> p i n", i=4)
            aexp0, bexp, kexp, vexp, A_ab, A_ak_T, G, T, X, Bt, Kt, V = (full(i) for i in range(12))
            aexp = [aexp0, sb("a_spread", [P, 4, P])[:]]
            BK = flat[:, 9 * 512:11 * 512].rearrange("p (m i n) -> p m i n", m=2, i=4)
            U, Z, S = (flat2[:, i * 512:(i + 1) * 512].rearrange("p (i n) -> p i n", i=4) for i in range(3))
            A_r_T = flat2[:, 1536:2048].rearrange("p (m i n) -> p m i n", m=2, i=4)
            e = sb("decay_factors", [P, 3, 4, CH])
            rc = sb("r_decayed", [P, 2, 4, CH])
            before = sb("mask_before", [P, 2, P])
            before_T = sb("mask_before_T", [P, 2, P])
            upto_T = sb("mask_upto_T", [P, 2, CH])
            level = sb("level_masks", [P, LEVELS, 2, P], U8)
            level_f32 = flat[:, 9 * 512:12 * 512]
            loaded, zeroed, levels_cast = sem("loaded"), sem("zeroed"), sem("levels_cast")
            made = {"PE": sem("product_made"), "DVE": sem("vector_made"), "ACT": sem("scalar_made"), "POOL": sem("pool_made")}
            places = recurrence_orders()

            def need(eng, who, what, d, c):
                if c >= 0:
                    eng.wait_ge(made[who], places[who][(what, d, c)])

            def chunk(d, c):
                return c if d == 0 else (CTX_CH - 1 - c if c < CTX_CH else NCH + CTX_CH - 1 - c)

            def tokens(d, c):
                return slice(chunk(d, c) * CH, (chunk(d, c) + 1) * CH)

            def items(x, d):
                return x[:, 2 * d:2 * d + 2, :]

            def both_items(mask):
                return mask.unsqueeze(1).broadcast_to([P, 2, mask.shape[1]])

            def bank(d, b, n=P, at=0):
                return ps[4 * d + b][:, at:at + 2 * n].rearrange("p (i n) -> p i n", i=2)

            halves = [(slice(0, HD), slice(0, CH)), (slice(HD, P), slice(CH, P))]

            with nc.Block() as block:
                @block.sync
                def _(sp):
                    for dst, name in ((before, "mask_before"), (before_T, "mask_before_T"), (upto_T, "mask_upto_T")):
                        sp.dma_start(dst[:], dram[name]).then_inc(loaded, 16)
                    sp.dma_start(level_f32, dram["level_masks"]).then_inc(loaded, 16)

                @block.gpsimd
                def _(pool):
                    cleared = (bexp, kexp, aexp[0], vexp, aexp[1], S, y[:])
                    for x in cleared:
                        nc.gpsimd.memset(x, 0.0).then_inc(zeroed, 1)
                    pool.wait_ge(zeroed, len(cleared))
                    for c in range(NCH):
                        for d in range(2):
                            cols2 = slice(2 * d, 2 * d + 2)
                            need(pool, "PE", "v_A_r", d, c - 1)
                            need(pool, "ACT", "e2" if d == 0 else "e21", d, c)
                            for name, dst, src in (("b", bexp, bb), ("k", kexp, kdir)):
                                for rows_, cols in halves:
                                    last = nc.gpsimd.tensor_tensor(dst[rows_, cols2, cols], src[rows_, cols2, tokens(d, c)],
                                                                   e[rows_, 2, cols2, :], ALU.mult)
                                last.then_inc(made["POOL"], 1)
                            for rows_, cols in halves:
                                last = nc.gpsimd.tensor_copy(vexp[rows_, cols2, cols], v[rows_, :, tokens(d, c)])
                            last.then_inc(made["POOL"], 1)

                @block.scalar
                def _(act):
                    R = run[:].rearrange("p i (c w) -> p i c w", w=CW)

                    def factors(d, c, which):
                        if which[0] == 0:
                            need(act, "DVE", "r", d, c - 1)
                            need(act, "POOL", "k", d, c - 1)
                        if d == 0:
                            for j in which:
                                lo, sign = ((0, -DECAY), (1, -DECAY), (1, DECAY))[j]
                                nc.scalar.activation(e[:, j, 0:2, :], R[:, 0:2, chunk(0, c), lo:lo + CH], ACT.Exp, scale=sign).then_inc(made["ACT"], 1)
                        else:
                            cb = chunk(1, c)
                            for n in which:
                                j, i = n // 2, 2 + n % 2
                                lo, sign, total = ((1, DECAY, 1), (0, DECAY, 1), (0, -DECAY, 2))[j]
                                nc.scalar.activation(e[:, j, i, :], R[:, i, cb, lo:lo + CH], ACT.Exp, scale=sign,
                                                     bias=gam[:, total, i, cb:cb + 1]).then_inc(made["ACT"], 1)

                    def G_init(c):
                        for d in range(2):
                            nc.scalar.copy(items(G, d), both_items(ident[:])).then_inc(made["ACT"], 1)
                        for d in range(2):
                            nc.scalar.copy(items(T, d), both_items(ident[:])).then_inc(made["ACT"], 1)

                    factors(0, 0, [0, 1, 2])
                    factors(1, 0, [0, 1, 2, 3, 4, 5])
                    G_init(0)
                    act.wait_ge(levels_cast, 1)
                    for c in range(NCH):
                        for d in range(2):
                            need(act, "PE", "bk_turned", d, c)
                            nc.scalar.copy(BK[:, :, 2 * d:2 * d + 2, :], ps[4 * d][:].rearrange("p (m i n) -> p m i n", m=2, i=2)).then_inc(made["ACT"], 1)
                        for d in range(2):
                            need(act, "PE", "v_A_r", d, c)
                            nc.scalar.copy(items(V, d), bank(d, 1)).then_inc(made["ACT"], 1)
                        for l in range(1, LEVELS):
                            for d in range(2):
                                need(act, "PE", f"X{l}", d, c)
                                nc.scalar.copy(items(X, d), bank(d, 1)).then_inc(made["ACT"], 1)
                                if l > 1:
                                    need(act, "PE", f"T{l - 1}", d, c)
                                    nc.scalar.copy(items(T, d), bank(d, 0)).then_inc(made["ACT"], 1)
                            if c + 1 < NCH and l in (1, 2, 3):
                                factors(min(l - 1, 1), c + 1, [3, 4, 5] if l == 3 else [0, 1, 2])
                        for d in range(2):
                            need(act, "PE", "U", d, c)
                            nc.scalar.copy(items(U, d), bank(d, 3)).then_inc(made["ACT"], 1)
                        if c + 1 < NCH:
                            G_init(c + 1)

                @block.vector
                def _(dve):
                    def decayed(d, c):
                        need(dve, "PE", "Z", d, c - 2)
                        need(dve, "ACT", "e0" if d == 0 else "e01", d, c)
                        for rows_, cols in halves:
                            last = nc.vector.scalar_tensor_tensor(out=aexp[c % 2][rows_, 2 * d:2 * d + 2, cols], in0=kk[rows_, :, tokens(d, c)],
                                                                  scalar=-1.0, in1=e[rows_, 0, 2 * d:2 * d + 2, :], op0=ALU.mult, op1=ALU.mult)
                        last.then_inc(made["DVE"], 1)
                        need(dve, "PE", "Y", d, c - 2)
                        need(dve, "ACT", "e1" if d == 0 else "e11", d, c)
                        nc.vector.tensor_tensor(rc[:, c % 2, 2 * d:2 * d + 2, :], r[:, :, tokens(d, c)], e[:, 1, 2 * d:2 * d + 2, :],
                                                ALU.mult).then_inc(made["DVE"], 1)

                    def masked_A(d, c):
                        need(dve, "PE", "A", d, c)
                        nc.vector.tensor_tensor(items(A_ab, d), bank(d, 2), both_items(before[:, d, :]), ALU.mult).then_inc(made["DVE"], 1)
                        nc.vector.tensor_tensor(items(A_ak_T, d), bank(d, 2, at=2 * P), both_items(before_T[:, d, :]), ALU.mult).then_inc(made["DVE"], 1)

                    dve.wait_ge(loaded, 64)
                    nc.vector.tensor_copy(level[:].rearrange("p l d n -> p (l d n)"), level_f32).then_inc(levels_cast, 1)
                    dve.wait_ge(levels_cast, 1)
                    dve.wait_ge(zeroed, 7)
                    for d in range(2):
                        decayed(d, 0)
                    for d in range(2):
                        masked_A(d, 0)
                    for c in range(NCH):
                        def extend(l):
                            for d in range(2):
                                need(dve, "ACT", "G_init", d, c)
                                need(dve, "PE", "N" if l == 0 else f"GX{l}", d, c)
                                nc.vector.copy_predicated(items(G, d), both_items(level[:, l, d, :]), bank(d, 3)).then_inc(made["DVE"], 1)

                        extend(0)
                        for d in range(2):
                            need(dve, "ACT", "v", d, c)
                            upto = upto_T[:, d, :].unsqueeze(1).unsqueeze(1).broadcast_to([P, 2, 2, CH])
                            nc.vector.tensor_tensor(A_r_T[:, :, 2 * d:2 * d + 2, :], ps[4 * d + 1][:, 2 * P:4 * P].rearrange("p (m i n) -> p m i n", m=2, i=2),
                                                    upto, ALU.mult).then_inc(made["DVE"], 1)
                        for d in range(2):
                            need(dve, "ACT", "T_init", d, c)
                            need(dve, "DVE", "A_ab", d, c)
                            nc.vector.copy_predicated(items(T, d), both_items(level[:, 0, 1 - d, :]), items(A_ab, d)).then_inc(made["DVE"], 1)
                        for l in range(1, LEVELS):
                            extend(l)
                            if l in (2, 3):
                                need(dve, "PE", "Z", l - 2, c)
                                nc.vector.tensor_copy(items(Z, l - 2), bank(l - 2, 2)).then_inc(made["DVE"], 1)
                            if l in (2, 3) and c + 1 < NCH:
                                decayed(l - 2, c + 1)
                        if c + 1 < NCH:
                            for d in range(2):
                                masked_A(d, c + 1)
                        for d in range(2):
                            cols = tokens(d, c)
                            need(dve, "PE", "Y", d, c)
                            if d == 1:
                                need(dve, "DVE", "Y", 0, c)
                            nc.vector.tensor_tensor(y[:, :, cols], y[:, :, cols], bank(d, 0, CH), ALU.add).then_inc(made["DVE"], 1)
                            need(dve, "PE", "S", d, c)
                            nc.vector.tensor_tensor(items(S, d), items(S, d), bank(d, 1), ALU.add).then_inc(made["DVE"], 1)
                            need(dve, "DVE", "S_sum", d, c)
                            decay = gam[:, 0, 2 * d:2 * d + 2, chunk(d, c)].unsqueeze(2).broadcast_to([P, 2, P])
                            nc.vector.tensor_tensor(items(S, d), items(S, d), decay, ALU.mult).then_inc(made["DVE"], 1)
                        need(dve, "DVE", "S", 1, c)

                @block.tensor
                def _(pe):
                    def sums(d, out, terms):
                        for i in range(2):
                            for n, (lhs, rhs) in enumerate(terms):
                                last = nc.tensor.matmul(out[:, i, :], lhs[:, 2 * d + i, :], rhs[:, 2 * d + i, :], start=(n == 0), stop=(n == len(terms) - 1))
                        return last

                    def turn(d, out, x):
                        for i in range(2):
                            last = nc.tensor.transpose(out[:, i, :], x[:, 2 * d + i, :], ident[:])
                        return last

                    def A_products(d, c):
                        need(pe, "POOL", "k", d, c)
                        need(pe, "DVE", "r", d, c)
                        need(pe, "DVE", "Z", d, c - 1)
                        sums(d, bank(d, 2), [(aexp[c % 2], bexp)])
                        sums(d, bank(d, 2, at=2 * P), [(kexp, aexp[c % 2])]).then_inc(made["PE"], 1)

                    for d in range(2):
                        A_products(d, 0)
                    for c in range(NCH):
                        for d in range(2):
                            need(pe, "ACT", "U", d, c - 1)
                            sums(d, bank(d, 3), [(bexp, aexp[c % 2])]).then_inc(made["PE"], 1)
                        for d in range(2):
                            need(pe, "DVE", "Y", d, c - 1)
                            turn(d, bank(d, 0), bexp)
                            turn(d, bank(d, 0, at=2 * P), kexp).then_inc(made["PE"], 1)
                        for d in range(2):
                            need(pe, "POOL", "v", d, c)
                            need(pe, "DVE", "S_sum", d, c - 1)
                            turn(d, bank(d, 1), vexp)
                            sums(d, bank(d, 1, CH, 2 * P), [(bexp, rc[:, c % 2])])
                            sums(d, bank(d, 1, CH, 3 * P), [(kexp, rc[:, c % 2])]).then_inc(made["PE"], 1)
                        for l in range(1, LEVELS):
                            for d in range(2):
                                need(pe, "DVE", f"G{l - 1}" if l > 1 else "A_r", d, c)
                                if l == 1:
                                    need(pe, "ACT", "v", d, c)
                                sums(d, bank(d, 1), [(A_ab, G)]).then_inc(made["PE"], 1)
                                if l > 1:
                                    turn(d, bank(d, 0), G).then_inc(made["PE"], 1)
                            if l in (2, 3):
                                need(pe, "DVE", "S", l - 2, c - 1)
                                sums(l - 2, bank(l - 2, 2), [(aexp[c % 2], S), (A_ak_T, V)]).then_inc(made["PE"], 1)
                            if l in (4, 5) and c + 1 < NCH:
                                A_products(l - 4, c + 1)
                            for d in range(2):
                                need(pe, "ACT", f"X{l}" if l == 1 else f"T{l - 1}", d, c)
                                if l == 1:
                                    need(pe, "DVE", "T0", d, c)
                                sums(d, bank(d, 3), [(T, X)]).then_inc(made["PE"], 1)
                        for d in range(2):
                            need(pe, "DVE", "G5", d, c)
                            sums(d, bank(d, 3), [(G, Z)]).then_inc(made["PE"], 1)
                        for d in range(2):
                            need(pe, "ACT", "U", d, c)
                            sums(d, bank(d, 0, CH), [(S, rc[:, c % 2]), (U, A_r_T[:, 0]), (V, A_r_T[:, 1])]).then_inc(made["PE"], 1)
                        for d in range(2):
                            sums(d, bank(d, 1), [(Bt, U), (Kt, V)]).then_inc(made["PE"], 1)

    def head_norm_stage(half, rcols, lora, r, y, v, mixT, flat):
        f0 = 2 * half
        inv = flat[:, 0:2 * TOK].rearrange("p (b n) -> p b n", b=2)
        jobs = [(f, s) for f in range(2) for s in HALVES]
        with stage():
            g2 = sb("g2", [P, 2 * P])
            brought = sem("brought_back")
            loaded, mean_mm, centred, squared, var_mm, var_ready, root_ready, gate_mm, chained = (sem(n) for n in (
                "loaded", "mean_product", "centred", "squared", "var_product", "var_ready", "root_ready", "gate_product", "vector_step"))
            with nc.Block() as block:
                @block.sync
                def _(sp):
                    sp.dma_start(g2[:], dram["g2"][half]).then_inc(loaded, 16)
                    if half == 0:
                        sp.dma_start(flat_of(r), parked_rkv[:, 0:2 * TOK]).then_inc(brought, 16)
                        sp.dma_start(flat_of(v), parked_rkv[:, 4 * TOK:6 * TOK]).then_inc(brought, 16)
                        sp.wait_ge(brought, 32)
                    else:
                        sp.dma_start(flat[:, CTX_T * D:], parked[:, CTX_T * D:]).then_inc(brought, 16)
                        sp.wait_ge(brought, 16)

                @block.tensor
                def _(pe):
                    for i, (f, s) in enumerate(jobs):
                        nc.tensor.matmul(ps[i][:, 0:s.stop - s.start], head_ones[:], y[:, f, s], start=True, stop=True).then_inc(mean_mm, 1)
                    for i, (f, s) in enumerate(jobs):
                        pe.wait_ge(squared, i + 1)
                        nc.tensor.matmul(ps[4 + i][:, 0:s.stop - s.start], head_ones[:], inv[:, f, s], start=True, stop=True).then_inc(var_mm, 1)
                    pe.wait_ge(loaded, 16)
                    for i, (f, s) in enumerate(jobs):
                        nc.tensor.matmul(ps[i][:, 0:s.stop - s.start], g2[:, f * P:(f + 1) * P], lora[:, 2, s], start=True, stop=True).then_inc(gate_mm, 1)

                @block.scalar
                def _(act):
                    for i, (f, s) in enumerate(jobs):
                        act.wait_ge(centred, i + 1)
                        nc.scalar.activation(inv[:, f, s], y[:, f, s], ACT.Square).then_inc(squared, 1)
                    for i, (f, s) in enumerate(jobs):
                        act.wait_ge(var_ready, i + 1)
                        nc.scalar.activation(inv[:, f, s], inv[:, f, s], ACT.Sqrt).then_inc(root_ready, 1)

                @block.vector
                def _(dve):
                    step = Chain(dve, chained)
                    for i, (f, s) in enumerate(jobs):
                        dve.wait_ge(mean_mm, i + 1)
                        nc.vector.scalar_tensor_tensor(out=y[:, f, s], in0=ps[i][:, 0:s.stop - s.start], scalar=-1.0 / HD, in1=y[:, f, s],
                                                       op0=ALU.mult, op1=ALU.add).then_inc(centred, 1)
                    for i, (f, s) in enumerate(jobs):
                        dve.wait_ge(var_mm, i + 1)
                        nc.vector.tensor_scalar(inv[:, f, s], ps[4 + i][:, 0:s.stop - s.start], 1.0 / HD, GN_EPS, ALU.mult, ALU.add).then_inc(var_ready, 1)
                    dve.wait_ge(centred, 4)
                    for i, (f, s) in enumerate(jobs):
                        dve.wait_ge(root_ready, i + 1)
                        step(nc.vector.reciprocal(inv[:, f, s], inv[:, f, s]))
                        step(nc.vector.tensor_tensor(y[:, f, s], y[:, f, s], inv[:, f, s], ALU.mult))
                        step(nc.vector.tensor_scalar(y[:, f, s], y[:, f, s], rcols[:, R_GW + f0 + f:R_GW + f0 + f + 1],
                                                     rcols[:, R_GB + f0 + f:R_GB + f0 + f + 1], ALU.mult, ALU.add))
                        step(nc.vector.tensor_tensor(y[:, f, s], y[:, f, s], mixT[:, f0 + f, s], ALU.add))
                        dve.wait_ge(gate_mm, i + 1)
                        step(nc.vector.tensor_tensor(mixT[:, f0 + f, s], y[:, f, s], ps[i][:, 0:s.stop - s.start], ALU.mult))

    def second_block():
        for layer in range(DEPTH):
            tiles = all_tiles if layer == 0 else lat_tiles
            streams = 2 if layer == 0 else 1
            modulation2_stage(layer, 0)
            with stage():
                bring = None
                if layer == 0:
                    mixT = sb("mixT", [P, DK, TOK])
                    even_mixer(mixT)
                    dump("rwkv", mixT[:, 0:4, :])
                    back = sem("residual_back")

                    def bring(sp):
                        sp.dma_start(flat_of(resid)[:, 0:CTX_T * D], parked[:, 0:CTX_T * D]).then_inc(back, 16)
                        sp.wait_ge(back, 16)
                else:
                    mixT = odd_mixer()
                    dump("odd", mixT[:])
                gates2_stage(layer, GATE, streams, beside=bring)
                out_product_rms_stage(f"out{layer}", lambda k: mixT[:, k:k + 2, :], tiles)
            dump(f"h{layer}", resid[:])
            modulation2_stage(layer, 1)
            ffn2_stages(layer, tiles)
            dump(f"g{layer}", resid[:])
        with stage():
            with nc.Block() as block:
                @block.sync
                def _(sp):
                    sp.dma_start(out_dram[0].rearrange("(t p) d -> p t d", p=P), resid[:, CTX_T:TOK_T, :]).then_inc(stored, 16)
                    sp.wait_ge(stored, 16)

    setup_stage()
    sgu_pool_mixer(modulate1("ada_mix0"))
    dump("x1", resid[:])
    ffn1_stages(0, modulate1("ada_ffn0"))
    dump("x2", resid[:])
    conformer_mixer(modulate1("ada_mix1"))
    dump("x3", resid[:])
    ffn1_stages(1, modulate1("ada_ffn1"))
    dump("x4", resid[:])
    second_block()


def blocks_of(w, plan):
    w = np.asarray(w)
    parts = [w[k * P:(k + nk) * P, c:c + nc].reshape(nk, P, nc).transpose(1, 0, 2).ravel() for k, nk, c, nc in plan]
    return np.ascontiguousarray(np.concatenate(parts))


def columns(v, *shape):
    v = np.asarray(v)
    return np.ascontiguousarray(v.reshape(-1, P).T)


def interleaved(w, half):
    a, b = w[..., :half], w[..., half:]
    n = half // P
    stacked = np.stack([a.reshape(*a.shape[:-1], n, P), b.reshape(*b.shape[:-1], n, P)], axis=-2)
    return stacked.reshape(*w.shape)


def shape_constants():
    same_head = np.kron(np.eye(P // HD), np.ones((HD, HD))).astype(np.float32)
    t = np.arange(SEQ)
    counts = [np.minimum(t + w // 2, SEQ) - np.maximum(t - w // 2, 0) for w in (2, 4, 8, 16)]
    return {
        "identity": np.eye(P, dtype=np.float32),
        "head_ones": same_head,
        "inv_count": (1.0 / np.stack(counts)).astype(np.float32),
    }


def lay_out_first(i):
    plans = dict(WEIGHTS)
    i = {k: np.asarray(v) for k, v in i.items()}
    out = dict(shape_constants())
    out["x"] = i["x"][0]
    out["ctx"] = i["ctx_2"][0]
    out["c1"] = columns(i["c"][0])
    out["c2"] = np.ascontiguousarray(np.stack([columns(i["c_2"][0]), columns(i["c_ctx_2"])], axis=-1))
    for l in range(DEPTH):
        out[f"bias_ada_mix{l}"], out[f"bias_ada_ffn{l}"] = columns(i["mix_ada_b"][l]), columns(i["ffn_ada_b"][l])
        out[f"bias_ada{l}"] = columns(i["b_ada_2"][l])
    w_in = i["ab_w_in"][0]
    out["ab_uv"] = blocks_of(w_in[:, :1024], plans["ab_uv"])
    out["ab_z"] = blocks_of(w_in[:, 1024:], plans["ab_z"])
    out["ab_out"] = blocks_of(i["ab_w_out"][0], plans["ab_out"])
    out["sgu_g"], out["sgu_b"] = i["ab_sgu_ln_g"][0], i["ab_sgu_ln_b"][0]
    out["wsT"] = np.ascontiguousarray(i["ab_ws"][0].transpose(2, 0, 1))
    out["bs"] = np.ascontiguousarray(i["ab_bs"][0].T)
    out["pool_w"] = np.ascontiguousarray(i["ab_pool_w"][0].transpose(1, 0, 2))
    out["pool_scale"] = columns(i["ab_pool_scale"][0])
    out["cv_in"] = blocks_of(interleaved(i["cv_w_in"][0], D), plans["cv_in"])
    out["cv_out"] = blocks_of(i["cv_w_out"][0], plans["cv_out"])
    taps = np.concatenate([i["cv_dw"][0], i["cv_dw_b"][0][None]])
    out["cv_taps"] = np.ascontiguousarray(taps.reshape(CONV_W + 1, DK, P).transpose(2, 1, 0))
    out["cv_ln"] = np.ascontiguousarray(np.stack([columns(i["cv_ln_g"][0]), columns(i["cv_ln_b"][0])], axis=1))
    ffn_taps = []
    for l in range(DEPTH):
        out[f"ada_mix{l}"] = blocks_of(i["mix_ada_w"][l], ADA1)
        out[f"ada_ffn{l}"] = blocks_of(i["ffn_ada_w"][l], ADA1)
        out[f"up{l}"] = blocks_of(interleaved(i["ffn_w_up"][l], FFN), plans[f"up{l}"])
        out[f"down{l}"] = blocks_of(i["ffn_w_down"][l], plans[f"down{l}"])
        for kind in ("mix", "ffn"):
            out[f"{kind}_ln_g{l}"], out[f"{kind}_ln_b{l}"] = i[f"{kind}_ln_g"][l], i[f"{kind}_ln_b"][l]
        taps = np.concatenate([i["ffn_dw"][l], i["ffn_dw_b"][l][None]])
        ffn_taps.append(interleaved(taps, FFN).reshape(4, 2 * FK, P).transpose(2, 1, 0))
    out["ffn_taps"] = np.ascontiguousarray(np.stack(ffn_taps))
    return out


def second_constants():
    out = {}
    t = np.arange(SEQ)
    n_freq = HD // 4
    inv_freq = 10000.0 ** (-np.arange(n_freq, dtype=np.float32) / n_freq)
    row = (t // GRID_W).astype(np.float32)[:, None] * inv_freq.astype(np.float32)
    col = (t % GRID_W).astype(np.float32)[:, None] * inv_freq.astype(np.float32)
    ang = np.concatenate([row, row, col, col], axis=-1).astype(np.float64).T
    out["rope_cos"] = np.tile(np.cos(ang), (2, 1)).astype(np.float32)
    out["rope_sin"] = np.tile(np.sin(ang), (2, 1)).astype(np.float32)
    turn = np.zeros((P, P), np.float32)
    for base in range(0, P, 2 * n_freq):
        for i in range(n_freq):
            turn[base + n_freq + i, base + i] = -1.0
            turn[base + i, base + n_freq + i] = 1.0
    out["rope_turn"] = turn
    q, k = np.arange(P)[:, None], np.arange(3 * P)[None, :]
    out["window_mask"] = np.where(np.abs(k - P - q) <= P, 0.0, NEG_INF).astype(np.float32)
    reset = np.ones((NCH, CW), np.float32)
    reset[:, 0] = 0
    out["reset"] = reset.ravel()
    i = np.arange(CH)
    earlier = (i[None, :] < i[:, None])
    both = np.stack([earlier, earlier.T])
    blocks = np.stack([np.kron(np.eye(2), m) for m in both])
    out["mask_before"] = np.ascontiguousarray(blocks.transpose(1, 0, 2)).astype(np.float32)
    out["mask_before_T"] = np.ascontiguousarray(blocks.transpose(2, 0, 1)).astype(np.float32)
    upto = both | np.eye(CH, dtype=bool)
    out["mask_upto_T"] = np.ascontiguousarray(np.tile(upto.transpose(2, 0, 1), (2, 1, 1))).astype(np.float32)
    levels = []
    for l in range(LEVELS):
        m = 1 << l
        pair = (i[:, None] // (2 * m) == i[None, :] // (2 * m))
        fwd = pair & (i[:, None] // m < i[None, :] // m)
        levels.append(np.stack([np.kron(np.eye(2), fwd), np.kron(np.eye(2), fwd.T)]))
    out["level_masks"] = np.ascontiguousarray(np.stack(levels).transpose(2, 0, 1, 3).reshape(P, -1)).astype(np.float32)
    return out


def rpb_layout(rpb):
    t = np.arange(SEQ)
    r, c = t // GRID_W, t % GRID_W
    start = np.clip(c - 8, 0, GRID_W - 16)
    ok = (c[None, :] >= start[:, None]) & (c[None, :] < start[:, None] + 16)
    dr = r[None, :] - r[:, None] + 7
    dc = np.clip(c[None, :] - c[:, None] + 15, 0, 30)
    out = rpb[:, dr, dc]
    out[:, ~ok] = NEG_INF
    return np.ascontiguousarray(out)


def lay_out(i):
    plans = dict(WEIGHTS)
    out = lay_out_first(i)
    i = {k: np.asarray(v) for k, v in i.items()}
    out.update(second_constants())
    out["gains"] = np.ascontiguousarray(np.stack([np.stack([columns(i[n][l]) for n in (
        "g_pre_mix_2", "g_post_mix_2", "g_pre_ff_2", "g_post_ff_2")], axis=1) for l in range(DEPTH)]))
    for l in range(DEPTH):
        out[f"ada{l}"] = blocks_of(i["w_ada_2"][l], ADA2)
        out[f"out{l}"] = blocks_of(i["w_out_2"][l], plans[f"out{l}"])
        out[f"ff1_{l}"] = blocks_of(i["w_ff1_2"][l], plans[f"ff1_{l}"])
        out[f"ff2_{l}"] = blocks_of(i["w_ff2_2"][l], plans[f"ff2_{l}"])
    even, odd = i["w_in_even_2"][0], i["w_in_odd_2"][0]

    def grouped(w):
        k0, k1 = w[:, 512:512 + HD], w[:, 512 + HD:512 + 2 * HD]
        return np.concatenate([w[:, :512], k0, k0, k1, k1], axis=1), w[:, 640:768]

    qk, v = grouped(even[:, 1920:])
    out["b_qk"], out["b_v"] = blocks_of(qk, plans["b_qk"]), blocks_of(v, plans["b_v"])
    qk, v = grouped(odd[:, 1536:])
    out["d_qk"], out["d_v"] = blocks_of(qk, plans["d_qk"]), blocks_of(v, plans["d_v"])
    out["c_qk"], out["c_v"] = blocks_of(odd[:, :1024], plans["c_qk"]), blocks_of(odd[:, 1024:1536], plans["c_v"])
    out["lora"] = blocks_of(even[:, 1536:1920], plans["lora"])
    for h in range(2):
        cols = [even[:, x * 512 + h * 256:x * 512 + (h + 1) * 256] for x in range(3)]
        out[f"rkv{h}"] = blocks_of(np.concatenate(cols, axis=1), plans[f"rkv{h}"])
    mu = np.stack([columns(i["a_mu_prev_2"][0]), columns(i["a_mu_next_2"][0])], axis=-1).reshape(P, 30)
    two = lambda x: np.concatenate([columns(x[0]), columns(x[1])], axis=1)
    out["r_cols"] = np.ascontiguousarray(np.concatenate([
        mu, two(i["a_w0_2"][0]), two(i["a_a0_2"][0]), columns(i["a_k_k_2"][0]), columns(i["a_k_a_2"][0]),
        columns(i["a_r_k_2"][0].reshape(-1)), columns(i["a_gn_w_2"][0]), columns(i["a_gn_b_2"][0])], axis=1))
    for name, src in (("w2", i["a_w2_2"][0]), ("a2", i["a_a2_2"][0])):
        full = np.zeros((2, P, 2, 2 * P), np.float32)
        for d in range(2):
            for h in range(2):
                full[h, d * HD:(d + 1) * HD, d] = src[d][:, h * 256:(h + 1) * 256]
        out[name] = full
    out["g2"] = np.ascontiguousarray(i["a_g2_2"][0].reshape(P, 2, 2 * P).transpose(1, 0, 2))
    out["b_sink"] = i["b_sink_2"][0]
    out["rpb_table"] = rpb_layout(i["c_rpb_2"][0])
    out["d_gain"] = np.ascontiguousarray(np.stack([np.tile(i["d_q_gain_2"][0], 2), np.tile(i["d_k_gain_2"][0], 2)], axis=1))
    return out


def kernel(**inputs):
    import concourse.bacc as bacc
    from concourse.bass_utils import run_bass_kernel_spmd

    arrays = lay_out(inputs)
    nc = bacc.Bacc("TRN2", target_bir_lowering=False, num_devices=1)
    dram = {name: nc.dram_tensor(name, a.shape, mybir.dt.from_np(a.dtype), kind="ExternalInput").ap() for name, a in arrays.items()}
    out = nc.dram_tensor("out", (1, SEQ, D), F32, kind="ExternalOutput").ap()
    build(nc, dram, out)
    got = run_bass_kernel_spmd(nc, [arrays], core_ids=[0])
    return got.results[0]["out"]
```
